# Optimizing a Trainium2 kernel written in Bass

```python
import jax
import jax.numpy as jnp
from jax import lax
import numpy as np

D_MODEL = 2048
BATCH = 1
SEQ = 256
DEPTH = 2

GRID_W = 64
CTX_LEN = 256

GLA_HEADS = 4
GLA_DK = 256
GLA_DV = 256
GLA_KEY_W = GLA_HEADS * GLA_DK
GLA_VAL_W = GLA_HEADS * GLA_DV
GLA_GATE_RANK = 16
GLA_TAU = 16.0
GLA_CHUNK = 64

CONV_W = D_MODEL // 2
CONV_K = 3

POOL_W = D_MODEL
POOL_WINDOWS = (2, 4, 8, 16)
POOL_GROUP = POOL_W // len(POOL_WINDOWS)

E_SIZES = (GLA_KEY_W, GLA_VAL_W, GLA_GATE_RANK, GLA_GATE_RANK, GLA_KEY_W, GLA_VAL_W,
           CONV_W, CONV_W, CONV_W, CONV_W)
E_IN = sum(E_SIZES)
E_STATE_COLS = GLA_KEY_W + GLA_VAL_W + 2 * GLA_GATE_RANK
E_MIX = GLA_VAL_W + CONV_W
O_IN = 2 * POOL_W
LN_EPS = 1e-5


def layer_norm(x, g, b):
    xf = x.astype(jnp.float32)
    mu = jnp.mean(xf, axis=-1, keepdims=True)
    var = jnp.mean(jnp.square(xf - mu), axis=-1, keepdims=True)
    return ((xf - mu) * lax.rsqrt(var + LN_EPS)).astype(x.dtype) * g + b

def rms_norm(x, g):
    xf = x.astype(jnp.float32)
    return xf * lax.rsqrt(jnp.mean(jnp.square(xf), axis=-1, keepdims=True) + LN_EPS) * g.astype(jnp.float32)

def modulation(cond, w, b, n):
    m = jax.nn.silu(cond) @ w[:, :n * D_MODEL] + b[:n * D_MODEL]
    return jnp.split(m, n, axis=-1)

def split_cols(h, sizes):
    idx = [int(i) for i in np.cumsum(sizes)[:-1]]
    return jnp.split(h, idx, axis=-1)

def to_heads(t, d):
    bn, L, _ = t.shape
    return t.reshape(bn, L, -1, d).transpose(0, 2, 1, 3)

def from_heads(t):
    bn, H, L, d = t.shape
    return t.transpose(0, 2, 1, 3).reshape(bn, L, H * d)

def flip_seq(t):
    return jnp.flip(t, axis=2)

def gate_log(r, w, b):
    return jax.nn.log_sigmoid((r @ w + b).astype(jnp.float32)) / GLA_TAU

def gla_chunked(q, k, v, log_a, s0):
    bn, H, L, _ = q.shape
    dv = v.shape[-1]
    C = GLA_CHUNK
    nc = L // C

    def to_chunks(t):
        return jnp.moveaxis(t.astype(jnp.float32).reshape(bn, H, nc, C, t.shape[-1]), 2, 0)

    lower = np.tril(np.ones((C, C), dtype=bool))[:, :, None]

    def step(s, inp):
        qc, kc, vc, lac = inp
        g = jnp.cumsum(lac, axis=-2)
        diff = g[..., :, None, :] - g[..., None, :, :]
        decay = jnp.exp(jnp.where(lower, diff, -jnp.inf))
        scores = jnp.einsum('bhik,bhjk,bhijk->bhij', qc, kc, decay)
        o = (jnp.einsum('bhij,bhjv->bhiv', scores, vc)
             + jnp.einsum('bhik,bhkv->bhiv', qc * jnp.exp(g), s))
        g_last = g[..., -1:, :]
        s_new = (jnp.exp(g_last)[..., 0, :, None] * s
                 + jnp.einsum('bhjk,bhjv->bhkv', kc * jnp.exp(g_last - g), vc))
        return s_new, o

    s_fin, o = lax.scan(step, s0, (to_chunks(q), to_chunks(k), to_chunks(v), to_chunks(log_a)))
    o = jnp.moveaxis(o, 0, 2).reshape(bn, H, L, dv)
    return o, s_fin

def gla_final_state(k, v, log_a):
    g = jnp.cumsum(log_a, axis=-2)
    return jnp.einsum('bhtk,bhtv->bhkv', k * jnp.exp(g[..., -1:, :] - g), v)

def context_states(hs, w_gf, b_gf, w_gb, b_gb):
    k, v, rf, rb = split_cols(hs, E_SIZES[:4])
    k = to_heads(k, GLA_DK).astype(jnp.float32)
    v = to_heads(v, GLA_DV).astype(jnp.float32)
    la_f = to_heads(gate_log(rf, w_gf, b_gf), GLA_DK)
    la_b = to_heads(gate_log(rb, w_gb, b_gb), GLA_DK)
    s_f = gla_final_state(k, v, la_f)
    s_b = gla_final_state(flip_seq(k), flip_seq(v), flip_seq(la_b))
    return s_f, s_b

def conv3_centred(x, w):
    zero = jnp.zeros_like(x[..., :1, :])
    x_prev = jnp.concatenate([zero, x[..., :-1, :]], axis=-2)
    x_next = jnp.concatenate([x[..., 1:, :], zero], axis=-2)
    return w[0] * x_prev + w[1] * x + w[2] * x_next

def centred_window_mean(x, window, axis):
    L = x.shape[axis]
    xf = jnp.moveaxis(x, axis, 0).astype(jnp.float32)
    cs = jnp.concatenate([jnp.zeros_like(xf[:1]), jnp.cumsum(xf, axis=0)], axis=0)
    t = np.arange(L)
    lo = np.clip(t - window // 2, 0, L)
    hi = np.clip(t + window - window // 2, 0, L)
    cnt = (hi - lo).astype(np.float32).reshape((L,) + (1,) * (xf.ndim - 1))
    mean = (cs[hi] - cs[lo]) / cnt
    return jnp.moveaxis(mean, 0, axis).astype(x.dtype)

def even_mixer(h, s0_f, s0_b, w_gf, b_gf, w_gb, b_gb, gla_norm_w, conv_w, w_out, grid):
    bn, L, _ = h.shape
    k, v, rf, rb, q, gate_b, a_b, a_c, a_x, gate_a = split_cols(h, E_SIZES)
    qh = to_heads(q * (GLA_DK ** -0.5), GLA_DK)
    kh = to_heads(k, GLA_DK)
    vh = to_heads(v, GLA_DV)
    la_f = to_heads(gate_log(rf, w_gf, b_gf), GLA_DK)
    la_b = to_heads(gate_log(rb, w_gb, b_gb), GLA_DK)
    o_f, s_f = gla_chunked(qh, kh, vh, la_f, s0_f)
    o_b, s_b = gla_chunked(flip_seq(qh), flip_seq(kh), flip_seq(vh), flip_seq(la_b), s0_b)
    o = rms_norm(o_f + flip_seq(o_b), gla_norm_w)
    y_b = from_heads(o).astype(h.dtype) * jax.nn.silu(gate_b)
    u = (a_c * a_x).reshape(bn, grid[0], grid[1], CONV_W)
    u = conv3_centred(u, conv_w).reshape(bn, L, CONV_W)
    y_a = a_b * u * jax.nn.silu(gate_a)
    return jnp.concatenate([y_b, y_a], axis=-1) @ w_out, s_f, s_b

def odd_mixer(h, w_pool, pool_scale, w_out, grid):
    bn, L, _ = h.shape
    xp, gate = jnp.split(h, 2, axis=-1)
    xg = xp.reshape(bn, grid[0], grid[1], POOL_W)
    groups = jnp.split(xg, len(POOL_WINDOWS), axis=-1)
    z = jnp.stack([centred_window_mean(g, w, 1) - g for g, w in zip(groups, POOL_WINDOWS)], axis=-2)
    z = jnp.einsum('brcgi,gio->brcgo', z, w_pool).reshape(bn, L, POOL_W) * pool_scale
    return (z * jax.nn.silu(gate)) @ w_out

def first_inputs(seed: int = 0) -> dict:
    key = jax.random.key(seed)
    ks = jax.random.split(key, 20)
    ne = (DEPTH + 1) // 2
    no = DEPTH // 2
    beta = (8.0 * DEPTH) ** -0.25

    def nrm(k, shape, s):
        return jax.random.normal(k, shape, jnp.float32) * s

    return {
        'x': nrm(ks[0], (BATCH, SEQ, D_MODEL), 1.0),
        'c': nrm(ks[1], (BATCH, D_MODEL), 1.0),
        'ctx': nrm(ks[2], (BATCH, CTX_LEN, D_MODEL), 1.0),
        'c_ctx': nrm(ks[3], (D_MODEL,), 1.0),
        'w_ada': nrm(ks[4], (DEPTH, D_MODEL, 3 * D_MODEL), 0.5 * D_MODEL ** -0.5),
        'b_ada': nrm(ks[5], (DEPTH, 3 * D_MODEL), 0.02),
        'ln_g': 1.0 + nrm(ks[6], (DEPTH, D_MODEL), 0.02),
        'ln_b': nrm(ks[7], (DEPTH, D_MODEL), 0.02),
        'w_in_e': nrm(ks[8], (ne, D_MODEL, E_IN), D_MODEL ** -0.5),
        'w_gate_f': nrm(ks[9], (ne, GLA_GATE_RANK, GLA_KEY_W), GLA_GATE_RANK ** -0.5),
        'b_gate_f': nrm(ks[10], (ne, GLA_KEY_W), 0.1),
        'w_gate_b': nrm(ks[11], (ne, GLA_GATE_RANK, GLA_KEY_W), GLA_GATE_RANK ** -0.5),
        'b_gate_b': nrm(ks[12], (ne, GLA_KEY_W), 0.1),
        'gla_norm_w': 1.0 + nrm(ks[13], (ne, GLA_DV), 0.02),
        'conv_w': nrm(ks[14], (ne, CONV_K, CONV_W), CONV_K ** -0.5),
        'w_out_e': nrm(ks[15], (ne, E_MIX, D_MODEL), beta * E_MIX ** -0.5),
        'w_in_o': nrm(ks[16], (no, D_MODEL, O_IN), D_MODEL ** -0.5),
        'w_pool': nrm(ks[17], (no, len(POOL_WINDOWS), POOL_GROUP, POOL_GROUP), POOL_GROUP ** -0.5),
        'pool_scale': 1.0 + nrm(ks[18], (no, POOL_W), 0.02),
        'w_out_o': nrm(ks[19], (no, POOL_W, D_MODEL), beta * POOL_W ** -0.5),
    }

def first_block(x, c, ctx, c_ctx, w_ada, b_ada, ln_g, ln_b, w_in_e, w_gate_f, b_gate_f,
              w_gate_b, b_gate_b, gla_norm_w, conv_w, w_out_e, w_in_o, w_pool, pool_scale, w_out_o):
    alpha = (2.0 * DEPTH) ** 0.25
    bn, L, _ = x.shape
    rows = L // GRID_W
    lc = ctx.shape[1]
    c_lat = c[:, None, :]
    c_c = c_ctx[None, None, :]
    s_zero = jnp.zeros((bn, GLA_HEADS, GLA_DK, GLA_DV), jnp.float32)
    ctx_s = ctx
    for i in range(DEPTH):
        j = i // 2
        ctx_needed = any(l % 2 == 0 for l in range(i + 1, DEPTH))
        sh, sc, gt = modulation(c_lat, w_ada[i], b_ada[i], 3)
        u = x * (1.0 + sc) + sh
        if i % 2 == 0:
            if ctx_needed:
                sh_c, sc_c, gt_c = modulation(c_c, w_ada[i], b_ada[i], 3)
                uc = ctx_s * (1.0 + sc_c) + sh_c
                yc, s_f, s_b = even_mixer(uc @ w_in_e[j], s_zero, s_zero, w_gate_f[j], b_gate_f[j],
                                          w_gate_b[j], b_gate_b[j], gla_norm_w[j], conv_w[j],
                                          w_out_e[j], (1, lc))
                ctx_s = layer_norm(alpha * ctx_s + gt_c * yc, ln_g[i], ln_b[i])
            else:
                sh_c, sc_c = modulation(c_c, w_ada[i], b_ada[i], 2)
                uc = ctx_s * (1.0 + sc_c) + sh_c
                s_f, s_b = context_states(uc @ w_in_e[j][:, :E_STATE_COLS], w_gate_f[j], b_gate_f[j],
                                          w_gate_b[j], b_gate_b[j])
            y, _, _ = even_mixer(u @ w_in_e[j], s_f, s_b, w_gate_f[j], b_gate_f[j], w_gate_b[j],
                                 b_gate_b[j], gla_norm_w[j], conv_w[j], w_out_e[j], (rows, GRID_W))
        else:
            if ctx_needed:
                sh_c, sc_c, gt_c = modulation(c_c, w_ada[i], b_ada[i], 3)
                uc = ctx_s * (1.0 + sc_c) + sh_c
                yc = odd_mixer(uc @ w_in_o[j], w_pool[j], pool_scale[j], w_out_o[j], (lc, 1))
                ctx_s = layer_norm(alpha * ctx_s + gt_c * yc, ln_g[i], ln_b[i])
            y = odd_mixer(u @ w_in_o[j], w_pool[j], pool_scale[j], w_out_o[j], (rows, GRID_W))
        x = layer_norm(alpha * x + gt * y, ln_g[i], ln_b[i])
    return x


DEPTH_2 = 1

MIX_WIDTH = D_MODEL
RWKV_WIDTH = MIX_WIDTH // 2
RWKV_HEAD = 64
RWKV_HEADS = RWKV_WIDTH // RWKV_HEAD
DECAY_LORA = 64
AAA_LORA = 64
GATE_LORA = 160
RWKV_LN_EPS = 64e-5
ATT_WIDTH = MIX_WIDTH - RWKV_WIDTH
ATT_HEAD = 128
ATT_HEADS = ATT_WIDTH // ATT_HEAD
ATT_KV_HEADS = 2
IDX_HEADS = 16
IDX_HEAD = 64
TOPK_MAX = 256
Q_BLOCK = 128
ROPE_THETA = 500000.0
N_MEM = 256
CROSS_HEADS = 4
CROSS_HEAD = 128
D_FF = 4 * D_MODEL
NORM_EPS = 1e-5

RWKV_SPLITS = (RWKV_WIDTH, RWKV_WIDTH, RWKV_WIDTH, DECAY_LORA, AAA_LORA, GATE_LORA)
ATT_SPLITS = (ATT_WIDTH, ATT_KV_HEADS * ATT_HEAD, ATT_KV_HEADS * ATT_HEAD,
              IDX_HEADS * IDX_HEAD, IDX_HEAD, IDX_HEADS)
RWKV_COLS = sum(RWKV_SPLITS)
ATT_COLS = sum(ATT_SPLITS)
IN_COLS = RWKV_COLS + ATT_COLS


def split_cols_2(t, sizes):
    out, start = [], 0
    for s in sizes:
        out.append(t[..., start:start + s])
        start += s
    return out

def rms_norm_2(x, g):
    xf = x.astype(jnp.float32)
    y = xf * lax.rsqrt(jnp.mean(xf * xf, axis=-1, keepdims=True) + NORM_EPS)
    return (y * g.astype(jnp.float32)).astype(x.dtype)

def partial_rope(x, pos):
    dh = x.shape[-1]
    rot = dh // 4
    half = rot // 2
    inv_freq = ROPE_THETA ** (-jnp.arange(half, dtype=jnp.float32) / half)
    ang = pos.astype(jnp.float32)[..., None] * inv_freq
    cos = jnp.cos(ang)[:, :, None, :]
    sin = jnp.sin(ang)[:, :, None, :]
    xr = x[..., :rot].astype(jnp.float32)
    x1, x2 = xr[..., :half], xr[..., half:]
    rotated = jnp.concatenate([x1 * cos - x2 * sin, x2 * cos + x1 * sin], axis=-1).astype(x.dtype)
    return jnp.concatenate([rotated, x[..., rot:]], axis=-1)

def rwkv7_group(p, mu, w0, w_decay_up, a0, a_up, g_up, k_k, k_a, r_k, lnx_w, lnx_b):
    B, S, _ = p.shape
    H, N = RWKV_HEADS, RWKV_HEAD
    f32 = jnp.float32
    prev = jnp.pad(p, ((0, 0), (1, 0), (0, 0)))[:, :-1]
    p = p + (prev - p) * mu
    r, k, v, xw, xa, xg = split_cols_2(p, RWKV_SPLITS)
    w = -jax.nn.softplus(-(w0 + jnp.tanh(xw) @ w_decay_up)) - 0.5
    decay = jnp.exp(-jnp.exp(w.astype(f32)))
    a = jax.nn.sigmoid(a0 + xa @ a_up)
    g = jax.nn.sigmoid(xg) @ g_up
    heads = lambda t: t.astype(f32).reshape(B, S, H, N)
    kk = heads(k * k_k)
    kk = kk / jnp.maximum(jnp.sqrt(jnp.sum(kk * kk, axis=-1, keepdims=True)), 1e-12)
    k = k * (1.0 + (a - 1.0) * k_a)
    r4, k4, v4, a4, w4 = heads(r), heads(k), heads(v), heads(a), decay.reshape(B, S, H, N)

    def step(state, inp):
        r_t, w_t, k_t, v_t, kk_t, a_t = inp
        sa = jnp.einsum('bhvk,bhk->bhv', state, -kk_t)
        state = (state * w_t[:, :, None, :]
                 + sa[..., None] * (kk_t * a_t)[:, :, None, :]
                 + v_t[..., None] * k_t[:, :, None, :])
        return state, jnp.einsum('bhvk,bhk->bhv', state, r_t)

    tm = lambda t: jnp.swapaxes(t, 0, 1)
    s0 = jnp.zeros((B, H, N, N), f32)
    _, y = lax.scan(step, s0, (tm(r4), tm(w4), tm(k4), tm(v4), tm(kk), tm(a4)))
    y = tm(y)
    mean = jnp.mean(y, axis=-1, keepdims=True)
    var = jnp.mean(jnp.square(y - mean), axis=-1, keepdims=True)
    yn = ((y - mean) * lax.rsqrt(var + RWKV_LN_EPS)).reshape(B, S, RWKV_WIDTH)
    yn = yn * lnx_w.astype(f32) + lnx_b.astype(f32)
    bonus = (jnp.sum(r4 * k4 * r_k.astype(f32), axis=-1, keepdims=True) * v4).reshape(B, S, RWKV_WIDTH)
    return ((yn + bonus) * g.astype(f32)).astype(p.dtype)

def dsa_group(p, pos):
    B, S, _ = p.shape
    f32 = jnp.float32
    G = ATT_HEADS // ATT_KV_HEADS
    q, k, v, qi, ki, wi = split_cols_2(p, ATT_SPLITS)
    q = partial_rope(q.reshape(B, S, ATT_HEADS, ATT_HEAD), pos)
    k = partial_rope(k.reshape(B, S, ATT_KV_HEADS, ATT_HEAD), pos)
    v = v.reshape(B, S, ATT_KV_HEADS, ATT_HEAD)
    qi = partial_rope(qi.reshape(B, S, IDX_HEADS, IDX_HEAD), pos)
    ki = partial_rope(ki.reshape(B, S, 1, IDX_HEAD), pos)[:, :, 0].astype(f32)
    wi = wi.astype(f32) * (IDX_HEADS ** -0.5 * IDX_HEAD ** -0.5)
    n_sel = min(TOPK_MAX, S // 4)
    nblk = S // Q_BLOCK
    key_pos = jnp.arange(S)
    gather = jax.vmap(lambda t, i: t[i])

    def to_blocks(t):
        return jnp.swapaxes(t.reshape((B, nblk, Q_BLOCK) + t.shape[2:]), 0, 1)

    def block(args):
        bi, qb, qib, wib = args
        q_pos = bi * Q_BLOCK + jnp.arange(Q_BLOCK)
        rel = jax.nn.relu(jnp.einsum('bqhd,bsd->bqhs', qib.astype(f32), ki))
        score = jnp.einsum('bqhs,bqh->bqs', rel, wib)
        causal = key_pos[None, :] <= q_pos[:, None]
        score = jnp.where(causal[None], score, -1e30)
        _, idx = lax.top_k(score, n_sel)
        valid = idx <= q_pos[None, :, None]
        kg = gather(k, idx)
        vg = gather(v, idx)
        qg = qb.reshape(B, Q_BLOCK, ATT_KV_HEADS, G, ATT_HEAD)
        s = jnp.einsum('bqhgd,bqkhd->bqhgk', qg, kg).astype(f32) * (ATT_HEAD ** -0.5)
        s = jnp.where(valid[:, :, None, None, :], s, -jnp.inf)
        prob = jax.nn.softmax(s, axis=-1).astype(vg.dtype)
        o = jnp.einsum('bqhgk,bqkhd->bqhgd', prob, vg)
        return o.reshape(B, Q_BLOCK, ATT_WIDTH)

    out = lax.map(block, (jnp.arange(nblk), to_blocks(q), to_blocks(qi), to_blocks(wi)))
    return jnp.swapaxes(out, 0, 1).reshape(B, S, ATT_WIDTH)

def memory_cross_attention(hn, mem_n, w_q, w_kv, w_o):
    B, S, _ = hn.shape
    M = mem_n.shape[1]
    q = (hn @ w_q).reshape(B, S, CROSS_HEADS, CROSS_HEAD)
    k, v = split_cols_2(mem_n @ w_kv, (CROSS_HEADS * CROSS_HEAD, CROSS_HEADS * CROSS_HEAD))
    k = k.reshape(B, M, CROSS_HEADS, CROSS_HEAD)
    v = v.reshape(B, M, CROSS_HEADS, CROSS_HEAD)
    s = jnp.einsum('bshd,bmhd->bhsm', q, k).astype(jnp.float32) * (CROSS_HEAD ** -0.5)
    prob = jax.nn.softmax(s, axis=-1).astype(v.dtype)
    o = jnp.einsum('bhsm,bmhd->bshd', prob, v).reshape(B, S, CROSS_HEADS * CROSS_HEAD)
    return o @ w_o

def second_inputs(seed: int = 0) -> dict:
    key = jax.random.key(seed)
    ks = jax.random.split(key, 32)
    f32 = jnp.float32
    L = DEPTH_2

    def dense(k, fan_in, shape):
        return jax.random.normal(k, shape, f32) * fan_in ** -0.5

    def gain(k, shape):
        return 1.0 + 0.02 * jax.random.normal(k, shape, f32)

    return {
        'x': jax.random.normal(ks[0], (BATCH, SEQ, D_MODEL), f32),
        'mem': jax.random.normal(ks[1], (BATCH, N_MEM, D_MODEL), f32),
        'positions': jnp.tile(jnp.arange(SEQ, dtype=jnp.int32)[None, :], (BATCH, 1)),
        'norm_mix': gain(ks[2], (L, D_MODEL)),
        'w_in': dense(ks[3], D_MODEL, (L, D_MODEL, IN_COLS)),
        'rwkv_mu': jax.random.uniform(ks[4], (L, RWKV_COLS), f32),
        'w_decay0': jax.random.uniform(ks[5], (L, RWKV_WIDTH), f32, -6.0, 1.0),
        'w_decay_up': dense(ks[6], DECAY_LORA, (L, DECAY_LORA, RWKV_WIDTH)),
        'a0': 0.1 * jax.random.normal(ks[7], (L, RWKV_WIDTH), f32),
        'a_up': dense(ks[8], AAA_LORA, (L, AAA_LORA, RWKV_WIDTH)),
        'g_up': dense(ks[9], GATE_LORA, (L, GATE_LORA, RWKV_WIDTH)),
        'k_k': 0.85 + 0.05 * jax.random.normal(ks[10], (L, RWKV_WIDTH), f32),
        'k_a': 1.0 + 0.05 * jax.random.normal(ks[11], (L, RWKV_WIDTH), f32),
        'r_k': 0.1 * jax.random.normal(ks[12], (L, RWKV_HEADS, RWKV_HEAD), f32),
        'lnx_w': gain(ks[13], (L, RWKV_WIDTH)),
        'lnx_b': 0.02 * jax.random.normal(ks[14], (L, RWKV_WIDTH), f32),
        'w_mix_out': dense(ks[15], MIX_WIDTH, (L, MIX_WIDTH, D_MODEL)),
        'norm_cross': gain(ks[16], (L, D_MODEL)),
        'norm_mem': gain(ks[17], (L, D_MODEL)),
        'w_q_cross': dense(ks[18], D_MODEL, (L, D_MODEL, CROSS_HEADS * CROSS_HEAD)),
        'w_kv_cross': dense(ks[19], D_MODEL, (L, D_MODEL, 2 * CROSS_HEADS * CROSS_HEAD)),
        'w_o_cross': dense(ks[20], CROSS_HEADS * CROSS_HEAD, (L, CROSS_HEADS * CROSS_HEAD, D_MODEL)),
        'norm_mlp': gain(ks[21], (L, D_MODEL)),
        'w_up': dense(ks[22], D_MODEL, (L, D_MODEL, D_FF)),
        'w_down': dense(ks[23], D_FF, (L, D_FF, D_MODEL)),
        'norm_final': gain(ks[24], (D_MODEL,)),
    }

def second_block(x, mem, positions, norm_mix, w_in, rwkv_mu, w_decay0, w_decay_up, a0, a_up, g_up,
              k_k, k_a, r_k, lnx_w, lnx_b, w_mix_out, norm_cross, norm_mem, w_q_cross,
              w_kv_cross, w_o_cross, norm_mlp, w_up, w_down, norm_final):
    h = x
    for l in range(DEPTH_2):
        p = rms_norm_2(h, norm_mix[l]) @ w_in[l]
        y_rwkv = rwkv7_group(p[..., :RWKV_COLS], rwkv_mu[l], w_decay0[l], w_decay_up[l], a0[l],
                             a_up[l], g_up[l], k_k[l], k_a[l], r_k[l], lnx_w[l], lnx_b[l])
        y_att = dsa_group(p[..., RWKV_COLS:], positions)
        h = h + jnp.concatenate([y_rwkv, y_att], axis=-1) @ w_mix_out[l]
        h = h + memory_cross_attention(rms_norm_2(h, norm_cross[l]), rms_norm_2(mem, norm_mem[l]),
                                       w_q_cross[l], w_kv_cross[l], w_o_cross[l])
        u = rms_norm_2(h, norm_mlp[l]) @ w_up[l]
        h = h + jnp.square(jax.nn.relu(u)) @ w_down[l]
    return rms_norm_2(h, norm_final)


def setup_inputs(seed=0):
    out = dict(first_inputs(seed))
    for name, value in second_inputs(seed + 1).items():
        if name != "x":
            out[name + "_2"] = value
    return out


def reference(
    x, c, ctx, c_ctx, w_ada, b_ada, ln_g, ln_b, w_in_e, w_gate_f, b_gate_f, w_gate_b, b_gate_b,
    gla_norm_w, conv_w, w_out_e, w_in_o, w_pool, pool_scale, w_out_o, mem_2, positions_2,
    norm_mix_2, w_in_2, rwkv_mu_2, w_decay0_2, w_decay_up_2, a0_2, a_up_2, g_up_2, k_k_2, k_a_2,
    r_k_2, lnx_w_2, lnx_b_2, w_mix_out_2, norm_cross_2, norm_mem_2, w_q_cross_2, w_kv_cross_2,
    w_o_cross_2, norm_mlp_2, w_up_2, w_down_2, norm_final_2,
):
    x = first_block(
        x, c, ctx, c_ctx, w_ada, b_ada, ln_g, ln_b, w_in_e, w_gate_f, b_gate_f, w_gate_b,
        b_gate_b, gla_norm_w, conv_w, w_out_e, w_in_o, w_pool, pool_scale, w_out_o,
    )
    return second_block(
        x, mem_2, positions_2, norm_mix_2, w_in_2, rwkv_mu_2, w_decay0_2, w_decay_up_2, a0_2,
        a_up_2, g_up_2, k_k_2, k_a_2, r_k_2, lnx_w_2, lnx_b_2, w_mix_out_2, norm_cross_2,
        norm_mem_2, w_q_cross_2, w_kv_cross_2, w_o_cross_2, norm_mlp_2, w_up_2, w_down_2,
        norm_final_2,
    )


_drawn_inputs = setup_inputs


def setup_inputs(seed=0):
    import zlib

    import numpy as np

    out = dict(_drawn_inputs(seed))
    spreads = {}
    factors = {'ctx': 3.641,
     'c_ctx': 5.223,
     'b_ada': 3.533,
     'w_gate_f': 4.601,
     'b_gate_f': 8.0,
     'w_gate_b': 5.102,
     'b_gate_b': 8.0,
     'gla_norm_w': 8.0,
     'pool_scale': 8.0,
     'w_decay_up_2': 2.754,
     'a0_2': 3.759,
     'k_k_2': 4.012,
     'lnx_w_2': 6.905,
     'lnx_b_2': 7.772,
     'norm_cross_2': 8.0,
     'norm_mem_2': 8.0,
     'norm_mlp_2': 9.501,
     'norm_final_2': 8.131}
    for name, (base, spread) in spreads.items():
        noise = np.random.default_rng([zlib.crc32(name.encode()), seed]).standard_normal(out[name].shape)
        drawn = base * np.exp(spread * noise) if base else spread * noise
        out[name] = jnp.asarray(drawn.astype(out[name].dtype))
    for name, factor in factors.items():
        out[name] = (out[name] * factor).astype(out[name].dtype)
    return out
```

```python
from contextlib import ExitStack

import numpy as np

import concourse.bass as bass
from concourse import mybir

F32 = mybir.dt.float32
F32R = mybir.dt.float32r
I32 = mybir.dt.int32
ALU = mybir.AluOpType
ACT = mybir.ActivationFunctionType
AX = mybir.AxisListType

STOP = None
P = 128
T = 256
D = 2048
NB = 512
KT = D // P
HEADS, DK = 4, 256
ROW = 64
EPS = 1e-5
ALPHA = 4.0 ** 0.25


def packed(parts, first=0):
    at, n = {}, first
    for name, m in parts:
        at[name] = (n, m.shape[1])
        n += m.shape[1]
    return at, np.concatenate([m for _, m in parts], 1).astype(np.float32)


J_ = np.arange(P)[:, None]
I_ = np.arange(P)[None, :]


def common_constants():
    comb = np.zeros((P, 2))
    comb[[0, 1, 4], 0] = 1
    comb[[2, 3, 4], 1] = 1
    wide = np.zeros((P, P))
    wide[[0, 1, 4]] = 1
    return packed([("ident", (J_ == I_) * 1.0), ("comb", comb), ("comb_wide", wide)])


COMMON = P + 2 + P


def gla_constants():
    tau = 1.0 / 16.0
    parts = [("le", (J_ <= I_) * tau), ("ones16", np.full((P, P), tau)), ("ge", (J_ >= I_) * tau),
             ("gt", (J_ > I_) * tau), ("lt", (J_ < I_) * tau)]
    for d in range(2):
        for l in range(7):
            b = 1 << l
            m = (J_ // (2 * b) == I_ // (2 * b)) & (J_ // b % 2 == d) & (I_ // b % 2 == 1 - d)
            parts.append((f"mask{d}_{l}", m * 1.0))
    return packed(parts, COMMON)


def pool_constants():
    t = np.arange(T)
    parts = []
    rows = T // ROW
    for w in (2, 4, 8):
        m = np.zeros((T, T))
        for r in range(rows):
            lo, hi = max(r - w // 2, 0), min(r + w - w // 2, rows)
            for q in range(lo, hi):
                m[(q * ROW + np.arange(ROW)), (r * ROW + np.arange(ROW))] = np.float32(1.0 / (hi - lo))
        m[t, t] -= 1.0
        for h in range(2):
            parts.append((f"pool{w}_{h}", m[h * P:(h + 1) * P]))
    return packed(parts, COMMON)


C = 32
RH, RN = 16, 64


def second_constants():
    c = np.arange(C)[None, :]
    p = np.arange(P)[:, None]
    key = np.arange(T)[None, :]
    inv = 500000.0 ** (-np.arange(16, dtype=np.float32) / np.float32(16))
    parts = [("head_ones", (J_ // RN == I_ // RN) * 1.0), ("head_mean", (J_ // RN == I_ // RN) / RN),
             ("below", (c < p % C) * 1.0), ("above", (p % C < c) * 1.0), ("above_eq", (p % C <= c) * 1.0),
             ("restart", np.broadcast_to(np.arange(T) % C != 0, (P, T)) * 1.0),
             ("inv_freq", np.broadcast_to(inv, (P, 16)))]
    for h in range(2):
        parts.append((f"causal_{h}", np.where(key <= p + h * P, 0.0, -1e30)))
    parts.append(("eye32", np.broadcast_to(np.eye(C).reshape(1, -1), (P, C * C))))
    return packed(parts, COMMON)


COL_NAMES = ["c", "c_ctx", "conv_w0", "conv_w1", "conv_w2", "pool_scale", "norm_mix_2", "norm_cross_2",
             "norm_mem_2", "norm_mlp_2", "mu_r", "mu_k", "mu_v", "mu_lora", "w_decay0_2", "a0_2", "k_k_2", "k_a_2", "r_k_2",
             "lnx_w_2", "lnx_b_2"]
COL_TILES = [16, 16, 8, 8, 8, 16, 16, 16, 16, 16, 8, 8, 8, 3] + [8] * 7
COL_AT = {n: sum(COL_TILES[:k]) for k, n in enumerate(COL_NAMES)}
NCOLS = sum(COL_TILES)


class Stage:

    def __init__(self, name, view, nblk, n=NB, kc=4, loop=True, rows_only=False, dest=None, kt0=None, func=None,
                 x=None):
        self.name, self.view, self.nblk, self.n, self.kc = name, view, nblk, n, kc
        self.loop, self.rows_only, self.dest = loop, rows_only, dest
        self.kt0 = kt0 or (lambda blk: 0)
        self.func = func
        self.x = x


def build(nc, a, out, stop=None):
    ctx = ExitStack()
    BASE = 16512

    def place(name, kb, shape, dt=F32):
        assert kb * 1024 + int(np.prod(shape[1:])) * 4 <= 207.8 * 1024, name
        return nc.alloc_sbuf_tensor_at(name, shape, dt, offset=BASE + int(kb * 1024))

    sems = {}

    def S(name):
        if name not in sems:
            sems[name] = ctx.enter_context(nc.semaphore(name))
        return sems[name]

    RAW = place("weights_raw", 0, [P, 4, 4, NB])
    WHI = place("weights_hi", 32, [P, 2, 4, NB], F32R)
    WLO = place("weights_lo", 48, [P, 2, 4, NB], F32R)
    CM = place("cond_parts", 64, [P, 192], F32R)
    STAT = place("stats", 64.75, [P, 128])
    RN2 = place("gate_rank_rows", 65.25, [P, 2, 64])
    RT = place("gate_rank_T", 65.75, [64, T])
    MODT = place("modulation_cols", 66.75, [P, 48, 2])
    COLS = place("feature_cols", 67.25, [P, NCOLS])
    CONST = place("constants", 68.75, [P, 2752])
    XTH = place("acts_hi", 79.5, [P, KT, T], F32R)
    XTL = place("acts_lo", 95.5, [P, KT, T], F32R)
    NAT = place("natural_blocks", 111.5, [P, 16, 2, NB])
    XS = place("acts_T", 111.5, [P, KT, T])
    XS2 = place("acts_T_latent", 143.5, [P, KT, T])
    S0 = place("context_states", 175.5, [P, 2, HEADS, 2, DK])
    ADAROW = place("modulation_rows", 191.5, [5, 8 * NB])
    WG = place("gate_weights", 191.5, [64, 1024])
    W0 = place("decayed_a", 191.5, [P, 8, T])
    ACCD = place("scores_diag", 199.5, [P, HEADS, 2, P])
    ACCX = place("scores_cross", 203.5, [P, HEADS, 2, P])
    LA_C = place("log_decay_ctx", 127.5, [P, 2, 2, 2, NB])
    TMP_C = place("decay_ctx", 159.5, [P, 2, 2, NB])
    LA_L = place("log_decay", 79.5, [P, 2, 2, 2, NB])
    TMP_L = place("gate_tmp", 95.5, [P, 2, 2, NB])
    GB_ = place("cum_decay_b", 95.5, [P, 8, T])
    GF_ = place("cum_decay_f", 103.5, [P, 8, T])
    W1 = place("decayed_b", 79.5, [P, 8, T])
    MTMP = place("masked_scores", 87.5, [P, 4, P])
    QT = place("q_T", 159.5, [P, 8, T])
    KTT = place("k_T", 167.5, [P, 8, T])
    O = place("gla_out", 127.5, [P, 2, HEADS, DK])
    GNW = place("gla_norm_row", 91.5, [P, DK])
    P1T = place("conv_in_T", 159.5, [P, 8, T])
    P2T = place("conv_gate_T", 167.5, [P, 8, T])
    CV = place("conv_out_T", 199.5, [P, 8, T])
    XN = place("residual", 127.5, [P, 4, 2, NB])
    Y = place("projected", 143.5, [P, 4, 2, NB])
    GTB = place("gate_bcast", 159.5, [P, 4, NB])
    ADAROW2 = place("modulation_gate_row", 175.5, [5, 4 * NB])
    LNG = place("ln_gain_bcast", 183.5, [P, 4, NB])
    LNB = place("ln_bias_bcast", 191.5, [P, 4, NB])

    ADAROW1 = place("modulation_rows_1", 79.5, [5, 12 * NB])
    GTB1 = place("gate_bcast_1", 167.5, [P, 4, NB])
    NATO = place("pool_natural", 175.5, [P, 8, 2, NB])
    NR = place("rkv_natural", 143.5, [P, 6, 2, NB])
    NA = place("att_natural", 167.5, [P, 5, 2, NB])
    LORA = place("lora_natural", 187.5, [P, 2, 288])
    KIWI = place("index_key_natural", 189.75, [P, 2, 80])
    QTA = place("att_q_T", 79.5, [P, 8, T])
    QIT = place("index_q_T", 87.5, [P, 8, T])
    KTA = place("att_k_T", 95.5, [P, 2, T])
    KIT = place("index_k_T", 97.5, [P, T])
    SC = place("index_scores", 98.5, [P, 2, T])
    BIAS = place("att_bias", 100.5, [P, 2, T])
    RL = place("index_relu", 102.5, [P, 2, 2, T])
    SP = place("probs", 106.5, [P, 2, 2, T])
    PT = place("probs_T", 199.5, [P, 2, NB])
    ROPE = place("rope_angles", 203.5, [P, 8, 2, 16])
    ROT = place("rope_products", 204.5, [P, 4, 128])
    KI2 = place("index_key_twice", 206.5, [P, 2, P])
    RTT = place("r_T", 79.5, [P, 8, T])
    KTR = place("key_T", 87.5, [P, 8, T])
    VTR = place("value_T", 95.5, [P, 8, T])
    KK = place("unit_key_T", 103.5, [P, 8, T])
    WDU = place("decay_rate_up", 111.5, [P, 1024])
    TMPR = place("delta_tmp", 111.5, [P, 8, T])
    SIG = place("decay_T", 143.5, [P, 8, T])
    AT = place("rate_T", 151.5, [P, 8, T])
    GT = place("gate_T", 159.5, [P, 8, T])
    VN = place("value_nat", 175.5, [P, 2, 1024])
    LT = place("lora_T", 183.5, [P, 3, T])
    GU = place("gate_up", 191.5, [P, 2, 1024])
    NRM = place("norms_T", 191.5, [P, 8, T])
    LG = place("cum_decay_T", 199.5, [P, 8, T])
    GE = place("chunk_decay", 66.75, [P, 8, 8])
    BN = place("b_nat", 167.5, [P, 2, 1024])
    KN = place("key_nat", 183.5, [P, 2, 1024])
    AAB = place("a_ab", 191.5, [P, 32, C])
    AAK = place("a_ak", 111.5, [P, 32, C])
    ARB = place("a_rb", 115.5, [P, 32, C])
    ARK = place("a_rk", 143.5, [P, 32, C])
    TT = place("inverse_T", 147.5, [P, 32, C])
    AC = place("a_by_chunk", 195.5, [P, C, C])
    TC = place("inverse_by_chunk", 199.5, [P, C, C])
    TMPC = place("inverse_products", 203.5, [P, C * C])
    RS = place("chunk_rhs", 87.5, [P, 2, 1024])
    U = place("chunk_u", 151.5, [P, 2, 1024])
    ST = place("delta_state", 191.5, [P, 8, P])
    YT = place("delta_out_T", 167.5, [P, 8, T])
    SQ = place("delta_sq_T", 183.5, [P, 8, T])
    VAR = place("delta_var_T", 191.5, [P, 8, T])
    MEMN = place("memory_natural", 159.5, [P, 4, 2, NB])
    CQ = place("cross_q", 175.5, [P, 1, 2, NB])
    CKV = place("cross_kv", 179.5, [P, 2, 2, NB])
    CQT = place("cross_q_T", 187.5, [P, 4, T])
    CKT = place("cross_k_T", 191.5, [P, 4, T])
    CSP = place("cross_probs", 195.5, [P, 2, 2, T])
    CPT = place("cross_probs_T", 199.5, [P, 2, NB])
    UPN = place("hidden", 143.5, [P, 4, 2, NB])
    Y3 = place("down_out", 159.5, [P, 4, 2, NB])
    XTH2 = place("hidden_hi", 175.5, [P, KT, T], F32R)
    XTL2 = place("hidden_lo", 191.5, [P, KT, T], F32R)
    NFB = place("final_gain_bcast", 159.5, [P, 4, NB])

    BANKS = ctx.enter_context(nc.psum_tensor("banks", [P, 8, NB], F32))
    c_at = {}
    for f in (common_constants, gla_constants, pool_constants, second_constants):
        c_at.update(f()[0])

    def const(name, rows=P):
        o, n = c_at[name]
        return CONST[0:rows, o:o + n]

    def cols(name, f):
        return COLS[:, COL_AT[name] + f:COL_AT[name] + f + 1]

    ident = const("ident")

    def wv(w, r0, rows, c0, n):
        v = w[r0:r0 + rows, :].rearrange("(c k p) n -> c p k n", p=P, k=4)
        return lambda kc, blk: v[kc][:, :, bass.ds(c0 + blk * NB, n)]

    ada0, ada1 = a["w_ada"][0], a["w_ada"][1]
    ine = a["w_in_e"][0]
    stages = [
        Stage("ada0", wv(ada0, 0, D, 0, NB), 8, rows_only=True, dest=lambda b: ADAROW[0:4, bass.ds(b * NB, NB)]),
        Stage("ctx_kv", wv(ine, 0, D, 0, NB), 4, dest=lambda b, h: NAT[:, bass.ds(b, 1), h, :]),
        Stage("ctx_r", wv(ine, 0, D, 2048, 32), 1, n=32, loop=False, dest="rank"),
        Stage("lat_kv", wv(ine, 0, D, 0, NB), 4, dest=lambda b, h: NAT[:, bass.ds(b, 1), h, :]),
        Stage("lat_r", wv(ine, 0, D, 2048, 32), 1, n=32, loop=False, dest="rank"),
        Stage("lat_rest", wv(ine, 0, D, 2080, NB), 12, dest=lambda b, h: NAT[:, bass.ds(b + 4, 1), h, :]),
        Stage("gla_o", None, 2, loop=False),
        Stage("ada0_gate", wv(ada0, 0, D, 4096, NB), 4, rows_only=True,
              dest=lambda b: ADAROW2[0:4, bass.ds(b * NB, NB)]),
        Stage("out_e", wv(a["w_out_e"][0], 0, D, 0, NB), 4, dest=lambda b, h: Y[:, bass.ds(b, 1), h, :]),
        Stage("ada1", wv(ada1, 0, D, 0, NB), 12, rows_only=True, dest=lambda b: ADAROW1[0:4, bass.ds(b * NB, NB)]),
        Stage("in_o", wv(a["w_in_o"][0], 0, D, 0, NB), 8, dest=lambda b, h: NATO[:, bass.ds(b, 1), h, :]),
        Stage("pool", lambda kc, blk: a["w_pool"][0, blk].rearrange("(k p) n -> p k n", p=P), 4, kc=1, loop=False,
              kt0=lambda b: 4 * b, dest=lambda b, h: Y[:, b:b + 1, h, :]),
        Stage("out_o", wv(a["w_out_o"][0], 0, D, 0, NB), 4, dest=lambda b, h: Y[:, bass.ds(b, 1), h, :]),
        Stage("rkv", wv(a["w_in_2"][0], 0, D, 0, NB), 6, dest=lambda b, h: NR[:, bass.ds(b, 1), h, :]),
        Stage("lora", wv(a["w_in_2"][0], 0, D, 3072, 288), 1, n=288, loop=False, dest=lambda b, h: LORA[:, h, :]),
        Stage("att4", wv(a["w_in_2"][0], 0, D, 3360, NB), 4, dest=lambda b, h: NA[:, bass.ds(b, 1), h, :]),
        Stage("att1", wv(a["w_in_2"][0], 0, D, 5408, NB), 1, loop=False, dest=lambda b, h: NA[:, 4, h, :]),
        Stage("kiwi", wv(a["w_in_2"][0], 0, D, 5920, 80), 1, n=80, loop=False, dest=lambda b, h: KIWI[:, h, :]),
        Stage("delta_y", None, 2, loop=False),
        Stage("mix", wv(a["w_mix_out"][0], 0, D, 0, NB), 4, dest=lambda b, h: Y[:, bass.ds(b, 1), h, :]),
        Stage("cross_kv", wv(a["w_kv_cross"][0], 0, D, 0, NB), 2, dest=lambda b, h: CKV[:, bass.ds(b, 1), h, :]),
        Stage("cross_q", wv(a["w_q_cross"][0], 0, D, 0, NB), 1, loop=False, dest=lambda b, h: CQ[:, 0, h, :]),
        Stage("cross_o", lambda kc, blk: a["w_o_cross"][0][:, blk * NB:(blk + 1) * NB].rearrange(
              "(k p) n -> p k n", p=P), 4, kc=1, loop=False, dest=lambda b, h: Y[:, b:b + 1, h, :]),
    ]

    def up(q):
        return Stage(f"up{q}", wv(a["w_up"][0], 0, D, q * D, NB), 4, func=ACT.Relu,
                     dest=lambda b, h: UPN[:, bass.ds(b, 1), h, :])

    def down(q):
        return Stage(f"down{q}", wv(a["w_down"][0], q * D, D, 0, NB), 4, x=(XTH2, XTL2),
                     dest=lambda b, h: Y3[:, bass.ds(b, 1), h, :])

    FF = 4
    stages += [up(0), up(1), down(0), up(2), down(1), up(3), down(2), down(3)]
    if stop:
        stages = stages[:{"x1": 9, "x2": 13}[stop]]
    g = b = 0
    st = {}
    for s in stages:
        s.g0, s.b0 = g, b
        if s.view is not None:
            g += s.nblk * s.kc
        b += s.nblk + s.nblk % 2
        st[s.name] = s
        assert g % 4 == 0
    total_chunks = g

    job_counts = [("mod0", 1), ("ctx_rT", 1), ("ctx_z", 8), ("ctx_D0", 4), ("ctx_S0", 4), ("ctx_D1", 4), ("ctx_S1", 4),
                  ("lat_rT", 1), ("lat_z", 8), ("G0", 4), ("G1", 4), ("qT", 4), ("kT", 4), ("diag", 2)]
    for d in range(2):
        for l in range(8):
            job_counts.append((f"level{d}_{l}", 2 if l < 7 else 1))
    job_counts += [("yT", 4), ("p1T", 4), ("p2T", 4), ("gt0", 4)]
    job_counts += [("mod1", 1), ("gt1", 4), ("x1T", 8), ("zT", 8), ("pT", 8)]
    job_counts += [("x2T", 8), ("aqT", 4), ("akT", 1), ("aiT", 4), ("aiiT", 1), ("idx", 16)]

    def attention_jobs(pre, units):
        out_ = []
        for u in range(units + 1):
            if u < units:
                out_.append((f"{pre}_s{u}", 1))
            if u >= 1:
                out_ += [(f"{pre}_p{u - 1}", 1), (f"{pre}_o{u - 1}", 1)]
        return out_

    job_counts += attention_jobs("dsa", 8)
    job_counts += [("rT", 4), ("keyT", 4), ("valT", 4), ("loraT", 3), ("decay", 4), ("rate", 4), ("dgate", 4),
                   ("valN", 4), ("kknorm", 4), ("bonus", 4), ("bN", 4), ("keyN", 4), ("Aab", 8), ("Aak", 8),
                   ("Arb", 8), ("Ark", 8)]
    for c in range(8):
        job_counts += [(f"chunkR{c}", 2), (f"chunkU{c}", 2)]
        if c < 7:
            job_counts.append((f"chunkS{c}", 2))
    job_counts += [("ymean", 4), ("yvar", 4), ("memT", 8), ("x3T", 8), ("ckT", 2), ("cqT", 2)]
    job_counts += attention_jobs("cross", 4)
    job_counts += [("x4T", 8), ("h0T", 8), ("h1T", 8), ("h2T", 8), ("h3T", 8)]
    J, n = {}, 0
    for name, k in job_counts:
        J[name] = n
        n += k
    NJ = dict(job_counts)

    def bank(j):
        return BANKS[:, 4 + j % 4, :]

    def bank_free(eng, j):
        if j >= 4:
            eng.wait_ge(S(f"side_free{j % 4}"), j // 4)

    def bank_full(eng, j):
        eng.wait_ge(S(f"side_full{j % 4}"), j // 4 + 1)

    def full(ins, j):
        ins.then_inc(S(f"side_full{j % 4}"), 1)

    def free(ins, j):
        ins.then_inc(S(f"side_free{j % 4}"), 1)

    def index_head(j, e):
        return 4 * (j % 4) + 2 * e + j // 4 % 2

    def copied(eng, j):
        eng.wait_ge(S(f"side_free{j % 4}"), j // 4 + 1)

    def jobs_out(eng, name):
        last = J[name] + NJ[name]
        for q in range(4):
            k = (last - q + 3) // 4
            if k > 0:
                eng.wait_ge(S(f"side_free{q}"), k)

    class Chain:

        def __init__(self, eng, name):
            self.eng, self.sem, self.n = eng, S(name), 0

        def add(self, ins):
            ins.then_inc(self.sem, 1)
            self.n += 1

        def wait(self):
            if self.n:
                self.eng.wait_ge(self.sem, self.n)

        def link(self, ins):
            self.add(ins)
            self.wait()

        def done(self, name, k=1):
            self.wait()
            self.eng.sem_inc(S(name), k)

    landed = [S(f"chunk_landed{i}") for i in range(4)]
    hi_ready, lo_ready, chunk_used, block_out = S("hi_ready"), S("lo_ready"), S("chunk_used"), S("block_out")

    def acc(B, h):
        return BANKS[:, (B % 2) * 2 + h, :]

    ACTS = {"ctx": 1, "lat": 2, "out_e": 3, "in_o": 4, "pool": 5, "out_o": 6, "rkv": 7, "mix": 8, "cross_kv": 9,
            "cross_q": 10, "cross_o": 11, "up": 12, "h0": 13, "h1": 14, "h2": 15, "h3": 16}

    block = ctx.enter_context(nc.Block())

    @block.sync
    def _(eng):
        def load(s, blk, kc, g):
            if not isinstance(g, int) or g >= 4:
                eng.wait_ge(lo_ready, g - 3)
            sl = (s.kc * 0 + kc) if s.kc == 4 else g % 4
            eng.dma_start(RAW[:, sl, :, 0:s.n], s.view(kc, blk)).then_inc(landed[sl], 16)

        for s in stages:
            if s.view is None:
                continue
            if s.loop:
                first = 1 if s.g0 == 0 else 0
                for kc in range(4 * first):
                    load(s, 0, kc, kc)
                with eng.Fori(first, s.nblk) as i:
                    for kc in range(4):
                        load(s, i, kc, s.g0 + 4 * i + kc)
            else:
                for blk in range(s.nblk):
                    for kc in range(s.kc):
                        load(s, blk, kc, s.g0 + blk * s.kc + kc)

    def row_bcast(v):
        return v.rearrange("(a n) -> a n", a=1).to_broadcast([P, v.shape[0]])

    @block.gpsimd
    def _(eng):
        eng.dma_start(COLS[:, :], a["cols"]).then_inc(S("cols_in"), 16)
        eng.dma_start(CONST[:, 0:COMMON], a["common_consts"]).then_inc(S("consts_in"), 16)
        eng.dma_start(CONST[:, COMMON:COMMON + a["gla_consts"].shape[1]], a["gla_consts"]).then_inc(S("consts_in"), 16)
        eng.memset(RN2[:, :, :], 0.0).then_inc(S("rank_zeroed"), 1)
        eng.wait_ge(S("rank_zeroed"), 1)
        eng.memset(RN2[:, :, 16:17], 1.0).then_inc(S("rank_zeroed"), 1)
        eng.memset(RN2[:, :, 48:49], 1.0).then_inc(S("rank_zeroed"), 1)
        eng.dma_start(ADAROW[4:5, :], a["b_ada"][0:1, 0:4096]).then_inc(S("ada0_bias_in"), 16)
        eng.dma_start(XS[:, :, :], a["ctxT"]).then_inc(S("ctxT_in"), 16)
        eng.dma_start(XS2[:, :, :], a["xT"]).then_inc(S("xT_in"), 16)

        def gate_weights():
            eng.memset(WG[:, :], 0.0).then_inc(S("gate_w_zeroed"), 1)
            eng.wait_ge(S("gate_w_zeroed"), 1)
            eng.dma_start(WG[0:16, :], a["w_gate_f"][0]).then_inc(S("gate_w_in"), 16)
            eng.dma_start(WG[16:17, :], a["b_gate_f"]).then_inc(S("gate_w_in"), 16)
            eng.dma_start(WG[32:48, :], a["w_gate_b"][0]).then_inc(S("gate_w_in"), 16)
            eng.dma_start(WG[48:49, :], a["b_gate_b"]).then_inc(S("gate_w_in"), 16)

        jobs_out(eng, "mod0")
        gate_weights()
        eng.wait_ge(S("gla_o_out"), 1)
        eng.dma_start(GNW[:, :], row_bcast(a["gla_norm_w"][0])).then_inc(S("gnw_in"), 16)
        eng.dma_start(ADAROW2[4:5, :], a["b_ada"][0:1, 4096:6144]).then_inc(S("ada0_gate_bias_in"), 16)
        eng.dma_start(LNG[:, :, :].rearrange("p a b -> p (a b)"), row_bcast(a["ln_g"][0])).then_inc(S("ln_in"), 16)
        eng.wait_ge(S("scores_read"), 1)
        eng.dma_start(LNB[:, :, :].rearrange("p a b -> p (a b)"), row_bcast(a["ln_b"][0])).then_inc(S("ln_in"), 16)
        jobs_out(eng, "p2T")
        for h in range(2):
            eng.dma_start(XN[:, :, h, :], a["x"][0, h * P:(h + 1) * P, :].rearrange("p (b n) -> p b n", n=NB))\
               .then_inc(S("x_in"), 16)
        def store():
            for h in range(2):
                eng.dma_start(out[0, h * P:(h + 1) * P, :].rearrange("p (b n) -> p b n", n=NB), XN[:, :, h, :])\
                   .then_inc(S("stored"), 16)
            eng.wait_ge(S("stored"), 32)

        def natural(dst, src, sem):
            for h in range(2):
                eng.dma_start(dst[:, :, h, :], src[h * P:(h + 1) * P, :].rearrange("p (b n) -> p b n", n=NB))\
                   .then_inc(S(sem), 16)

        def bcast(dst, v, sem):
            eng.dma_start(dst[:, :, :].rearrange("p a b -> p (a b)"), row_bcast(v)).then_inc(S(sem), 16)

        eng.dma_start(CONST[:, COMMON:COMMON + 1536], a["pool_consts"]).then_inc(S("pool_consts_in"), 16)
        if stop == "x1":
            eng.wait_ge(S("x1_done"), 1)
            store()
            return
        eng.wait_ge(chunk_used, st["ada1"].g0 + 2)
        eng.dma_start(ADAROW1[4:5, :], a["b_ada"][1:2, :]).then_inc(S("ada1_bias_in"), 16)
        jobs_out(eng, "zT")
        eng.dma_start(CONST[:, COMMON:COMMON + a["second_consts"].shape[1]], a["second_consts"])\
           .then_inc(S("second_consts_in"), 16)
        bcast(LNG, a["ln_g"][1], "ln_in")
        eng.wait_ge(S("gated_z"), 1)
        bcast(LNB, a["ln_b"][1], "ln_in")
        if stop == "x2":
            eng.wait_ge(S("x2_done"), 1)
            store()
            return
        eng.wait_ge(S("x2_done"), 1)
        eng.dma_start(ROPE[:, 7, 0, 0:2].bitcast(I32), a["positions"]).then_inc(S("positions_in"), 16)
        eng.wait_ge(S("acts_lo"), ACTS["rkv"])
        eng.dma_start(WDU[0:64, :], a["w_decay_up_2"][0]).then_inc(S("ups_in"), 16)
        eng.dma_start(WDU[64:128, :], a["a_up_2"][0]).then_inc(S("ups_in"), 16)
        eng.dma_start(GU[:, 0, :], a["g_up_2"][0, 0:128, :]).then_inc(S("ups_in"), 16)
        eng.dma_start(GU[0:32, 1, :], a["g_up_2"][0, 128:160, :]).then_inc(S("ups_in"), 16)
        eng.wait_ge(S("a_ab_ready"), 1)
        sa = a["scratch_a"].rearrange("(u c) t s -> c t u s", c=4)
        for c in range(4):
            eng.dma_start(sa[c], AAB[C * c:C * (c + 1), :, :]).then_inc(S("a_ab_stored"), 16)
        eng.wait_ge(S("a_ab_stored"), 64)
        eng.dma_start(AC[:, :, :], a["scratch_a"]).then_inc(S("a_by_chunk_in"), 16)
        eng.wait_ge(S("inverse_ready"), 1)
        eng.dma_start(a["scratch_t"], TC[:, :, :]).then_inc(S("inverse_stored"), 16)
        eng.wait_ge(S("inverse_stored"), 16)
        sb = a["scratch_t"].rearrange("(u c) s t -> c s u t", c=4)
        for c in range(4):
            eng.dma_start(TT[C * c:C * (c + 1), :, :], sb[c]).then_inc(S("inverse_in"), 16)
        eng.wait_ge(S("y_delta"), 1)
        natural(MEMN, a["mem"][0], "mem_in")
        eng.wait_ge(S("h_summed"), 1 + FF)
        bcast(NFB, a["norm_final_2"], "final_gain_in")
        eng.wait_ge(S("out_ready"), 1)
        store()

    @block.scalar
    def _(eng):
        ch = Chain(eng, "act_steps")

        def cut_hi(kc, g):
            sl = kc
            eng.wait_ge(landed[sl], 16 * (g // 4 + 1) if isinstance(g, int) else g)
            return sl

        def hi(s, g0, i, c):
            sl = c % 4
            n = s.n
            eng.wait_ge(landed[sl], 16 * (g0 // 4 + i + c // 4 + 1))
            eng.wait_ge(chunk_used, g0 + 4 * i + c + 1)
            eng.activation(WHI[:, c % 2, :, 0:n], RAW[:, sl, :, 0:n], ACT.Copy).then_inc(hi_ready, 1)

        def evac(s, i, par, last=False):
            eng.wait_ge(chunk_used, s.g0 + s.kc * i + s.kc + 2)
            if s.rows_only:
                eng.activation(s.dest(i), BANKS[0:4, par * 2, :], ACT.Copy).then_inc(block_out, 2)
                return
            for h in range(2):
                src = BANKS[:, par * 2 + h, 0:s.n]
                if s.dest == "rank":
                    eng.activation(RN2[:, h, 0:16], src[:, 0:16], ACT.Copy).then_inc(S("rank_out"), 1)
                    eng.activation(RN2[:, h, 32:48], src[:, 16:32], ACT.Copy).then_inc(block_out, 1 if h == 0 else 3)
                else:
                    eng.activation(s.dest(i, h), src, s.func or ACT.Copy)\
                       .then_inc(block_out, 3 if h == 1 and s.nblk % 2 else 1)

        def stream(s):
            if s.loop:
                for c in range(4):
                    hi(s, s.g0, 0, c)
                if s.nblk > 2:
                    with eng.Fori(0, s.nblk // 2 - 1) as j:
                        for c in range(4, 12):
                            hi(s, s.g0, 2 * j, c)
                            if c == 5:
                                evac(s, 2 * j, 0)
                            if c == 9:
                                evac(s, 2 * j + 1, 1)
                e = s.nblk - 2
                for c in range(4, 8):
                    hi(s, s.g0, e, c)
                    if c == 5:
                        evac(s, e, 0)
                evac(s, e + 1, 1)
            else:
                for c in range(s.nblk * s.kc):
                    hi(s, s.g0, 0, c)
                    if c % s.kc == s.kc - 1 and c >= s.kc:
                        evac(s, c // s.kc - 1, (c // s.kc - 1) % 2)
                evac(s, s.nblk - 1, (s.nblk - 1) % 2)

        def silu_c():
            eng.wait_ge(S("cols_in"), 16)
            ch.link(eng.activation(STAT[:, 0:32], COLS[:, 0:32], ACT.Silu))
            src = STAT[:, 0:32].rearrange("p (v k) -> p v k", v=2)
            eng.wait_ge(S("cond_zeroed"), 1)
            ch.add(eng.activation(CM[:, 0:64].rearrange("p (k v e) -> p e v k", v=2, e=2)[:, 0], src, ACT.Copy))
            ch.done("cond_hi")

        def split_hi(src, ready, dst=None):
            ready()
            ch.add(eng.activation(XTH[:, :, :] if dst is None else dst, src, ACT.Copy))
            ch.done("acts_hi")

        def modulate(X, col, dma_sem):
            eng.wait_ge(S(dma_sem), 16)
            eng.wait_ge(S("mod0_ready"), 1)
            for k in range(KT):
                ch.add(eng.activation(X[:, k, :], X[:, k, :], ACT.Identity, scale=MODT[:, 16 + k, col:col + 1],
                                      bias=MODT[:, k, col:col + 1]))
            ch.done("modulated")

        roots = [0]

        def root(v):
            roots[0] += 1
            eng.wait_ge(S("square_in"), roots[0])
            ch.add(eng.activation(v, v, ACT.Sqrt))
            ch.done("root_out")

        def gate_logs(pre, LA, TMP):
            bank_full(eng, J[pre + "_rT"])
            free(eng.activation(RT[:, :], bank(J[pre + "_rT"])[0:64, 0:T], ACT.Copy), J[pre + "_rT"])
            for j in range(8):
                d, h, cb = j // 4, j // 2 % 2, j % 2
                jj = J[pre + "_z"] + j
                bank_full(eng, jj)
                free(eng.activation(LA[:, d, cb, h, :], bank(jj), ACT.Copy), jj)
            for d in range(2):
                eng.wait_ge(S("neg_abs"), (1 if pre == "ctx" else 3) + d)
                ch.link(eng.activation(TMP[:, :, :, :], TMP[:, :, :, :], ACT.Exp))
                ch.add(eng.activation(TMP[:, :, :, :], TMP[:, :, :, :], ACT.Ln, bias=1.0))
                ch.done("log1p")

        silu_c()
        stream(st["ada0"])
        modulate(XS, 1, "ctxT_in")
        split_hi(XS[:, :, :], lambda: ch.wait())
        stream(st["ctx_kv"])
        stream(st["ctx_r"])
        gate_logs("ctx", LA_C, TMP_C)
        for d in range(2):
            for j in range(4):
                jj = J[f"ctx_D{d}"] + j
                if j == 0:
                    if d == 0:
                        eng.wait_ge(S("ctx_la"), 1)
                    else:
                        eng.wait_ge(S("side_full%d" % ((J["ctx_S0"] + 3) % 4)), (J["ctx_S0"] + 3) // 4 + 1)
                bank_full(eng, jj)
                free(eng.activation(TMP_C[:, j % 2, j // 2, :], bank(jj), ACT.Exp), jj)
            for j in range(4):
                jj = J[f"ctx_S{d}"] + j
                bank_full(eng, jj)
                free(eng.activation(S0[:, d, j, :, :].rearrange("p a b -> p (a b)"), bank(jj), ACT.Copy), jj)
        modulate(XS2, 0, "xT_in")
        eng.wait_ge(chunk_used, st["ctx_r"].g0 + 4 + 2)
        split_hi(XS2[:, :, :], lambda: ch.wait())
        stream(st["lat_kv"])
        stream(st["lat_r"])
        stream(st["lat_rest"])
        eng.wait_ge(block_out, 4 + 2 * st["gla_o"].b0)
        ch.add(eng.activation(NAT[:, 6:8, :, :], NAT[:, 6:8, :, :], ACT.Silu))
        ch.add(eng.activation(NAT[:, 14:16, :, :], NAT[:, 14:16, :, :], ACT.Silu))
        ch.done("silu_gates")
        gate_logs("lat", LA_L, TMP_L)
        for j in range(4):
            jj = J["G0"] + j
            bank_full(eng, jj)
            free(eng.activation(GF_[:, 2 * j:2 * j + 2, :].rearrange("p a b -> p (a b)"), bank(jj), ACT.Copy), jj)
        for j in range(4):
            jj = J["G1"] + j
            bank_full(eng, jj)
            free(eng.activation(GB_[:, 2 * j:2 * j + 2, :].rearrange("p a b -> p (a b)"), bank(jj), ACT.Copy), jj)
        eng.wait_ge(S("mixed_products"), 1)
        for j in range(4):
            jj = J["qT"] + j
            bank_full(eng, jj)
            free(eng.activation(QT[:, 2 * j:2 * j + 2, :].rearrange("p a b -> p (a b)"), bank(jj), ACT.Copy,
                                scale=DK ** -0.5), jj)
        for j in range(4):
            jj = J["kT"] + j
            bank_full(eng, jj)
            free(eng.activation(KTT[:, 2 * j:2 * j + 2, :].rearrange("p a b -> p (a b)"), bank(jj), ACT.Copy), jj)
        for n in range(18):
            Wn = (W0, W1)[n % 2]
            if n < 16:
                eng.wait_ge(S("decay_args"), n + 1)
                ch.add(eng.activation(Wn[:, :, :], Wn[:, :, :], ACT.Exp))
            else:
                if n == 16:
                    jobs_out(eng, "level1_6")
                else:
                    jobs_out(eng, "level1_7")
                ch.add(eng.activation(Wn[:, :, :], (GF_, GB_)[n - 16][:, :, :], ACT.Exp))
            ch.done("decay_exp")
        s = st["gla_o"]
        for B in range(2):
            eng.wait_ge(S("gla_o_full"), B + 1)
            for h in range(2):
                eng.activation(O[:, B, 2 * h:2 * h + 2, :].rearrange("p a b -> p (a b)"), acc(B, h), ACT.Copy)\
                   .then_inc(block_out, 1)
        eng.wait_ge(block_out, 4 + 2 * (s.b0 + 2))
        eng.sem_inc(S("gla_o_out"), 1)
        for h in range(2):
            for k in range(HEADS):
                ch.add(eng.activation(MTMP[:, 0:2, :].rearrange("p a b -> p (a b)"), O[:, h, k, :], ACT.Square,
                                      accum_out=STAT[:, h * 4 + k:h * 4 + k + 1]))
                ch.wait()
        ch.done("o_squares")
        root(STAT[:, 0:8])
        for name, dst in (("p1T", P1T), ("p2T", P2T)):
            pass
        for name, dst in (("yT", XS), ("p1T", P1T), ("p2T", P2T)):
            for j in range(4):
                jj = J[name] + j
                bank_full(eng, jj)
                free(eng.activation(dst[:, 2 * j:2 * j + 2, :].rearrange("p a b -> p (a b)"), bank(jj), ACT.Copy), jj)
        stream(st["ada0_gate"])

        def ready():
            eng.wait_ge(S("conv_done"), 1)
            jobs_out(eng, "p2T")
        split_hi(XS[:, :, :], ready)
        jobs = range(J["gt0"], J["gt0"] + 4)
        for j, jj in enumerate(jobs):
            bank_full(eng, jj)
            free(eng.activation(GTB[:, j, :], bank(jj), ACT.Copy), jj)
        stream(st["out_e"])
        root(STAT[:, 66:71:4])

        if stop == "x1":
            return

        def tiles_out(name, dst, n=T, scale=None, bias=None, func=None, f0=0):
            for j in range(NJ[name]):
                jj = J[name] + j
                bank_full(eng, jj)
                if scale is None:
                    free(eng.activation(dst[:, f0 + 2 * j:f0 + 2 * j + 2, :].rearrange("p a b -> p (a b)"), bank(jj),
                                        func or ACT.Copy), jj)
                    continue
                for e in range(2):
                    f = 2 * j + e
                    ins = eng.activation(dst[:, f0 + f, :], bank(jj)[:, e * T:(e + 1) * T], func or ACT.Identity,
                                         scale=scale(f), bias=bias(f) if bias else 0.0)
                free(ins, jj)

        def wait_jobs(*names):
            for n in names:
                jobs_out(eng, n)

        stream(st["ada1"])
        for j in range(4):
            jj = J["gt1"] + j
            bank_full(eng, jj)
            free(eng.activation(GTB1[:, j, :], bank(jj), ACT.Copy), jj)
        eng.wait_ge(S("mod1_ready"), 1)
        tiles_out("x1T", XS, scale=lambda f: MODT[:, 16 + f, 0:1], bias=lambda f: MODT[:, f, 0:1])
        split_hi(XS[:, :, :], lambda: wait_jobs("x1T"))
        stream(st["in_o"])
        tiles_out("zT", XS)
        split_hi(XS[:, :, :], lambda: wait_jobs("zT"))
        eng.wait_ge(block_out, 4 + 2 * st["pool"].b0)
        ch.add(eng.activation(NATO[:, 4:8, :, :], NATO[:, 4:8, :, :], ACT.Silu))
        ch.done("silu_pool")
        stream(st["pool"])
        tiles_out("pT", XS, scale=lambda f: cols("pool_scale", f))
        split_hi(XS[:, :, :], lambda: wait_jobs("pT"))
        stream(st["out_o"])
        root(STAT[:, 66:71:4])
        if stop == "x2":
            return

        rms_count = [0]

        def rms_squares(src):
            rms_count[0] += 1
            eng.wait_ge(S("rms_in"), rms_count[0])
            for h in range(2):
                ch.link(eng.activation(NORMED[:, :, h, :], src[:, :, h, :], ACT.Square,
                                       accum_out=STAT[:, h:h + 1]))
            ch.done("rms_squares")
            root(STAT[:, 0:2])

        def softmax_rows(pre, units, SPb, PTb, dst, f0):
            def copies(u):
                pair, half = u // 2, u % 2
                jj = J[f"{pre}_p{u}"]
                if u >= 2:
                    bank_full(eng, J[f"{pre}_o{u - 2}"])
                bank_full(eng, jj)
                free(eng.activation(PTb[:, u % 2, :], bank(jj), ACT.Copy), jj)
                jj = J[f"{pre}_o{u}"]
                bank_full(eng, jj)
                free(eng.activation(dst[:, f0 + 2 * pair:f0 + 2 * pair + 2, half * P:(half + 1) * P],
                                    bank(jj)[:, 0:T].rearrange("p (a b) -> p a b", a=2), ACT.Copy), jj)

            for u in range(units):
                eng.wait_ge(S(pre + "_shifted"), u + 1)
                for e in range(2):
                    ch.add(eng.activation(SPb[:, u % 2, e, :], SPb[:, u % 2, e, :], ACT.Exp,
                                          bias=STAT[:, 64 + 4 * (u % 2) + e:65 + 4 * (u % 2) + e],
                                          accum_out=STAT[:, 66 + 4 * (u % 2) + e:67 + 4 * (u % 2) + e]))
                ch.done(pre + "_exp")
                if u >= 1:
                    copies(u - 1)
            copies(units - 1)

        NORMED = Y
        rms_squares(XN)
        tiles_out("x2T", XS, scale=lambda f: cols("norm_mix_2", f))
        split_hi(XS[:, :, :], lambda: wait_jobs("x2T"))
        for n in ("rkv", "lora", "att4", "att1", "kiwi"):
            stream(st[n])
        eng.wait_ge(S("angles"), 1)
        ch.add(eng.activation(ROPE[:, 0:2, :, :], ROPE[:, 2:4, :, :], ACT.Sin))
        ch.done("sines")
        tiles_out("aqT", QTA)
        jj = J["akT"]
        bank_full(eng, jj)
        free(eng.activation(KTA[:, :, :].rearrange("p a b -> p (a b)"), bank(jj), ACT.Copy), jj)
        tiles_out("aiT", QIT)
        jj = J["aiiT"]
        bank_full(eng, jj)
        free(eng.activation(KIT[:, :], bank(jj)[:, 0:T], ACT.Copy), jj)
        for j in range(16):
            jj = J["idx"] + j
            if j >= 2:
                eng.wait_ge(S("index_added"), j - 1)
            bank_full(eng, jj)
            free(eng.activation(RL[:, j % 2, :, :].rearrange("p a b -> p (a b)"), bank(jj), ACT.Relu), jj)
        softmax_rows("dsa", 8, SP, PT, XS, 8)
        tiles_out("rT", RTT)
        tiles_out("keyT", KTR)
        tiles_out("valT", VTR)
        for j, w in enumerate((P, P, 32)):
            jj = J["loraT"] + j
            bank_full(eng, jj)
            free(eng.activation(LT[0:w, j, :], bank(jj)[0:w, 0:T], ACT.Copy), jj)
        eng.wait_ge(S("lora_mixed"), 1)
        ch.add(eng.activation(LT[0:64, 0, :], LT[0:64, 0, :], ACT.Tanh))
        ch.add(eng.activation(LT[:, 1, :], LT[:, 1, :], ACT.Sigmoid))
        ch.add(eng.activation(LT[0:32, 2, :], LT[0:32, 2, :], ACT.Sigmoid))
        ch.done("lora_acts")
        tiles_out("decay", SIG, scale=lambda f: 1.0, bias=lambda f: cols("w_decay0_2", f), func=ACT.Sigmoid)
        tiles_out("rate", AT, scale=lambda f: 1.0, bias=lambda f: cols("a0_2", f), func=ACT.Sigmoid)
        tiles_out("dgate", GT)

        def natural_out(name, dst):
            for j in range(4):
                jj = J[name] + j
                bank_full(eng, jj)
                free(eng.activation(dst[:, j // 2, (j % 2) * NB:(j % 2 + 1) * NB], bank(jj), ACT.Copy), jj)

        natural_out("valN", VN)
        tiles_out("kknorm", NRM, func=ACT.Sqrt)
        DEC = float(np.exp(-0.5))
        eng.wait_ge(S("cum_ready"), 1)
        ch.add(eng.activation(NRM[:, :, :], LG[:, :, :], ACT.Exp, scale=DEC))
        ch.add(eng.activation(SIG[:, :, :], SIG[:, :, :], ACT.Exp, scale=-DEC))
        ch.done("inv_decay")
        eng.wait_ge(S("cum_read"), 1)
        ch.wait()
        ch.add(eng.activation(LG[:, :, :], LG[:, :, :], ACT.Exp, scale=-DEC))
        ch.done("decays")
        natural_out("bN", BN)
        natural_out("keyN", KN)
        for c in range(8):
            half, r = c // 4, slice(C * (c % 4), C * (c % 4) + C)
            for name, dst in ((f"chunkR{c}", RS), (f"chunkU{c}", U)):
                jj = J[name]
                bank_full(eng, jj)
                free(eng.activation(dst[r, half, 0:NB], bank(jj)[r, :], ACT.Copy), jj)
        s = st["delta_y"]
        eng.wait_ge(S("delta_y_full"), 1)
        for q in range(4):
            eng.activation(YT[:, 2 * q:2 * q + 2, :].rearrange("p a b -> p (a b)"), BANKS[:, q, :], ACT.Copy)\
               .then_inc(block_out, 1)
        eng.wait_ge(S("y_centred"), 1)
        ch.add(eng.activation(SQ[:, :, :], YT[:, :, :], ACT.Square))
        ch.done("y_squares")
        eng.wait_ge(S("y_var"), 1)
        ch.add(eng.activation(VAR[:, :, :], VAR[:, :, :], ACT.Sqrt))
        ch.done("y_std")
        split_hi(XS[:, :, :], lambda: eng.wait_ge(S("y_delta"), 1) or wait_jobs("dsa_o7"))
        stream(st["mix"])
        rms_squares(MEMN)
        tiles_out("memT", XS, scale=lambda f: cols("norm_mem_2", f))
        split_hi(XS[:, :, :], lambda: wait_jobs("memT"))
        stream(st["cross_kv"])
        rms_squares(XN)
        tiles_out("x3T", XS, scale=lambda f: cols("norm_cross_2", f))
        eng.wait_ge(chunk_used, st["cross_q"].g0 + 2)
        split_hi(XS[:, :, :], lambda: wait_jobs("x3T"))
        stream(st["cross_q"])
        tiles_out("ckT", CKT)
        tiles_out("cqT", CQT)
        softmax_rows("cross", 4, CSP, CPT, XS, 0)
        split_hi(XS[:, 0:4, :], lambda: wait_jobs("cross_o3"), XTH[:, 0:4, :])
        stream(st["cross_o"])
        rms_squares(XN)
        tiles_out("x4T", XS, scale=lambda f: cols("norm_mlp_2", f))
        split_hi(XS[:, :, :], lambda: wait_jobs("x4T"))
        stream(st["up0"])
        tiles_out("h0T", XS, func=ACT.Square)
        split_hi(XS[:, :, :], lambda: wait_jobs("h0T"), XTH2[:, :, :])
        stream(st["up1"])
        eng.wait_ge(S("acts_lo"), ACTS["h0"])
        tiles_out("h1T", XS, func=ACT.Square)
        for q in range(FF):
            stream(st[f"down{q}"])
            if q + 1 < FF:
                eng.wait_ge(chunk_used, st[f"down{q}"].g0 + 16 + 2)
                split_hi(XS[:, :, :], lambda: wait_jobs(f"h{q + 1}T"), XTH2[:, :, :])
            if q + 2 < FF:
                stream(st[f"up{q + 2}"])
                eng.wait_ge(S("acts_lo"), ACTS[f"h{q + 1}"])
                tiles_out(f"h{q + 2}T", XS, func=ACT.Square)
        NORMED = UPN
        rms_squares(XN)

    @block.vector
    def _(eng):
        ch = Chain(eng, "dve_steps")

        def lo(s, g0, i, c):
            n = s.n
            eng.wait_ge(hi_ready, g0 + 4 * i + c + 1)
            eng.tensor_tensor(WLO[:, c % 2, :, 0:n], RAW[:, c % 4, :, 0:n], WHI[:, c % 2, :, 0:n].bitcast(F32),
                              ALU.subtract).then_inc(lo_ready, 1)

        def stream(s):
            if s.loop:
                with eng.Fori(0, s.nblk) as i:
                    for c in range(4):
                        lo(s, s.g0, i, c)
            else:
                for c in range(s.nblk * s.kc):
                    lo(s, s.g0, 0, c)

        def split_lo(src, n, hi_=None, lo_=None):
            hi_ = XTH[:, :, :] if hi_ is None else hi_
            lo_ = XTL[:, :, :] if lo_ is None else lo_
            eng.wait_ge(S("acts_hi"), n)
            ch.add(eng.tensor_tensor(lo_, src, hi_.bitcast(F32), ALU.subtract))
            ch.done("acts_lo")

        roots = [0]

        def rsqrt(v):
            roots[0] += 1
            ch.done("square_in")
            eng.wait_ge(S("root_out"), roots[0])
            ch.link(eng.reciprocal(v, v))

        def gate_logs(pre, LA, TMP):
            jobs_out(eng, pre + "_z")
            for d in range(2):
                z = LA[:, d, :, :, :].rearrange("p a b c -> p (a b c)")
                t = TMP[:, :, :, :].rearrange("p a b c -> p (a b c)")
                ch.add(eng.scalar_tensor_tensor(out=t, in0=z, scalar=-1.0, in1=z, op0=ALU.mult, op1=ALU.min))
                ch.done("neg_abs")
                eng.wait_ge(S("log1p"), (1 if pre == "ctx" else 3) + d)
                ch.link(eng.scalar_tensor_tensor(out=z, in0=z, scalar=0.0, in1=t, op0=ALU.min, op1=ALU.subtract))
            ch.done(pre + "_la")

        eng.memset(CM[:, :].bitcast(F32), 0.0).then_inc(S("cond_zeroed"), 1)
        eng.sem_inc(block_out, 4)
        eng.wait_ge(S("cond_hi"), 1)
        e2 = CM[:, 0:64].rearrange("p (k v e) -> p e v k", v=2, e=2)
        ch.add(eng.tensor_tensor(e2[:, 1], STAT[:, 0:32].rearrange("p (v k) -> p v k", v=2), e2[:, 0].bitcast(F32),
                                 ALU.subtract))
        ch.done("cond_lo")
        stream(st["ada0"])
        jm = J["mod0"]
        bank_full(eng, jm)
        ch.add(eng.tensor_copy(MODT[:, 0:16, :].rearrange("p a b -> p (a b)"), bank(jm)[:, 0:32]))
        free(eng.tensor_scalar(MODT[:, 16:32, :].rearrange("p a b -> p (a b)"), bank(jm)[:, 32:64], 1.0, None,
                               ALU.add), jm)
        jobs_out(eng, "mod0")
        ch.done("mod0_ready")
        split_lo(XS[:, :, :], 1)
        stream(st["ctx_kv"])
        stream(st["ctx_r"])
        gate_logs("ctx", LA_C, TMP_C)
        for d in range(2):
            jobs_out(eng, f"ctx_D{d}")
            ch.add(eng.tensor_tensor(TMP_C[:, :, :, :].rearrange("p a b c -> p (a b c)"),
                                     TMP_C[:, :, :, :].rearrange("p a b c -> p (a b c)"),
                                     NAT[:, 0:2, :, :].rearrange("p a b c -> p (a b c)"), ALU.mult))
            ch.done("ctx_kd")
        split_lo(XS2[:, :, :], 2)
        stream(st["lat_kv"])
        stream(st["lat_r"])
        stream(st["lat_rest"])
        eng.wait_ge(S("silu_gates"), 1)
        ch.add(eng.tensor_tensor(NAT[:, 10:12, :, :].rearrange("p a b c -> p (a b c)"),
                                 NAT[:, 10:12, :, :].rearrange("p a b c -> p (a b c)"),
                                 NAT[:, 12:14, :, :].rearrange("p a b c -> p (a b c)"), ALU.mult))
        ch.add(eng.tensor_tensor(NAT[:, 8:10, :, :].rearrange("p a b c -> p (a b c)"),
                                 NAT[:, 8:10, :, :].rearrange("p a b c -> p (a b c)"),
                                 NAT[:, 14:16, :, :].rearrange("p a b c -> p (a b c)"), ALU.mult))
        ch.done("mixed_products")
        gate_logs("lat", LA_L, TMP_L)
        jobs_out(eng, "kT")
        steps = [(d, l) for d in range(2) for l in range(8)]

        def pairs(t, b):
            return t[:, :, :].rearrange("p f t -> p (f t)").rearrange("p (m two b) -> p two m b", two=2, b=b)

        def args(n):
            d, l = steps[n]
            b = 1 << l
            Wv, Gv = pairs((W0, W1)[n % 2], b), pairs((GF_, GB_)[d], b)
            m = 8 * T // (2 * b)
            if n >= 2:
                dd, ll = steps[n - 2]
                jobs_out(eng, f"level{dd}_{ll}")
            if d == 0:
                ref = Gv[:, 0, :, b - 1:b].to_broadcast([P, m, b])
                ch.add(eng.tensor_tensor(Wv[:, 0], ref, Gv[:, 0], ALU.subtract))
                ch.add(eng.tensor_tensor(Wv[:, 1], Gv[:, 1], ref, ALU.subtract))
            else:
                ref = Gv[:, 1, :, 0:1].to_broadcast([P, m, b])
                ch.add(eng.tensor_tensor(Wv[:, 0], Gv[:, 0], ref, ALU.subtract))
                ch.add(eng.tensor_tensor(Wv[:, 1], ref, Gv[:, 1], ALU.subtract))
            ch.done("decay_args")

        def factors(n):
            d, l = steps[n]
            b = 1 << l
            Wv = pairs((W0, W1)[n % 2], b)
            first, second = ((KTT, QT), (QT, KTT))[d]
            eng.wait_ge(S("decay_exp"), n + 1)
            ch.add(eng.tensor_tensor(Wv[:, 0], Wv[:, 0], pairs(first, b)[:, 0], ALU.mult))
            ch.add(eng.tensor_tensor(Wv[:, 1], Wv[:, 1], pairs(second, b)[:, 1], ALU.mult))
            ch.done("factors")

        def collect(n):
            d, l = steps[n]
            name = f"level{d}_{l}"
            if l == 7:
                jj = J[name]
                bank_full(eng, jj)
                free(eng.tensor_copy(ACCX[:, :, d, :], bank(jj).rearrange("p (a b) -> p a b", a=4)), jj)
                return
            for j in range(2):
                jj = J[name] + j
                bank_full(eng, jj)
                mask = const(f"mask{d}_{l}").rearrange("p (a b) -> p a b", a=1).to_broadcast([P, 4, P])
                ch.wait()
                free(eng.tensor_tensor(MTMP[:, :, :], bank(jj).rearrange("p (a b) -> p a b", a=4), mask, ALU.mult), jj)
                eng.wait_ge(S(f"side_free{jj % 4}"), jj // 4 + 1)
                dst = ACCD[:, 2 * j:2 * j + 2, :, :].rearrange("p a b c -> p (a b c)")
                ch.link(eng.tensor_tensor(dst, dst, MTMP[:, :, :].rearrange("p a b -> p (a b)"), ALU.add))

        for j in range(2):
            jj = J["diag"] + j
            bank_full(eng, jj)
            free(eng.scalar_tensor_tensor(out=ACCD[:, 2 * j:2 * j + 2, :, :].rearrange("p a b c -> p (a b) c"),
                                          in0=bank(jj).rearrange("p (a b) -> p a b", a=4), scalar=2.0,
                                          in1=ident.rearrange("p (a b) -> p a b", a=1).to_broadcast([P, 4, P]),
                                          op0=ALU.mult, op1=ALU.mult), jj)
        jobs_out(eng, "diag")
        args(0)
        for n in range(16):
            factors(n)
            if n >= 1:
                collect(n - 1)
            if n + 1 < 16:
                args(n + 1)
        collect(15)
        for n in (16, 17):
            eng.wait_ge(S("decay_exp"), n + 1)
            Wn = (W0, W1)[n % 2]
            ch.add(eng.tensor_tensor(Wn[:, :, :], Wn[:, :, :], QT[:, :, :], ALU.mult))
            ch.wait()
        jobs_out(eng, "level1_7")
        ch.done("state_factors")
        eng.wait_ge(S("o_squares"), 1)
        ch.link(eng.tensor_scalar(STAT[:, 0:8], STAT[:, 0:8], 1.0 / DK, EPS, ALU.mult, ALU.add))
        rsqrt(STAT[:, 0:8])
        eng.wait_ge(S("gnw_in"), 16)
        for h in range(2):
            for k in range(HEADS):
                ch.link(eng.scalar_tensor_tensor(out=O[:, h, k, :], in0=O[:, h, k, :],
                                                 scalar=STAT[:, h * 4 + k:h * 4 + k + 1], in1=GNW[:, :],
                                                 op0=ALU.mult, op1=ALU.mult))
        for h in range(2):
            ch.add(eng.tensor_tensor(O[:, h, :, :].rearrange("p (c k) v -> p c (k v)", c=2),
                                     O[:, h, :, :].rearrange("p (c k) v -> p c (k v)", c=2),
                                     NAT[:, 6:8, h, :], ALU.mult))
        ch.done("y_b")
        eng.sem_inc(S("scores_read"), 1)
        jobs_out(eng, "p2T")
        for f in range(8):
            x4 = P1T[:, f, :].rearrange("p (r c) -> p r c", c=ROW)
            o4 = CV[:, f, :].rearrange("p (r c) -> p r c", c=ROW)
            ch.link(eng.tensor_scalar(CV[:, f, :], P1T[:, f, :], cols("conv_w1", f), None, ALU.mult))
            ch.link(eng.scalar_tensor_tensor(out=o4[:, :, 1:ROW], in0=x4[:, :, 0:ROW - 1], scalar=cols("conv_w0", f),
                                             in1=o4[:, :, 1:ROW], op0=ALU.mult, op1=ALU.add))
            ch.link(eng.scalar_tensor_tensor(out=o4[:, :, 0:ROW - 1], in0=x4[:, :, 1:ROW], scalar=cols("conv_w2", f),
                                             in1=o4[:, :, 0:ROW - 1], op0=ALU.mult, op1=ALU.add))
            ch.add(eng.tensor_tensor(XS[:, 8 + f, :], CV[:, f, :], P2T[:, f, :], ALU.mult))
        ch.done("conv_done")
        stream(st["ada0_gate"])
        split_lo(XS[:, :, :], 3)
        stream(st["out_e"])

        def residual_norm(name, s, GTB):
            jobs_out(eng, name)
            eng.wait_ge(block_out, 4 + 2 * (s.b0 + s.nblk))
            for h in range(2):
                ch.add(eng.tensor_tensor(Y[:, :, h, :], Y[:, :, h, :], GTB[:, :, :], ALU.mult))
            ch.wait()
            ch.link(eng.scalar_tensor_tensor(out=XN[:, :, :, :].rearrange("p a b c -> p (a b c)"),
                                             in0=XN[:, :, :, :].rearrange("p a b c -> p (a b c)"), scalar=ALPHA,
                                             in1=Y[:, :, :, :].rearrange("p a b c -> p (a b c)"),
                                             op0=ALU.mult, op1=ALU.add))
            for h in range(2):
                for q in range(4):
                    ch.add(eng.bn_stats(STAT[:, h * 32 + 6 * q:h * 32 + 6 * q + 6], XN[:, q, h, :]))
            ch.wait()
            for h in range(2):
                ch.add(eng.bn_aggr(STAT[:, 64 + 4 * h:66 + 4 * h], STAT[:, h * 32:h * 32 + 24]))
            ch.wait()
            for h in range(2):
                ch.add(eng.tensor_scalar(STAT[:, 66 + 4 * h:67 + 4 * h], STAT[:, 65 + 4 * h:66 + 4 * h], EPS, None,
                                         ALU.add))
            rsqrt(STAT[:, 66:71:4])
            for h in range(2):
                ch.add(eng.tensor_scalar(XN[:, :, h, :], XN[:, :, h, :], STAT[:, 64 + 4 * h:65 + 4 * h],
                                         STAT[:, 66 + 4 * h:67 + 4 * h], ALU.subtract, ALU.mult))
            ch.wait()
            for h in range(2):
                ch.add(eng.tensor_tensor(XN[:, :, h, :], XN[:, :, h, :], LNG[:, :, :], ALU.mult))
            ch.wait()
            for h in range(2):
                ch.add(eng.tensor_tensor(XN[:, :, h, :], XN[:, :, h, :], LNB[:, :, :], ALU.add))

        eng.wait_ge(S("ln_in"), 32)
        eng.wait_ge(S("x_in"), 32)
        residual_norm("gt0", st["out_e"], GTB)
        ch.done("x1_done")
        if stop == "x1":
            return

        def flat(t):
            return t.rearrange("p a b c -> p (a b c)")

        stream(st["ada1"])
        jm = J["mod1"]
        bank_full(eng, jm)
        ch.add(eng.tensor_copy(MODT[:, 0:16, :].rearrange("p a b -> p (a b)"), bank(jm)[:, 0:32]))
        free(eng.tensor_scalar(MODT[:, 16:32, :].rearrange("p a b -> p (a b)"), bank(jm)[:, 32:64], 1.0, None,
                               ALU.add), jm)
        jobs_out(eng, "mod1")
        ch.done("mod1_ready")
        split_lo(XS[:, :, :], ACTS["in_o"])
        stream(st["in_o"])
        split_lo(XS[:, :, :], ACTS["pool"])
        stream(st["pool"])
        eng.wait_ge(S("silu_pool"), 1)
        eng.wait_ge(block_out, 4 + 2 * (st["pool"].b0 + 4))
        ch.add(eng.tensor_tensor(flat(Y[:, :, :, :]), flat(Y[:, :, :, :]), flat(NATO[:, 4:8, :, :]), ALU.mult))
        ch.done("gated_z")
        split_lo(XS[:, :, :], ACTS["out_o"])
        stream(st["out_o"])
        eng.wait_ge(S("ln_in"), 64)
        residual_norm("gt1", st["out_o"], GTB1)
        ch.done("x2_done")
        if stop == "x2":
            return

        def normed(src, dst, gain=None):
            ch.done("rms_in")
            normed.n += 1
            eng.wait_ge(S("rms_squares"), normed.n)
            ch.link(eng.tensor_scalar(STAT[:, 0:2], STAT[:, 0:2], 1.0 / D, EPS, ALU.mult, ALU.add))
            rsqrt(STAT[:, 0:2])
            for h in range(2):
                ch.add(eng.tensor_scalar(dst[:, :, h, :], src[:, :, h, :], STAT[:, h:h + 1], None, ALU.mult))
            ch.done("normed")

        normed.n = 0

        def softmax_rows(pre, units, SPb, scale, bias):
            for u in range(units):
                half = u % 2
                m, z = 64 + 4 * (u % 2), 66 + 4 * (u % 2)
                if u >= 2:
                    bank_full(eng, J[f"{pre}_p{u - 2}"])
                jj = J[f"{pre}_s{u}"]
                bank_full(eng, jj)
                sc = bank(jj).rearrange("p (a b) -> p a b", a=2)
                if bias is None:
                    free(eng.tensor_scalar(SPb[:, u % 2], sc, scale, None, ALU.mult), jj)
                else:
                    b = bias[:, half, :].rearrange("p (a b) -> p a b", a=1).to_broadcast([P, 2, T])
                    free(eng.scalar_tensor_tensor(out=SPb[:, u % 2], in0=sc, scalar=scale, in1=b, op0=ALU.mult,
                                                  op1=ALU.add), jj)
                copied(eng, jj)
                ch.link(eng.tensor_reduce(STAT[:, m:m + 2], SPb[:, u % 2], AX.X, ALU.max))
                ch.add(eng.tensor_scalar(STAT[:, m:m + 2], STAT[:, m:m + 2], -1.0, None, ALU.mult))
                ch.done(pre + "_shifted")
                eng.wait_ge(S(pre + "_exp"), u + 1)
                ch.link(eng.reciprocal(STAT[:, z:z + 2], STAT[:, z:z + 2]))
                for e in range(2):
                    ch.add(eng.tensor_scalar(SPb[:, u % 2, e, :], SPb[:, u % 2, e, :], STAT[:, z + e:z + e + 1], None,
                                             ALU.mult))
                ch.done(pre + "_probs")

        normed(XN, Y)
        split_lo(XS[:, :, :], ACTS["rkv"])
        for n in ("rkv", "lora", "att4", "att1", "kiwi"):
            stream(st[n])
        eng.wait_ge(S("positions_in"), 16)
        eng.wait_ge(S("second_consts_in"), 16)
        ch.link(eng.tensor_copy(ROPE[:, 6, 0, 0:2], ROPE[:, 7, 0, 0:2].bitcast(I32)))
        for h in range(2):
            ch.add(eng.tensor_scalar(ROPE[:, 2, h, :], const("inv_freq"), ROPE[:, 6, 0, h:h + 1], None, ALU.mult))
        ch.wait()
        magic = 1.5 * 2.0 ** 23
        ch.link(eng.tensor_scalar(ROPE[:, 4], ROPE[:, 2], float(1 / (2 * np.pi)), magic, ALU.mult, ALU.add))
        ch.link(eng.tensor_scalar(ROPE[:, 4], ROPE[:, 4], magic, None, ALU.subtract))
        for part in (-6.28125, -0.0019350051879882812, -3.019916050e-07):
            ch.link(eng.scalar_tensor_tensor(out=ROPE[:, 2], in0=ROPE[:, 4], scalar=part, in1=ROPE[:, 2],
                                             op0=ALU.mult, op1=ALU.add))
        ch.link(eng.tensor_scalar(ROPE[:, 3], ROPE[:, 2], float(np.pi / 2), None, ALU.add))
        ch.link(eng.tensor_scalar(ROPE[:, 4], ROPE[:, 3], float(np.pi), -float(2 * np.pi), ALU.is_gt, ALU.mult))
        ch.link(eng.tensor_tensor(ROPE[:, 3], ROPE[:, 3], ROPE[:, 4], ALU.add))
        ch.add(eng.tensor_scalar(ROPE[:, 2:4], ROPE[:, 2:4], 3.1415925, -3.1415925, ALU.min, ALU.max))
        ch.done("angles")
        eng.wait_ge(S("sines"), 1)
        eng.wait_ge(block_out, 4 + 2 * st["delta_y"].b0)

        def rope(x, heads, width, half, step):
            sin = ROPE[:, 0, rope.h, 0:16:step].rearrange("p (a b) -> p a b", a=1).to_broadcast([P, heads, half])
            cos = ROPE[:, 1, rope.h, 0:16:step].rearrange("p (a b) -> p a b", a=1).to_broadcast([P, heads, half])
            x1, x2 = x[:, :, 0:half], x[:, :, half:2 * half]
            t = [ROT[:, k, 0:heads * half].rearrange("p (a b) -> p a b", a=heads) for k in range(4)]
            ch.add(eng.tensor_tensor(t[0], x1, cos, ALU.mult))
            ch.add(eng.tensor_tensor(t[1], x2, sin, ALU.mult))
            ch.add(eng.tensor_tensor(t[2], x2, cos, ALU.mult))
            ch.link(eng.tensor_tensor(t[3], x1, sin, ALU.mult))
            ch.add(eng.tensor_tensor(x1, t[0], t[1], ALU.subtract))
            ch.link(eng.tensor_tensor(x2, t[2], t[3], ALU.add))

        for h in range(2):
            rope.h = h
            for b in range(2):
                rope(NA[:, b, h, :].rearrange("p (c d) -> p c d", d=128), 4, 128, 16, 1)
            rope(NA[:, 2, h, 0:256].rearrange("p (c d) -> p c d", d=128), 2, 128, 16, 1)
            for b in (3, 4):
                rope(NA[:, b, h, :].rearrange("p (c d) -> p c d", d=64), 8, 64, 8, 2)
            rope(KIWI[:, h, 0:64].rearrange("p (c d) -> p c d", d=64), 1, 64, 8, 2)
            for e in range(2):
                ch.add(eng.tensor_copy(KI2[:, h, e * 64:(e + 1) * 64], KIWI[:, h, 0:64]))
            ch.add(eng.tensor_scalar(KIWI[:, h, 64:80], KIWI[:, h, 64:80], 1.0 / 32.0, None, ALU.mult))
        ch.done("roped")
        ch.link(eng.memset(SC[:, :, :], 0.0))
        for j in range(16):
            half = j // 8
            jj = J["idx"] + j
            copied(eng, jj)
            for e in range(2):
                hd = index_head(j, e)
                ch.link(eng.scalar_tensor_tensor(out=SC[:, half, :], in0=RL[:, j % 2, e, :],
                                                 scalar=KIWI[:, half, 64 + hd:65 + hd], in1=SC[:, half, :],
                                                 op0=ALU.mult, op1=ALU.add))
            eng.sem_inc(S("index_added"), 1)
        for h in range(2):
            ch.link(eng.tensor_tensor(SC[:, h, :], SC[:, h, :], const(f"causal_{h}"), ALU.add))
        for r in range(8):
            for h in range(2):
                ch.add(eng.max(STAT[:, 72 + 8 * h:80 + 8 * h], SC[:, h, :]))
            ch.wait()
            for h in range(2):
                ch.add(eng.match_replace(SC[:, h, :], STAT[:, 72 + 8 * h:80 + 8 * h], SC[:, h, :], -3e38))
            ch.wait()
        ch.link(eng.tensor_scalar(BIAS[:, :, :], SC[:, :, :], -2e38, -1e30, ALU.is_ge, ALU.mult))
        for h in range(2):
            ch.add(eng.tensor_tensor(BIAS[:, h, :], BIAS[:, h, :], const(f"causal_{h}"), ALU.min))
        ch.wait()
        softmax_rows("dsa", 8, SP, 128.0 ** -0.5, BIAS)

        def mix(t, name, tile0, ntiles, rows=P, mu=None):
            d = TMPX[0:rows, 0:ntiles, :]
            x = t[0:rows, tile0:tile0 + ntiles, :]
            ch.add(eng.tensor_tensor(d[:, :, 1:T], x[:, :, 0:T - 1], x[:, :, 1:T], ALU.subtract))
            ch.link(eng.tensor_scalar(d[:, :, 0:1], x[:, :, 0:1], -1.0, None, ALU.mult))
            for f in range(ntiles):
                ch.add(eng.scalar_tensor_tensor(out=x[:, f, :], in0=d[:, f, :], scalar=mu(f)[0:rows, :],
                                                in1=x[:, f, :], op0=ALU.mult, op1=ALU.add))
            ch.wait()

        TMPX = KK
        jobs_out(eng, "dsa_o7")
        jobs_out(eng, "loraT")
        mix(LT, "lora", 0, 2, mu=lambda f: cols("mu_lora", f))
        mix(LT, "lora", 2, 1, 32, mu=lambda f: cols("mu_lora", 2))
        ch.done("lora_mixed")
        for t, name in ((VTR, "mu_v"), (KTR, "mu_k"), (RTT, "mu_r")):
            mix(t, name, 0, 8, mu=lambda f: cols(name, f))
            ch.done("mixed")

        def tt(o, x, y, op):
            ch.link(eng.tensor_tensor(o[:, :, :], x[:, :, :], y[:, :, :], op))

        for f in range(8):
            ch.add(eng.tensor_scalar(KK[:, f, :], KTR[:, f, :], cols("k_k_2", f), None, ALU.mult))
        ch.wait()
        jobs_out(eng, "rate")
        tt(TMPR, KK, KK, ALU.mult)
        ch.done("kk_squares")
        jobs_out(eng, "kknorm")
        ch.link(eng.tensor_scalar(NRM[:, :, :], NRM[:, :, :], 1e-12, None, ALU.max))
        ch.link(eng.reciprocal(NRM[:, :, :], NRM[:, :, :]))
        tt(KK, KK, NRM, ALU.mult)
        for f in range(8):
            ch.add(eng.tensor_scalar(TMPR[:, f, :], AT[:, f, :], -1.0, cols("k_a_2", f), ALU.add, ALU.mult))
        ch.wait()
        ch.link(eng.scalar_tensor_tensor(out=KTR[:, :, :], in0=TMPR[:, :, :], scalar=1.0, in1=KTR[:, :, :],
                                         op0=ALU.add, op1=ALU.mult))
        for f in range(8):
            ch.add(eng.scalar_tensor_tensor(out=TMPR[:, f, :], in0=RTT[:, f, :], scalar=cols("r_k_2", f),
                                            in1=KTR[:, f, :], op0=ALU.mult, op1=ALU.mult))
        ch.done("bonus_in")
        tt(AT, KK, AT, ALU.mult)
        for f in range(8):
            ch.add(eng.tensor_tensor_scan(LG[:, f, :], const("restart"), SIG[:, f, :], 0.0, ALU.mult, ALU.add))
        ch.wait()
        tt(SIG, LG, SIG, ALU.subtract)
        ch.done("cum_ready")
        eng.wait_ge(S("inv_decay"), 1)
        tt(KTR, KTR, NRM, ALU.mult)
        tt(AT, AT, NRM, ALU.mult)
        ch.link(eng.scalar_tensor_tensor(out=KK[:, :, :], in0=KK[:, :, :], scalar=-1.0, in1=SIG[:, :, :],
                                         op0=ALU.mult, op1=ALU.mult))
        ch.done("cum_read")
        eng.wait_ge(S("decays"), 1)
        tt(RTT, RTT, LG, ALU.mult)
        ch.link(eng.tensor_copy(GE[:, :, :], LG[:, :, C - 1:T:C]))
        ch.done("scaled")
        for j in range(4):
            jj = J["bonus"] + j
            bank_full(eng, jj)
            v = VTR[:, 2 * j:2 * j + 2, :].rearrange("p a b -> p (a b)")
            free(eng.tensor_tensor(v, v, bank(jj), ALU.mult), jj)

        def collect(name, dst, mask):
            for j in range(8):
                jj = J[name] + j
                bank_full(eng, jj)
                for c in range(4):
                    r = slice(C * c, C * (c + 1))
                    ins = eng.tensor_tensor(dst[r, 4 * j:4 * j + 4, :],
                                            bank(jj)[r, :].rearrange("p (u q) -> p u q", u=4)[:, :, C * c:C * (c + 1)],
                                            const(mask)[r, :].rearrange("p (a b) -> p a b", a=1)
                                            .to_broadcast([C, 4, C]), ALU.mult)
                free(ins, jj)

        jobs_out(eng, "keyN")
        collect("Aab", AAB, "below")
        jobs_out(eng, "Aab")
        eng.sem_inc(S("a_ab_ready"), 1)
        collect("Aak", AAK, "above")
        collect("Arb", ARB, "above_eq")
        collect("Ark", ARK, "above_eq")
        eng.wait_ge(S("a_by_chunk_in"), 16)
        jobs_out(eng, "Ark")
        ch.link(eng.tensor_copy(TC[:, :, :].rearrange("p a b -> p (a b)"), const("eye32")))
        for t in range(1, C):
            prod = TMPC[:, 0:t * t].rearrange("p (s r) -> p s r", s=t)
            ch.link(eng.tensor_tensor(prod, TC[:, 0:t, 0:t], AC[:, t:t + 1, 0:t].to_broadcast([P, t, t]), ALU.mult))
            ch.link(eng.tensor_reduce(TC[:, 0:t, t:t + 1], prod, AX.X, ALU.add))
        ch.done("inverse_ready")
        eng.wait_ge(S("a_by_chunk_in"), 16)
        ch.link(eng.memset(ST[:, :, :], 0.0))
        ch.done("state_ready")
        for c in range(8):
            half, r = c // 4, slice(C * (c % 4), C * (c % 4) + C)
            for name, dst in ((f"chunkR{c}", RS), (f"chunkU{c}", U)):
                jj = J[name] + 1
                bank_full(eng, jj)
                free(eng.tensor_copy(dst[r, half, NB:2 * NB], bank(jj)[r, :]), jj)
            if c == 7:
                break
            for b in range(2):
                jj = J[f"chunkS{c}"] + b
                bank_full(eng, jj)
                for p in range(2):
                    q = slice(RN * p, RN * (p + 1))
                    dst = ST[q, 4 * b:4 * b + 4, RN * p:RN * (p + 1)]
                    src = bank(jj)[q, :].rearrange("p (f v) -> p f v", f=4)[:, :, RN * p:RN * (p + 1)]
                    ins = eng.tensor_tensor(dst, dst, src, ALU.add)
                free(ins, jj)
            jobs_out(eng, f"chunkS{c}")
            for p in range(2):
                q = slice(RN * p, RN * (p + 1))
                dst = ST[q, :, RN * p:RN * (p + 1)]
                ch.add(eng.tensor_tensor(dst, dst, GE[q, :, c:c + 1].to_broadcast([RN, 8, RN]), ALU.mult))
            ch.done("state_ready")
        eng.wait_ge(block_out, 4 + 2 * (st["delta_y"].b0 + 2))
        for j in range(4):
            jj = J["ymean"] + j
            bank_full(eng, jj)
            y = YT[:, 2 * j:2 * j + 2, :].rearrange("p a b -> p (a b)")
            free(eng.tensor_tensor(y, y, bank(jj), ALU.subtract), jj)
        jobs_out(eng, "ymean")
        eng.sem_inc(S("y_centred"), 1)
        for j in range(4):
            jj = J["yvar"] + j
            bank_full(eng, jj)
            free(eng.tensor_scalar(VAR[:, 2 * j:2 * j + 2, :].rearrange("p a b -> p (a b)"), bank(jj), 64e-5, None,
                                   ALU.add), jj)
        jobs_out(eng, "yvar")
        eng.sem_inc(S("y_var"), 1)
        eng.wait_ge(S("y_std"), 1)
        ch.link(eng.reciprocal(VAR[:, :, :], VAR[:, :, :]))
        tt(YT, YT, VAR, ALU.mult)
        for f in range(8):
            ch.add(eng.tensor_scalar(YT[:, f, :], YT[:, f, :], cols("lnx_w_2", f), cols("lnx_b_2", f), ALU.mult,
                                     ALU.add))
        ch.wait()
        tt(YT, YT, VTR, ALU.add)
        tt(XS[:, 0:8], YT, GT, ALU.mult)
        ch.done("y_delta")
        split_lo(XS[:, :, :], ACTS["mix"])
        stream(st["mix"])

        def add_residual(buf, s):
            eng.wait_ge(block_out, 4 + 2 * (s.b0 + s.nblk))
            ch.link(eng.tensor_tensor(flat(XN[:, :, :, :]), flat(XN[:, :, :, :]), flat(buf[:, :, :, :]), ALU.add))

        add_residual(Y, st["mix"])
        eng.wait_ge(S("mem_in"), 32)
        normed(MEMN, MEMN)
        split_lo(XS[:, :, :], ACTS["cross_kv"])
        stream(st["cross_kv"])
        normed(XN, Y)
        split_lo(XS[:, :, :], ACTS["cross_q"])
        stream(st["cross_q"])
        softmax_rows("cross", 4, CSP, 128.0 ** -0.5, None)
        split_lo(XS[:, 0:4, :], ACTS["cross_o"], XTH[:, 0:4, :], XTL[:, 0:4, :])
        stream(st["cross_o"])
        add_residual(Y, st["cross_o"])
        ch.done("h_summed")
        normed(XN, Y)
        split_lo(XS[:, :, :], ACTS["up"])
        stream(st["up0"])
        split_lo(XS[:, :, :], ACTS["h0"], XTH2[:, :, :], XTL2[:, :, :])
        stream(st["up1"])
        for q in range(FF):
            stream(st[f"down{q}"])
            add_residual(Y3, st[f"down{q}"])
            ch.done("h_summed")
            if q + 1 < FF:
                split_lo(XS[:, :, :], ACTS[f"h{q + 1}"], XTH2[:, :, :], XTL2[:, :, :])
            if q + 2 < FF:
                stream(st[f"up{q + 2}"])
        normed(XN, XN)
        eng.wait_ge(S("final_gain_in"), 16)
        for h in range(2):
            ch.add(eng.tensor_tensor(XN[:, :, h, :], XN[:, :, h, :], NFB[:, :, :], ALU.mult))
        ch.done("out_ready")

    @block.tensor
    def _(eng):
        def chunk(s, B, par, kc, c, g, kt, nk):
            eng.wait_ge(lo_ready, g + 1)
            for k in range(4):
                t = kt + k
                if s.rows_only:
                    for m, w in enumerate((WHI, WLO)):
                        ins = eng.matmul(BANKS[:, par * 2, 0:s.n], CM[:, 4 * t:4 * t + P], w[:, c % 2, k, 0:s.n],
                                         start=(kc == 0 and k == 0 and m == 0),
                                         stop=(kc == nk - 1 and k == 3 and m == 1))
                    continue
                for h in range(2):
                    xh, xl = s.x or (XTH, XTL)
                    for m, (x, w) in enumerate(((xh, WHI), (xh, WLO), (xl, WHI))):
                        ins = eng.matmul(BANKS[:, par * 2 + h, 0:s.n], x[:, t, h * P:(h + 1) * P],
                                         w[:, c % 2, k, 0:s.n], start=(kc == 0 and k == 0 and m == 0),
                                         stop=(kc == nk - 1 and k == 3 and m == 2))
            ins.then_inc(chunk_used, 1)

        def stream(s):
            if s.loop:
                with eng.Fori(0, s.nblk // 2) as i:
                    for b in range(2):
                        eng.wait_ge(block_out, 2 * s.b0 + 4 * i + 2 * b + 2)
                        for kc in range(4):
                            chunk(s, None, b, kc, kc, s.g0 + 8 * i + 4 * b + kc, 4 * kc, 4)
            else:
                for b in range(s.nblk):
                    eng.wait_ge(block_out, 2 * (s.b0 + b) + 2)
                    for kc in range(s.kc):
                        g = s.g0 + b * s.kc + kc
                        chunk(s, None, b % 2, kc, g, g, s.kt0(b) + 4 * kc, s.kc)

        def gate_logs(pre):
            eng.wait_ge(block_out, 4 + 2 * (st[pre + "_r"].b0 + 2))
            jj = J[pre + "_rT"]
            bank_free(eng, jj)
            for h in range(2):
                ins = eng.transpose(bank(jj)[0:64, h * P:(h + 1) * P], RN2[:, h, :], ident)
            full(ins, jj)
            jobs_out(eng, pre + "_rT")
            eng.wait_ge(S("gate_w_in"), 64)
            for j in range(8):
                d, h, cb = j // 4, j // 2 % 2, j % 2
                jj = J[pre + "_z"] + j
                bank_free(eng, jj)
                full(eng.matmul(bank(jj), RT[32 * d:32 * d + 17, h * P:(h + 1) * P],
                                WG[32 * d:32 * d + 17, cb * NB:(cb + 1) * NB], start=True, stop=True), jj)

        def transposes(name, src):
            for j in range(NJ[name]):
                jj = J[name] + j
                bank_free(eng, jj)
                for f in (2 * j, 2 * j + 1):
                    for h in range(2):
                        ins = eng.transpose(bank(jj)[:, (f % 2) * T + h * P:(f % 2) * T + (h + 1) * P], src(f, h), ident)
                full(ins, jj)

        eng.sem_inc(chunk_used, 2)
        eng.wait_ge(S("cond_lo"), 1)
        stream(st["ada0"])
        eng.wait_ge(block_out, 4 + 16)
        eng.wait_ge(S("ada0_bias_in"), 16)
        eng.wait_ge(S("consts_in"), 32)
        jj = J["mod0"]
        for f in range(32):
            ins = eng.matmul(bank(jj)[:, 2 * f:2 * f + 2], ADAROW[:, f * P:(f + 1) * P], const("comb", 5),
                             start=True, stop=True)
        full(ins, jj)
        eng.wait_ge(S("acts_lo"), 1)
        stream(st["ctx_kv"])
        stream(st["ctx_r"])
        eng.wait_ge(S("rank_zeroed"), 3)
        gate_logs("ctx")
        eng.wait_ge(S("ctx_la"), 1)
        for d in range(2):
            for j in range(4):
                th, cb = j // 2, j % 2
                jj = J[f"ctx_D{d}"] + j
                terms = [(th, "gt" if d == 0 else "lt")]
                if th == d:
                    terms.append((1 - d, "ones16"))
                bank_free(eng, jj)
                for n, (sh, m) in enumerate(terms):
                    ins = eng.matmul(bank(jj), const(m), LA_C[:, d, cb, sh, :], start=(n == 0),
                                     stop=(n == len(terms) - 1))
                full(ins, jj)
            eng.wait_ge(S("ctx_kd"), d + 1)
            for j in range(4):
                jj = J[f"ctx_S{d}"] + j
                bank_free(eng, jj)
                for k2 in range(2):
                    for h in range(2):
                        c0 = j * DK + k2 * P
                        v0 = j * DK
                        ins = eng.matmul(bank(jj)[:, k2 * DK:(k2 + 1) * DK],
                                         TMP_C[:, c0 // NB, h, c0 % NB:c0 % NB + P],
                                         NAT[:, 2 + v0 // NB, h, v0 % NB:v0 % NB + DK], start=(h == 0), stop=(h == 1))
                full(ins, jj)
        eng.wait_ge(S("acts_lo"), 2)
        stream(st["lat_kv"])
        stream(st["lat_r"])
        stream(st["lat_rest"])
        gate_logs("lat")
        eng.wait_ge(S("lat_la"), 1)
        for d in range(2):
            for j in range(4):
                jj = J[f"G{d}"] + j
                bank_free(eng, jj)
                for f in (2 * j, 2 * j + 1):
                    o0 = (f % 2) * T
                    la = [LA_L[:, d, f // 4, h, (f % 4) * P:(f % 4 + 1) * P] for h in range(2)]
                    o, _ = c_at["le" if d == 0 else "ones16"]
                    eng.matmul(bank(jj)[:, o0:o0 + T], la[d], CONST[:, o:o + T], start=True, stop=False,
                               skip_group_check=True)
                    ins = eng.matmul(bank(jj)[:, o0 + (1 - d) * P:o0 + (2 - d) * P], la[1 - d],
                                     const("le" if d == 0 else "ge"), start=False, stop=True, skip_group_check=True)
                full(ins, jj)
        transposes("qT", lambda f, h: NAT[:, 4 + f // 4, h, (f % 4) * P:(f % 4 + 1) * P])
        transposes("kT", lambda f, h: NAT[:, 0 + f // 4, h, (f % 4) * P:(f % 4 + 1) * P])
        jobs_out(eng, "kT")

        def scores(name, A, B):
            for j in range(2):
                jj = J[name] + j
                bank_free(eng, jj)
                for hd in (2 * j, 2 * j + 1):
                    for h in range(2):
                        for k2 in range(2):
                            o0 = (hd % 2) * T + h * P
                            ins = eng.matmul(bank(jj)[:, o0:o0 + P], A[:, 2 * hd + k2, h * P:(h + 1) * P],
                                             B[:, 2 * hd + k2, h * P:(h + 1) * P], start=(k2 == 0), stop=(k2 == 1))
                full(ins, jj)

        scores("diag", KTT, QT)
        n = 0
        for d in range(2):
            for l in range(8):
                Wn = (W0, W1)[n % 2]
                n += 1
                eng.wait_ge(S("factors"), n)
                if l < 7:
                    scores(f"level{d}_{l}", Wn, Wn)
                    continue
                jj = J[f"level{d}_7"]
                bank_free(eng, jj)
                for hd in range(HEADS):
                    for k2 in range(2):
                        ins = eng.matmul(bank(jj)[:, hd * P:(hd + 1) * P], Wn[:, 2 * hd + k2, d * P:(d + 1) * P],
                                         Wn[:, 2 * hd + k2, (1 - d) * P:(2 - d) * P], start=(k2 == 0), stop=(k2 == 1))
                full(ins, jj)
        eng.wait_ge(S("state_factors"), 1)
        s = st["gla_o"]
        for B in range(2):
            eng.wait_ge(block_out, 2 * (s.b0 + B) + 2)
            for hd in range(HEADS):
                dst = acc(B, hd // 2)[:, (hd % 2) * DK:(hd % 2 + 1) * DK]
                terms = [(ACCD[:, hd, B, :], B), (ACCX[:, hd, 1 - B, :], 1 - B)]
                v0 = hd * DK
                for n, (sc, jh) in enumerate(terms):
                    eng.matmul(dst, sc, NAT[:, 2 + v0 // NB, jh, v0 % NB:v0 % NB + DK], start=(n == 0), stop=False)
                for d in range(2):
                    for k2 in range(2):
                        ins = eng.matmul(dst, (W0, W1)[d][:, 2 * hd + k2, B * P:(B + 1) * P], S0[:, d, hd, k2, :],
                                         start=False, stop=(d == 1 and k2 == 1))
            ins.then_inc(S("gla_o_full"), 1)
        eng.wait_ge(S("y_b"), 1)
        transposes("yT", lambda f, h: O[:, h, f // 2, (f % 2) * P:(f % 2 + 1) * P])
        transposes("p1T", lambda f, h: NAT[:, 10 + f // 4, h, (f % 4) * P:(f % 4 + 1) * P])
        transposes("p2T", lambda f, h: NAT[:, 8 + f // 4, h, (f % 4) * P:(f % 4 + 1) * P])
        stream(st["ada0_gate"])

        def gate_bcast(name, s, row, c0, sem):
            eng.wait_ge(block_out, 4 + 2 * (s.b0 + s.nblk))
            eng.wait_ge(S(sem), 16)
            for j in range(4):
                jj = J[name] + j
                bank_free(eng, jj)
                full(eng.matmul(bank(jj), const("comb_wide", 5), row[:, c0 + j * NB:c0 + (j + 1) * NB], start=True,
                                stop=True), jj)

        eng.wait_ge(S("conv_done"), 1)
        gate_bcast("gt0", st["ada0_gate"], ADAROW2, 0, "ada0_gate_bias_in")
        eng.wait_ge(S("acts_lo"), 3)
        stream(st["out_e"])
        if stop == "x1":
            return

        stream(st["ada1"])
        eng.wait_ge(block_out, 4 + 2 * (st["ada1"].b0 + 12))
        eng.wait_ge(S("ada1_bias_in"), 16)
        jj = J["mod1"]
        bank_free(eng, jj)
        for f in range(32):
            ins = eng.matmul(bank(jj)[:, 2 * f:2 * f + 2], ADAROW1[:, f * P:(f + 1) * P], const("comb", 5),
                             start=True, stop=True)
        full(ins, jj)
        gate_bcast("gt1", st["ada1"], ADAROW1, 4096, "ada1_bias_in")
        eng.wait_ge(S("x1_done"), 1)

        def natural(buf):
            return lambda f, h: buf[:, f // 4, h, (f % 4) * P:(f % 4 + 1) * P]

        transposes("x1T", natural(XN))
        eng.wait_ge(S("acts_lo"), ACTS["in_o"])
        stream(st["in_o"])
        eng.wait_ge(block_out, 4 + 2 * st["pool"].b0)
        eng.wait_ge(S("pool_consts_in"), 16)
        for j in range(8):
            jj = J["zT"] + j
            bank_free(eng, jj)
            for f in (2 * j, 2 * j + 1):
                w = (2, 4, 8, 8)[f // 4]
                for h in range(2):
                    ins = eng.matmul(bank(jj)[:, (f % 2) * T:(f % 2 + 1) * T],
                                     NATO[:, f // 4, h, (f % 4) * P:(f % 4 + 1) * P], const(f"pool{w}_{h}"),
                                     start=(h == 0), stop=(h == 1))
            full(ins, jj)
        eng.wait_ge(S("acts_lo"), ACTS["pool"])
        stream(st["pool"])
        eng.wait_ge(S("gated_z"), 1)
        transposes("pT", natural(Y))
        eng.wait_ge(S("acts_lo"), ACTS["out_o"])
        stream(st["out_o"])
        if stop == "x2":
            return

        def attention(pre, units, q_T, k_T, kv, V, SPb, PTb):
            def values(u):
                pair, half = u // 2, u % 2
                eng.wait_ge(S(pre + "_probs"), u + 1)
                jj = J[f"{pre}_p{u}"]
                bank_free(eng, jj)
                for e in range(2):
                    for sh in range(2):
                        ins = eng.transpose(bank(jj)[:, (2 * e + sh) * P:(2 * e + sh + 1) * P],
                                            SPb[:, u % 2, e, sh * P:(sh + 1) * P], ident)
                full(ins, jj)
                copied(eng, jj)
                jj = J[f"{pre}_o{u}"]
                bank_free(eng, jj)
                for e in range(2):
                    for sh in range(2):
                        ins = eng.matmul(bank(jj)[:, e * P:(e + 1) * P], V(kv(2 * pair + e), sh),
                                         PTb[:, u % 2, (2 * e + sh) * P:(2 * e + sh + 1) * P], start=(sh == 0),
                                         stop=(sh == 1))
                full(ins, jj)

            for u in range(units):
                pair, half = u // 2, u % 2
                jj = J[f"{pre}_s{u}"]
                bank_free(eng, jj)
                for e in range(2):
                    ins = eng.matmul(bank(jj)[:, e * T:(e + 1) * T], q_T[:, 2 * pair + e, half * P:(half + 1) * P],
                                     k_T[:, kv(2 * pair + e), :], start=True, stop=True)
                full(ins, jj)
                if u >= 1:
                    values(u - 1)
            values(units - 1)

        eng.wait_ge(S("normed"), 1)
        transposes("x2T", natural(Y))
        eng.wait_ge(S("acts_lo"), ACTS["rkv"])
        for n in ("rkv", "lora", "att4", "att1", "kiwi"):
            stream(st[n])
        eng.wait_ge(S("roped"), 1)
        transposes("aqT", natural(NA))
        transposes("akT", lambda f, h: NA[:, 2, h, f * P:(f + 1) * P])
        transposes("aiT", lambda f, h: NA[:, 3 + f // 4, h, (f % 4) * P:(f % 4 + 1) * P])
        jj = J["aiiT"]
        bank_free(eng, jj)
        for h in range(2):
            ins = eng.transpose(bank(jj)[:, h * P:(h + 1) * P], KI2[:, h, :], ident)
        full(ins, jj)
        jobs_out(eng, "aiiT")
        for j in range(16):
            half = j // 8
            jj = J["idx"] + j
            bank_free(eng, jj)
            for e in range(2):
                hd = index_head(j, e)
                r = slice(64 * (hd % 2), 64 * (hd % 2) + 64)
                ins = eng.matmul(bank(jj)[:, e * T:(e + 1) * T], QIT[r, hd // 2, half * P:(half + 1) * P], KIT[r, :],
                                 start=True, stop=True)
            full(ins, jj)
        attention("dsa", 8, QTA, KTA, lambda hd: hd // 4,
                  lambda g, sh: NA[:, 2, sh, 256 + g * P:256 + (g + 1) * P], SP, PT)
        transposes("rT", lambda f, h: NR[:, f // 4, h, (f % 4) * P:(f % 4 + 1) * P])
        transposes("keyT", lambda f, h: NR[:, 2 + f // 4, h, (f % 4) * P:(f % 4 + 1) * P])
        transposes("valT", lambda f, h: NR[:, 4 + f // 4, h, (f % 4) * P:(f % 4 + 1) * P])
        for j, (c0, w) in enumerate(((0, P), (P, P), (2 * P, 32))):
            jj = J["loraT"] + j
            bank_free(eng, jj)
            for h in range(2):
                ins = eng.transpose(bank(jj)[0:w, h * P:(h + 1) * P], LORA[:, h, c0:c0 + w], ident)
            full(ins, jj)
        eng.wait_ge(S("lora_acts"), 1)
        eng.wait_ge(S("ups_in"), 64)

        def feature_jobs(name, terms):
            for j in range(4):
                jj = J[name] + j
                bank_free(eng, jj)
                for f in (2 * j, 2 * j + 1):
                    for n, (lhs, rhs) in enumerate(terms):
                        ins = eng.matmul(bank(jj)[:, (f % 2) * T:(f % 2 + 1) * T], lhs(f), rhs(f), start=(n == 0),
                                         stop=(n == len(terms) - 1))
                full(ins, jj)

        feature_jobs("decay", [(lambda f: WDU[0:64, f * P:(f + 1) * P], lambda f: LT[0:64, 0, :])])
        feature_jobs("rate", [(lambda f: WDU[64:128, f * P:(f + 1) * P], lambda f: LT[64:128, 0, :])])
        feature_jobs("dgate", [(lambda f: GU[:, 0, f * P:(f + 1) * P], lambda f: LT[:, 1, :]),
                               (lambda f: GU[0:32, 1, f * P:(f + 1) * P], lambda f: LT[0:32, 2, :])])

        def token_jobs(name, src):
            for j in range(4):
                jj = J[name] + j
                bank_free(eng, jj)
                h = j // 2
                for q in range(4):
                    ins = eng.transpose(bank(jj)[:, q * P:(q + 1) * P], src[:, (j % 2) * 4 + q, h * P:(h + 1) * P],
                                        ident)
                full(ins, jj)

        eng.wait_ge(S("mixed"), 1)
        token_jobs("valN", VTR)
        eng.wait_ge(S("kk_squares"), 1)
        feature_jobs("kknorm", [(lambda f: const("head_ones"), lambda f: TMPR[:, f, :])])
        eng.wait_ge(S("bonus_in"), 1)
        feature_jobs("bonus", [(lambda f: const("head_ones"), lambda f: TMPR[:, f, :])])
        eng.wait_ge(S("scaled"), 1)
        token_jobs("bN", AT)
        token_jobs("keyN", KTR)

        def unit(half, hd):
            return half * 16 + (hd % 2) * 8 + hd // 2

        def chunk_matrices(name, A, B):
            for j in range(8):
                jj = J[name] + j
                bank_free(eng, jj)
                half, par = j // 4, j // 2 % 2
                for q in range(4):
                    f = (j % 2) * 4 + q
                    r = slice(RN * par, RN * (par + 1))
                    ins = eng.matmul(bank(jj)[:, q * P:(q + 1) * P], A[r, f, half * P:(half + 1) * P],
                                     B[r, f, half * P:(half + 1) * P], start=True, stop=True)
                full(ins, jj)

        chunk_matrices("Aab", KK, AT)
        chunk_matrices("Aak", KTR, KK)
        chunk_matrices("Arb", AT, RTT)
        chunk_matrices("Ark", KTR, RTT)
        jobs_out(eng, "Ark")
        s = st["delta_y"]
        eng.wait_ge(block_out, 2 * (s.b0 + 1) + 2)
        for c in range(8):
            half, r = c // 4, slice(C * (c % 4), C * (c % 4) + C)
            tok = slice(C * c, C * (c + 1))
            eng.wait_ge(S("state_ready"), c + 1)
            for b in range(2):
                jj = J[f"chunkR{c}"] + b
                bank_free(eng, jj)
                for q in range(4):
                    f = 4 * b + q
                    eng.matmul(bank(jj)[r, q * P:(q + 1) * P], KK[:, f, tok], ST[:, f, :], start=True, stop=True,
                               skip_group_check=True)
                    for p in range(2):
                        hd = 2 * f + p
                        ins = eng.matmul(bank(jj)[r, q * P + RN * p:q * P + RN * (p + 1)], AAK[r, unit(half, hd), :],
                                         VN[r, half, hd * RN:(hd + 1) * RN], start=False, stop=True,
                                         skip_group_check=True)
                full(ins, jj)
            if c == 0:
                eng.wait_ge(S("inverse_in"), 64)
            for b in range(2):
                copied(eng, J[f"chunkR{c}"] + b)
            for b in range(2):
                jj = J[f"chunkU{c}"] + b
                bank_free(eng, jj)
                for q in range(8):
                    hd = 8 * b + q
                    ins = eng.matmul(bank(jj)[r, q * RN:(q + 1) * RN], TT[r, unit(half, hd), :],
                                     RS[r, half, hd * RN:(hd + 1) * RN], start=True, stop=True)
                full(ins, jj)
            for f in range(8):
                eng.matmul(BANKS[:, f // 2, (f % 2) * T + C * c:(f % 2) * T + C * (c + 1)], ST[:, f, :],
                           RTT[:, f, tok], start=(c == 0 and f % 2 == 0), stop=False, skip_group_check=True)
            for b in range(2):
                copied(eng, J[f"chunkU{c}"] + b)
            if c < 7:
                for b in range(2):
                    jj = J[f"chunkS{c}"] + b
                    bank_free(eng, jj)
                    for q in range(4):
                        for p in range(2):
                            hd = 2 * (4 * b + q) + p
                            dst = bank(jj)[RN * p:RN * (p + 1), q * P + RN * p:q * P + RN * (p + 1)]
                            v = slice(hd * RN, (hd + 1) * RN)
                            eng.matmul(dst, BN[r, half, v], U[r, half, v], start=True, stop=False)
                            ins = eng.matmul(dst, KN[r, half, v], VN[r, half, v], start=False, stop=True)
                    full(ins, jj)
            for hd in range(RH):
                f, p = hd // 2, hd % 2
                dst = BANKS[RN * p:RN * (p + 1), f // 2, (f % 2) * T + C * c:(f % 2) * T + C * (c + 1)]
                v = slice(hd * RN, (hd + 1) * RN)
                eng.matmul(dst, U[r, half, v], ARB[r, unit(half, hd), :], start=False, stop=False,
                           skip_group_check=True)
                ins = eng.matmul(dst, VN[r, half, v], ARK[r, unit(half, hd), :], start=False, stop=(c == 7),
                                 skip_group_check=True)
            if c == 7:
                ins.then_inc(S("delta_y_full"), 1)
        eng.wait_ge(block_out, 4 + 2 * (s.b0 + 2))
        feature_jobs("ymean", [(lambda f: const("head_mean"), lambda f: YT[:, f, :])])
        eng.wait_ge(S("y_squares"), 1)
        feature_jobs("yvar", [(lambda f: const("head_mean"), lambda f: SQ[:, f, :])])
        eng.wait_ge(S("acts_lo"), ACTS["mix"])
        stream(st["mix"])
        eng.wait_ge(S("normed"), 2)
        transposes("memT", natural(MEMN))
        eng.wait_ge(S("acts_lo"), ACTS["cross_kv"])
        stream(st["cross_kv"])
        eng.wait_ge(S("normed"), 3)
        transposes("x3T", natural(Y))
        eng.wait_ge(S("acts_lo"), ACTS["cross_q"])
        stream(st["cross_q"])
        eng.wait_ge(block_out, 4 + 2 * st["cross_o"].b0)
        transposes("ckT", natural(CKV))
        transposes("cqT", natural(CQ))
        jobs_out(eng, "cqT")
        attention("cross", 4, CQT, CKT, lambda hd: hd, lambda g, sh: CKV[:, 1, sh, g * P:(g + 1) * P], CSP, CPT)
        eng.wait_ge(S("acts_lo"), ACTS["cross_o"])
        stream(st["cross_o"])
        eng.wait_ge(S("normed"), 4)
        transposes("x4T", natural(Y))
        eng.wait_ge(S("acts_lo"), ACTS["up"])

        def hidden(q):
            s = st[f"up{q}"]
            eng.wait_ge(block_out, 4 + 2 * (s.b0 + 4))
            transposes(f"h{q}T", natural(UPN))

        stream(st["up0"])
        hidden(0)
        stream(st["up1"])
        hidden(1)
        for q in range(FF):
            eng.wait_ge(S("acts_lo"), ACTS[f"h{q}"])
            stream(st[f"down{q}"])
            if q + 2 < FF:
                stream(st[f"up{q + 2}"])
                hidden(q + 2)

    ctx.close()


def columns(v):
    return np.ascontiguousarray(v.reshape(-1, P).T)


def transposed(x):
    return np.ascontiguousarray(x.T.reshape(-1, P, x.shape[0]).transpose(1, 0, 2))


def kernel(**inputs):
    import concourse.bacc as bacc
    from concourse.bass_utils import run_bass_kernel_spmd as run

    v = {k: np.ascontiguousarray(x) for k, x in inputs.items()}
    mu = v["rwkv_mu_2"][0]
    col = {
        "c": v["c"][0], "c_ctx": v["c_ctx"], "conv_w0": v["conv_w"][0, 0], "conv_w1": v["conv_w"][0, 1],
        "conv_w2": v["conv_w"][0, 2], "pool_scale": v["pool_scale"][0], "norm_mix_2": v["norm_mix_2"][0],
        "norm_cross_2": v["norm_cross_2"][0], "norm_mem_2": v["norm_mem_2"][0], "norm_mlp_2": v["norm_mlp_2"][0],
        "mu_lora": np.concatenate([mu[3072:3360], np.zeros(96, np.float32)]),
        "mu_r": mu[0:1024], "mu_k": mu[1024:2048], "mu_v": mu[2048:3072],
    }
    for n in ("w_decay0_2", "a0_2", "k_k_2", "k_a_2", "r_k_2", "lnx_w_2", "lnx_b_2"):
        col[n] = v[n][0].reshape(-1)
    arrays = {"cols": np.concatenate([columns(col[n]) for n in COL_NAMES], 1),
              "common_consts": common_constants()[1], "gla_consts": gla_constants()[1],
              "pool_consts": pool_constants()[1], "second_consts": second_constants()[1],
              "mem": v["mem_2"], "positions": np.ascontiguousarray(v["positions_2"].reshape(2, P).T),
              "ctxT": transposed(v["ctx"][0]), "xT": transposed(v["x"][0])}
    for n in ("x", "w_ada", "b_ada", "ln_g", "ln_b", "w_in_e", "w_gate_f", "b_gate_f", "w_gate_b", "b_gate_b",
              "gla_norm_w", "w_out_e", "w_in_o", "w_pool", "w_out_o", "norm_final_2"):
        arrays[n] = v[n]
    for n in ("w_in", "w_mix_out", "w_q_cross", "w_kv_cross", "w_o_cross", "w_up", "w_down"):
        arrays[n if n != "w_in" else "w_in_2"] = v[n + "_2"]
    for n in ("w_decay_up_2", "a_up_2", "g_up_2"):
        arrays[n] = v[n]
    nc = bacc.Bacc("TRN2", target_bir_lowering=False, num_devices=1)
    args = {n: nc.dram_tensor("in_" + n, x.shape, mybir.dt.from_np(x.dtype), kind="ExternalInput").ap()
            for n, x in arrays.items()}
    for n in ("scratch_a", "scratch_t"):
        args[n] = nc.dram_tensor(n, (P, C, C), F32, kind="Internal").ap()
    out = nc.dram_tensor("out", (1, T, D), F32, kind="ExternalOutput").ap()
    build(nc, args, out, STOP)
    r = run(nc, [{"in_" + n: x for n, x in arrays.items()}], core_ids=[0])
    return r.results[0]["out"]
```

```python
from contextlib import ExitStack

import numpy as np

import concourse.bass as bass
from concourse import mybir

F32 = mybir.dt.float32
F32R = mybir.dt.float32r
I32 = mybir.dt.int32
ALU = mybir.AluOpType
ACT = mybir.ActivationFunctionType
AX = mybir.AxisListType

STOP = None
P = 128
T = 256
D = 2048
NB = 512
KT = D // P
HEADS, DK = 4, 256
ROW = 64
EPS = 1e-5
ALPHA = 4.0 ** 0.25


def packed(parts, first=0):
    at, n = {}, first
    for name, m in parts:
        at[name] = (n, m.shape[1])
        n += m.shape[1]
    return at, np.concatenate([m for _, m in parts], 1).astype(np.float32)


J_ = np.arange(P)[:, None]
I_ = np.arange(P)[None, :]


def common_constants():
    comb = np.zeros((P, 2))
    comb[[0, 1, 4], 0] = 1
    comb[[2, 3, 4], 1] = 1
    comb3 = np.stack([(J_[:, 0] % 32 == 0) | (J_[:, 0] % 32 == 2), (J_[:, 0] % 32 == 1) | (J_[:, 0] % 32 == 2)], 1)
    wide3 = np.broadcast_to((J_ % 32 == 0) | (J_ % 32 == 2), (P, P))
    return packed([("ident", (J_ == I_) * 1.0), ("comb", comb), ("comb3", comb3 * 1.0), ("comb_wide3", wide3 * 1.0)])


COMMON = P + 4 + P


def gla_constants():
    tau = 1.0 / 16.0
    parts = [("le", (J_ <= I_) * tau), ("ones16", np.full((P, P), tau)), ("ge", (J_ >= I_) * tau),
             ("gt", (J_ > I_) * tau), ("lt", (J_ < I_) * tau)]
    for d in range(2):
        for l in range(7):
            b = 1 << l
            m = (J_ // (2 * b) == I_ // (2 * b)) & (J_ // b % 2 == d) & (I_ // b % 2 == 1 - d)
            parts.append((f"mask{d}_{l}", m * 1.0))
    return packed(parts, COMMON)


def pool_constants():
    t = np.arange(T)
    parts = []
    rows = T // ROW
    for w in (2, 4, 8):
        m = np.zeros((T, T))
        for r in range(rows):
            lo, hi = max(r - w // 2, 0), min(r + w - w // 2, rows)
            for q in range(lo, hi):
                m[(q * ROW + np.arange(ROW)), (r * ROW + np.arange(ROW))] = np.float32(1.0 / (hi - lo))
        m[t, t] -= 1.0
        for h in range(2):
            parts.append((f"pool{w}_{h}", m[h * P:(h + 1) * P]))
    return packed(parts, COMMON)


C = 32
RH, RN = 16, 64


def second_constants():
    c = np.arange(C)[None, :]
    p = np.arange(P)[:, None]
    key = np.arange(T)[None, :]
    inv = 500000.0 ** (-np.arange(16, dtype=np.float32) / np.float32(16))
    parts = [("head_ones", (J_ // RN == I_ // RN) * 1.0), ("head_mean", (J_ // RN == I_ // RN) / RN),
             ("below", (c < p % C) * 1.0), ("above", (p % C < c) * 1.0), ("above_eq", (p % C <= c) * 1.0),
             ("restart", np.broadcast_to(np.arange(T) % C != 0, (P, T)) * 1.0),
             ("inv_freq", np.broadcast_to(inv, (P, 16)))]
    for h in range(2):
        parts.append((f"causal_{h}", np.where(key <= p + h * P, 0.0, -1e30)))
    parts.append(("eye32", np.broadcast_to(np.eye(C).reshape(1, -1), (P, C * C))))
    return packed(parts, COMMON)


COL_NAMES = ["c", "c_ctx", "conv_w0", "conv_w1", "conv_w2", "pool_scale", "norm_mix_2", "norm_cross_2",
             "norm_mem_2", "norm_mlp_2", "mu_r", "mu_k", "mu_v", "mu_lora", "w_decay0_2", "a0_2", "k_k_2", "k_a_2", "r_k_2",
             "lnx_w_2", "lnx_b_2", "ln_g0", "ln_b0", "ln_g1", "ln_b1"]
COL_TILES = [16, 16, 8, 8, 8, 16, 16, 16, 16, 16, 8, 8, 8, 3] + [8] * 7 + [16] * 4
COL_AT = {n: sum(COL_TILES[:k]) for k, n in enumerate(COL_NAMES)}
NCOLS = sum(COL_TILES)


class Stage:

    def __init__(self, name, view, nblk, n=NB, kc=4, loop=True, rows_only=False, dest=None, kt0=None, func=None,
                 x=None, acts=None, plain=False, scale=None):
        self.name, self.view, self.nblk, self.n, self.kc = name, view, nblk, n, kc
        self.loop, self.rows_only, self.dest = loop, rows_only, dest
        self.kt0 = kt0 or (lambda blk: 0)
        self.func = func
        self.x, self.acts, self.plain, self.scale = x, acts, plain, scale


def build(nc, a, out, stop=None):
    ctx = ExitStack()
    BASE = 16512

    def place(name, kb, shape, dt=F32):
        assert kb * 1024 + int(np.prod(shape[1:])) * 4 <= 207.8 * 1024, name
        return nc.alloc_sbuf_tensor_at(name, shape, dt, offset=BASE + int(kb * 1024))

    sems = {}

    def S(name):
        if name not in sems:
            sems[name] = ctx.enter_context(nc.semaphore(name))
        return sems[name]

    RAW = place("weights_raw", 0, [P, 4, 4, NB])
    WHI = place("weights_hi", 32, [P, 2, 4, NB], F32R)
    WLO = place("weights_lo", 48, [P, 2, 4, NB], F32R)
    CM = place("cond_parts", 64, [P, 192], F32R)
    TILE = place("shifted_tile", 205.5, [P, 2, T])
    RSTD = place("inverse_rms", 68.625, [P, 8])
    NORMC = place("norm_cols", 65.25, [P, 2, KT])
    STAT = place("stats", 64.75, [P, 128])
    RN2 = place("gate_rank_rows", 65.25, [P, 2, 64])
    RT = place("gate_rank_T", 65.75, [64, T])
    MODT = place("modulation_cols", 66.75, [P, 48, 2])
    COLS = place("feature_cols", 67.25, [P, NCOLS])
    CONST = place("constants", 68.75, [P, 2752])
    XTH = place("acts_hi", 79.5, [P, KT, T], F32R)
    XTL = place("acts_lo", 95.5, [P, KT, T], F32R)
    NAT = place("natural_blocks", 111.5, [P, 16, 2, NB])
    XS = place("acts_T", 111.5, [P, KT, T])
    XS2 = place("acts_T_latent", 143.5, [P, KT, T])
    S0 = place("context_states", 175.5, [P, 2, HEADS, 2, DK])
    ADAROW = place("modulation_rows", 191.5, [5, 8 * NB])
    WG = place("gate_weights", 191.5, [64, 1024])
    W0 = place("decayed_a", 191.5, [P, 8, T])
    ACCD = place("scores_diag", 199.5, [P, HEADS, 2, P])
    ACCX = place("scores_cross", 203.5, [P, HEADS, 2, P])
    LA_C = place("log_decay_ctx", 127.5, [P, 2, 2, 2, NB])
    TMP_C = place("decay_ctx", 159.5, [P, 2, 2, NB])
    LA_L = place("log_decay", 79.5, [P, 2, 2, 2, NB])
    TMP_L = place("gate_tmp", 95.5, [P, 2, 2, NB])
    GB_ = place("cum_decay_b", 95.5, [P, 8, T])
    GF_ = place("cum_decay_f", 103.5, [P, 8, T])
    W1 = place("decayed_b", 79.5, [P, 8, T])
    MTMP = place("masked_scores", 87.5, [P, 4, P])
    QT = place("q_T", 159.5, [P, 8, T])
    KTT = place("k_T", 167.5, [P, 8, T])
    O = place("gla_out", 127.5, [P, 2, HEADS, DK])
    GNW = place("gla_norm_row", 91.5, [P, DK])
    P1T = place("conv_in_T", 159.5, [P, 8, T])
    P2T = place("conv_gate_T", 167.5, [P, 8, T])
    CV = place("conv_out_T", 199.5, [P, 8, T])
    XN = place("residual", 127.5, [P, 4, 2, NB])
    Y = place("projected", 143.5, [P, 4, 2, NB])
    GTB = place("gate_bcast", 159.5, [P, 4, NB])
    CF = place("cond", 68.5, [P, KT, 2])
    ADAR = place("modulation_rows_plain", 111.5, [P, 4, NB])
    LNG = place("ln_gain_bcast", 183.5, [P, 4, NB])
    LNB = place("ln_bias_bcast", 191.5, [P, 4, NB])

    GTB1 = place("gate_bcast_1", 167.5, [P, 4, NB])
    NATO = place("pool_natural", 175.5, [P, 8, 2, NB])
    NR = place("rkv_natural", 143.5, [P, 6, 2, NB])
    NA = place("att_natural", 167.5, [P, 5, 2, NB])
    LORA = place("lora_natural", 187.5, [P, 2, 288])
    KIWI = place("index_key_natural", 189.75, [P, 2, 80])
    QTA = place("att_q_T", 79.5, [P, 8, T])
    QIT = place("index_q_T", 87.5, [P, 8, T])
    KTA = place("att_k_T", 95.5, [P, 2, T])
    KIT = place("index_k_T", 97.5, [P, T])
    SC = place("index_scores", 98.5, [P, 2, T])
    BIAS = place("att_bias", 100.5, [P, 2, T])
    RL = place("index_relu", 102.5, [P, 2, 2, T])
    SP = place("probs", 106.5, [P, 2, 2, T])
    PT = place("probs_T", 199.5, [P, 2, NB])
    ROPE = place("rope_angles", 203.5, [P, 8, 2, 16])
    ROT = place("rope_products", 204.5, [P, 4, 128])
    KI2 = place("index_key_twice", 206.5, [P, 2, P])
    RTT = place("r_T", 79.5, [P, 8, T])
    KTR = place("key_T", 87.5, [P, 8, T])
    VTR = place("value_T", 95.5, [P, 8, T])
    KK = place("unit_key_T", 103.5, [P, 8, T])
    WDU = place("decay_rate_up", 111.5, [P, 1024])
    TMPR = place("delta_tmp", 111.5, [P, 8, T])
    SIG = place("decay_T", 143.5, [P, 8, T])
    AT = place("rate_T", 151.5, [P, 8, T])
    GT = place("gate_T", 159.5, [P, 8, T])
    VN = place("value_nat", 175.5, [P, 2, 1024])
    LT = place("lora_T", 183.5, [P, 3, T])
    GU = place("gate_up", 191.5, [P, 2, 1024])
    NRM = place("norms_T", 191.5, [P, 8, T])
    LG = place("cum_decay_T", 199.5, [P, 8, T])
    GE = place("chunk_decay", 66.75, [P, 8, 8])
    BN = place("b_nat", 167.5, [P, 2, 1024])
    KN = place("key_nat", 183.5, [P, 2, 1024])
    AAB = place("a_ab", 191.5, [P, 32, C])
    AAK = place("a_ak", 111.5, [P, 32, C])
    ARB = place("a_rb", 115.5, [P, 32, C])
    ARK = place("a_rk", 143.5, [P, 32, C])
    TT = place("inverse_T", 147.5, [P, 32, C])
    AC = place("a_by_chunk", 195.5, [P, C, C])
    TC = place("inverse_by_chunk", 199.5, [P, C, C])
    TMPC = place("inverse_products", 203.5, [P, C * C])
    RS = place("chunk_rhs", 87.5, [P, 2, 1024])
    U = place("chunk_u", 151.5, [P, 2, 1024])
    ST = place("delta_state", 191.5, [P, 8, P])
    YT = place("delta_out_T", 167.5, [P, 8, T])
    SQ = place("delta_sq_T", 183.5, [P, 8, T])
    VAR = place("delta_var_T", 191.5, [P, 8, T])
    MEMN = place("memory_natural", 159.5, [P, 4, 2, NB])
    CQ = place("cross_q", 175.5, [P, 1, 2, NB])
    CKV = place("cross_kv", 179.5, [P, 2, 2, NB])
    CQT = place("cross_q_T", 187.5, [P, 4, T])
    CKT = place("cross_k_T", 191.5, [P, 4, T])
    CSP = place("cross_probs", 195.5, [P, 2, 2, T])
    CPT = place("cross_probs_T", 199.5, [P, 2, NB])
    UPN = place("hidden", 143.5, [P, 4, 2, NB])
    Y3 = place("down_out", 159.5, [P, 4, 2, NB])
    XTH2 = place("hidden_hi", 175.5, [P, KT, T], F32R)
    XTL2 = place("hidden_lo", 191.5, [P, KT, T], F32R)
    NFB = place("final_gain_bcast", 159.5, [P, 4, NB])

    BANKS = ctx.enter_context(nc.psum_tensor("banks", [P, 8, NB], F32))
    c_at = {}
    for f in (common_constants, gla_constants, pool_constants, second_constants):
        c_at.update(f()[0])

    def const(name, rows=P):
        o, n = c_at[name]
        return CONST[0:rows, o:o + n]

    def cols(name, f):
        return COLS[:, COL_AT[name] + f:COL_AT[name] + f + 1]

    ident = const("ident")

    def wv(w, r0, rows, c0, n):
        v = w[r0:r0 + rows, :].rearrange("(c k p) n -> c p k n", p=P, k=4)
        return lambda kc, blk: v[kc][:, :, bass.ds(c0 + blk * NB, n)]

    ada0, ada1 = a["w_ada"][0], a["w_ada"][1]
    ine = a["w_in_e"][0]
    stages = [
        Stage("ada0", wv(ada0, 0, D, 0, NB), 8, rows_only=True, dest=lambda b: ADAROW[0:4, bass.ds(b * NB, NB)]),
        Stage("ctx_kv", wv(ine, 0, D, 0, NB), 4, dest=lambda b, h: NAT[:, bass.ds(b, 1), h, :]),
        Stage("ctx_r", wv(ine, 0, D, 2048, 32), 1, n=32, loop=False, dest="rank"),
        Stage("lat_kv", wv(ine, 0, D, 0, NB), 4, dest=lambda b, h: NAT[:, bass.ds(b, 1), h, :]),
        Stage("lat_r", wv(ine, 0, D, 2048, 32), 1, n=32, loop=False, dest="rank"),
        Stage("lat_rest", wv(ine, 0, D, 2080, NB), 12, dest=lambda b, h: NAT[:, bass.ds(b + 4, 1), h, :]),
        Stage("ada_plain", lambda kc, b: (wv(ada0, 0, D, 4096, NB)(kc, b) if b < 4 else wv(ada1, 0, D, 0, NB)(kc, b - 4)),
              16, loop=False, plain=True),
        Stage("gla_o", None, 2, loop=False),
        Stage("out_e", wv(a["w_out_e"][0], 0, D, 0, NB), 4, acts="y", dest=lambda b, h: Y[:, bass.ds(b, 1), h, :]),
        Stage("in_o", wv(a["w_in_o"][0], 0, D, 0, NB), 8, acts="x1T", dest=lambda b, h: NATO[:, bass.ds(b, 1), h, :]),
        Stage("pool", lambda kc, blk: a["w_pool"][0, blk].rearrange("(k p) n -> p k n", p=P), 4, kc=1, loop=False,
              acts="zT", kt0=lambda b: 4 * b, dest=lambda b, h: Y[:, b:b + 1, h, :]),
        Stage("out_o", wv(a["w_out_o"][0], 0, D, 0, NB), 4, acts="pT", dest=lambda b, h: Y[:, bass.ds(b, 1), h, :]),
        Stage("rkv", wv(a["w_in_2"][0], 0, D, 0, NB), 6, acts="x2T", scale=0, dest=lambda b, h: NR[:, bass.ds(b, 1), h, :]),
        Stage("lora", wv(a["w_in_2"][0], 0, D, 3072, 288), 1, n=288, loop=False, scale=0, dest=lambda b, h: LORA[:, h, :]),
        Stage("att4", wv(a["w_in_2"][0], 0, D, 3360, NB), 4, scale=0, dest=lambda b, h: NA[:, bass.ds(b, 1), h, :]),
        Stage("att1", wv(a["w_in_2"][0], 0, D, 5408, NB), 1, loop=False, scale=0, dest=lambda b, h: NA[:, 4, h, :]),
        Stage("kiwi", wv(a["w_in_2"][0], 0, D, 5920, 80), 1, n=80, loop=False, scale=0, dest=lambda b, h: KIWI[:, h, :]),
        Stage("delta_y", None, 2, loop=False),
        Stage("mix", wv(a["w_mix_out"][0], 0, D, 0, NB), 4, dest=lambda b, h: Y[:, bass.ds(b, 1), h, :]),
        Stage("cross_kv", wv(a["w_kv_cross"][0], 0, D, 0, NB), 2, acts="memT", scale=2, dest=lambda b, h: CKV[:, bass.ds(b, 1), h, :]),
        Stage("cross_q", wv(a["w_q_cross"][0], 0, D, 0, NB), 1, loop=False, acts="x3T", scale=4, dest=lambda b, h: CQ[:, 0, h, :]),
        Stage("cross_o", lambda kc, blk: a["w_o_cross"][0][:, blk * NB:(blk + 1) * NB].rearrange(
              "(k p) n -> p k n", p=P), 4, kc=1, loop=False, dest=lambda b, h: Y[:, b:b + 1, h, :]),
    ]

    def up(q):
        return Stage(f"up{q}", wv(a["w_up"][0], 0, D, q * D, NB), 4, func=ACT.Relu, acts="x4T", scale=6,
                     dest=lambda b, h: UPN[:, bass.ds(b, 1), h, :])

    def down(q):
        return Stage(f"down{q}", wv(a["w_down"][0], q * D, D, 0, NB), 4, x=(XTH2, XTL2), acts=f"h{q}T",
                     dest=lambda b, h: Y3[:, bass.ds(b, 1), h, :])

    FF = 4
    stages += [up(0), up(1), down(0), up(2), down(1), up(3), down(2), down(3)]
    if stop:
        stages = stages[:{"x1": 9, "x2": 12}[stop]]
    g = b = ring = 0
    st = {}
    for s in stages:
        s.g0, s.b0 = g, b
        s.ring0 = ring
        if s.view is not None:
            ring += s.nblk * s.kc
        if s.view is not None and not s.plain:
            g += s.nblk * s.kc
        b += s.nblk + s.nblk % 2
        st[s.name] = s
        assert g % 4 == 0

    job_counts = [("mod0", 1), ("ctx_rT", 1), ("ctx_z", 8), ("ctx_D0", 4), ("ctx_S0", 4), ("ctx_D1", 4), ("ctx_S1", 4),
                  ("lat_rT", 1), ("lat_z", 8), ("G0", 4), ("G1", 4), ("qT", 4), ("kT", 4), ("diag", 2)]
    for d in range(2):
        for l in range(8):
            job_counts.append((f"level{d}_{l}", 2 if l < 7 else 1))
    job_counts += [("yT", 4), ("p1T", 4), ("p2T", 4), ("gt0", 4)]
    job_counts += [("mod1", 4), ("gt1", 4), ("x1T", 8), ("zT", 8), ("pT", 8)]
    job_counts += [("x2T", 8), ("aqT", 4), ("akT", 1), ("aiT", 4), ("aiiT", 1), ("idx", 16)]

    def attention_jobs(pre, units):
        out_ = []
        for u in range(units + 1):
            if u < units:
                out_.append((f"{pre}_s{u}", 1))
            if u >= 1:
                out_ += [(f"{pre}_p{u - 1}", 1), (f"{pre}_o{u - 1}", 1)]
        return out_

    job_counts += attention_jobs("dsa", 8)
    job_counts += [("rT", 4), ("keyT", 4), ("valT", 4), ("loraT", 3), ("decay", 4), ("rate", 4), ("dgate", 4),
                   ("valN", 4), ("kknorm", 4), ("bonus", 4), ("bN", 4), ("keyN", 4), ("Aab", 8), ("Aak", 8),
                   ("Arb", 8), ("Ark", 8)]
    for c in range(8):
        job_counts += [(f"chunkR{c}", 2), (f"chunkU{c}", 2)]
        if c < 7:
            job_counts.append((f"chunkS{c}", 2))
    job_counts += [("ymean", 4), ("yvar", 4), ("memT", 8), ("x3T", 8), ("ckT", 2), ("cqT", 2)]
    job_counts += attention_jobs("cross", 4)
    job_counts += [("x4T", 8), ("h0T", 8), ("h1T", 8), ("h2T", 8), ("h3T", 8)]
    J, n = {}, 0
    for name, k in job_counts:
        J[name] = n
        n += k
    NJ = dict(job_counts)

    def bank(j):
        return BANKS[:, 4 + j % 4, :]

    def bank_free(eng, j):
        if j >= 4:
            eng.wait_ge(S(f"side_free{j % 4}"), j // 4)

    def bank_full(eng, j):
        eng.wait_ge(S(f"side_full{j % 4}"), j // 4 + 1)

    def full(ins, j):
        ins.then_inc(S(f"side_full{j % 4}"), 1)

    def free(ins, j):
        ins.then_inc(S(f"side_free{j % 4}"), 1)

    job_order = [n for n in NJ if n in ("yT", "x1T", "zT", "pT", "x2T", "memT", "x3T", "x4T", "h0T", "h1T", "h2T", "h3T")]
    CUT = {n: sum(NJ[k] for k in job_order[:i]) for i, n in enumerate(job_order)}

    def index_head(j, e):
        return 4 * (j % 4) + 2 * e + j // 4 % 2

    def copied(eng, j):
        eng.wait_ge(S(f"side_free{j % 4}"), j // 4 + 1)

    def jobs_out(eng, name):
        last = J[name] + NJ[name]
        for q in range(4):
            k = (last - q + 3) // 4
            if k > 0:
                eng.wait_ge(S(f"side_free{q}"), k)

    class Chain:

        def __init__(self, eng, name):
            self.eng, self.sem, self.n = eng, S(name), 0

        def add(self, ins):
            ins.then_inc(self.sem, 1)
            self.n += 1

        def wait(self):
            if self.n:
                self.eng.wait_ge(self.sem, self.n)

        def link(self, ins):
            self.add(ins)
            self.wait()

        def done(self, name, k=1):
            self.wait()
            self.eng.sem_inc(S(name), k)

    landed = [S(f"chunk_landed{i}") for i in range(4)]
    hi_ready, lo_ready, chunk_used, block_out = S("hi_ready"), S("lo_ready"), S("chunk_used"), S("block_out")

    def acc(B, h):
        return BANKS[:, (B % 2) * 2 + h, :]

    ACTS = {"ctx": 1, "lat": 2, "mix": 3, "cross_o": 4}

    block = ctx.enter_context(nc.Block())

    @block.sync
    def _(eng):
        def load(s, blk, kc, g):
            if not isinstance(g, int) or g >= 4:
                eng.wait_ge(lo_ready, g - 3)
            sl = kc if s.kc == 4 else g % 4
            eng.dma_start(RAW[:, sl, :, 0:s.n], s.view(kc, blk)).then_inc(landed[sl], 16)

        for s in stages:
            if s.view is None:
                continue
            if s.plain:
                for m in range(4 * s.nblk):
                    if m < 4:
                        eng.wait_ge(lo_ready, s.g0 - 3 + m)
                    else:
                        eng.wait_ge(S("plain_used"), m - 3)
                    eng.dma_start(RAW[:, m % 4], s.view(m % 4, m // 4)).then_inc(landed[m % 4], 16)
                eng.wait_ge(S("plain_used"), 4 * s.nblk)
            elif s.loop:
                first = 1 if s.g0 == 0 else 0
                for kc in range(4 * first):
                    load(s, 0, kc, kc)
                with eng.Fori(first, s.nblk) as i:
                    for kc in range(4):
                        load(s, i, kc, s.g0 + 4 * i + kc)
            else:
                for blk in range(s.nblk):
                    for kc in range(s.kc):
                        load(s, blk, kc, s.g0 + blk * s.kc + kc)

    def row_bcast(v):
        return v.rearrange("(a n) -> a n", a=1).to_broadcast([P, v.shape[0]])

    @block.gpsimd
    def _(eng):
        eng.dma_start(COLS[:, :], a["cols"]).then_inc(S("cols_in"), 16)
        eng.dma_start(CONST[:, 0:COMMON], a["common_consts"]).then_inc(S("consts_in"), 16)
        eng.dma_start(CONST[:, COMMON:COMMON + a["gla_consts"].shape[1]], a["gla_consts"]).then_inc(S("consts_in"), 16)
        eng.memset(RN2[:, :, :], 0.0).then_inc(S("rank_zeroed"), 1)
        eng.wait_ge(S("rank_zeroed"), 1)
        eng.memset(RN2[:, :, 16:17], 1.0).then_inc(S("rank_zeroed"), 1)
        eng.memset(RN2[:, :, 48:49], 1.0).then_inc(S("rank_zeroed"), 1)
        eng.dma_start(ADAROW[4:5, :], a["b_ada"][0:1, 0:4096]).then_inc(S("ada0_bias_in"), 16)
        eng.dma_start(XS[:, :, :], a["ctxT"]).then_inc(S("ctxT_in"), 16)
        eng.dma_start(XS2[:, :, :], a["xT"]).then_inc(S("xT_in"), 16)

        def gate_weights():
            eng.memset(WG[:, :], 0.0).then_inc(S("gate_w_zeroed"), 1)
            eng.wait_ge(S("gate_w_zeroed"), 1)
            eng.dma_start(WG[0:16, :], a["w_gate_f"][0]).then_inc(S("gate_w_in"), 16)
            eng.dma_start(WG[16:17, :], a["b_gate_f"]).then_inc(S("gate_w_in"), 16)
            eng.dma_start(WG[32:48, :], a["w_gate_b"][0]).then_inc(S("gate_w_in"), 16)
            eng.dma_start(WG[48:49, :], a["b_gate_b"]).then_inc(S("gate_w_in"), 16)

        jobs_out(eng, "mod0")
        gate_weights()
        jobs_out(eng, "kT")
        for b in range(16):
            bias = a["b_ada"][0:1, 4096 + b * NB:4096 + (b + 1) * NB] if b < 4 else \
                a["b_ada"][1:2, (b - 4) * NB:(b - 3) * NB]
            q = 32 * (b % 4) + 2
            eng.dma_start(ADAR[q:q + 1, b // 4, :], bias).then_inc(S("plain_bias_in"), 16)
        eng.wait_ge(S("gla_o_out"), 1)
        eng.dma_start(GNW[:, :], row_bcast(a["gla_norm_w"][0])).then_inc(S("gnw_in"), 16)
        eng.dma_start(LNG[:, :, :].rearrange("p a b -> p (a b)"), row_bcast(a["ln_g"][0])).then_inc(S("ln_in"), 16)
        eng.wait_ge(S("scores_read"), 1)
        eng.dma_start(LNB[:, :, :].rearrange("p a b -> p (a b)"), row_bcast(a["ln_b"][0])).then_inc(S("ln_in"), 16)
        jobs_out(eng, "p2T")
        for h in range(2):
            eng.dma_start(XN[:, :, h, :], a["x"][0, h * P:(h + 1) * P, :].rearrange("p (b n) -> p b n", n=NB))\
               .then_inc(S("x_in"), 16)
        def store():
            for h in range(2):
                eng.dma_start(out[0, h * P:(h + 1) * P, :].rearrange("p (b n) -> p b n", n=NB), XN[:, :, h, :])\
                   .then_inc(S("stored"), 16)
            eng.wait_ge(S("stored"), 32)

        def natural(dst, src, sem):
            for h in range(2):
                eng.dma_start(dst[:, :, h, :], src[h * P:(h + 1) * P, :].rearrange("p (b n) -> p b n", n=NB))\
                   .then_inc(S(sem), 16)

        def bcast(dst, v, sem):
            eng.dma_start(dst[:, :, :].rearrange("p a b -> p (a b)"), row_bcast(v)).then_inc(S(sem), 16)

        eng.dma_start(CONST[:, COMMON:COMMON + 1536], a["pool_consts"]).then_inc(S("pool_consts_in"), 16)
        if stop == "x1":
            eng.wait_ge(S("x1_done"), 1)
            store()
            return
        jobs_out(eng, "zT")
        eng.dma_start(CONST[:, COMMON:COMMON + a["second_consts"].shape[1]], a["second_consts"])\
           .then_inc(S("second_consts_in"), 16)
        bcast(LNG, a["ln_g"][1], "ln_in")
        eng.wait_ge(S("gated_z"), 4)
        bcast(LNB, a["ln_b"][1], "ln_in")
        if stop == "x2":
            eng.wait_ge(S("x2_done"), 1)
            store()
            return
        eng.wait_ge(S("x2_done"), 1)
        eng.dma_start(ROPE[:, 7, 0, 0:2].bitcast(I32), a["positions"]).then_inc(S("positions_in"), 16)
        eng.dma_start(WDU[0:64, :], a["w_decay_up_2"][0]).then_inc(S("ups_in"), 16)
        eng.dma_start(WDU[64:128, :], a["a_up_2"][0]).then_inc(S("ups_in"), 16)
        eng.dma_start(GU[:, 0, :], a["g_up_2"][0, 0:128, :]).then_inc(S("ups_in"), 16)
        eng.dma_start(GU[0:32, 1, :], a["g_up_2"][0, 128:160, :]).then_inc(S("ups_in"), 16)
        eng.wait_ge(S("a_ab_ready"), 1)
        sa = a["scratch_a"].rearrange("(u c) t s -> c t u s", c=4)
        for c in range(4):
            eng.dma_start(sa[c], AAB[C * c:C * (c + 1), :, :]).then_inc(S("a_ab_stored"), 16)
        eng.wait_ge(S("a_ab_stored"), 64)
        eng.dma_start(AC[:, :, :], a["scratch_a"]).then_inc(S("a_by_chunk_in"), 16)
        eng.wait_ge(S("inverse_ready"), 1)
        eng.dma_start(a["scratch_t"], TC[:, :, :]).then_inc(S("inverse_stored"), 16)
        eng.wait_ge(S("inverse_stored"), 16)
        sb = a["scratch_t"].rearrange("(u c) s t -> c s u t", c=4)
        for c in range(4):
            eng.dma_start(TT[C * c:C * (c + 1), :, :], sb[c]).then_inc(S("inverse_in"), 16)
        eng.wait_ge(S("y_delta"), 1)
        natural(MEMN, a["mem"][0], "mem_in")
        eng.wait_ge(S("h_summed"), 1 + FF)
        bcast(NFB, a["norm_final_2"], "final_gain_in")
        eng.wait_ge(S("out_ready"), 1)
        store()

    @block.scalar
    def _(eng):
        ch = Chain(eng, "act_steps")

        def hi(s, g0, i, c):
            sl = c % 4
            n = s.n
            eng.wait_ge(landed[sl], 16 * (s.ring0 // 4 + i + c // 4 + 1))
            eng.wait_ge(chunk_used, g0 + 4 * i + c + 1)
            eng.activation(WHI[:, c % 2, :, 0:n], RAW[:, sl, :, 0:n], ACT.Copy).then_inc(hi_ready, 1)

        def evac(s, i, par, last=False):
            eng.wait_ge(chunk_used, s.g0 + s.kc * i + s.kc + 2)
            if s.rows_only:
                eng.activation(s.dest(i), BANKS[0:4, par * 2, :], ACT.Copy).then_inc(block_out, 2)
                return
            for h in range(2):
                src = BANKS[:, par * 2 + h, 0:s.n]
                if s.dest == "rank":
                    eng.activation(RN2[:, h, 0:16], src[:, 0:16], ACT.Copy).then_inc(S("rank_out"), 1)
                    eng.activation(RN2[:, h, 32:48], src[:, 16:32], ACT.Copy).then_inc(block_out, 1 if h == 0 else 3)
                else:
                    scale = 1.0 if s.scale is None else RSTD[:, s.scale + h:s.scale + h + 1]
                    eng.activation(s.dest(i, h), src, s.func or ACT.Copy, scale=scale)\
                       .then_inc(block_out, 3 if h == 1 and s.nblk % 2 else 1)

        def stream(s, each=None):
            if s.loop and each is None:
                for c in range(4):
                    hi(s, s.g0, 0, c)
                if s.nblk > 2:
                    with eng.Fori(0, s.nblk // 2 - 1) as j:
                        for c in range(4, 12):
                            hi(s, s.g0, 2 * j, c)
                            if c == 5:
                                evac(s, 2 * j, 0)
                            if c == 9:
                                evac(s, 2 * j + 1, 1)
                e = s.nblk - 2
                for c in range(4, 8):
                    hi(s, s.g0, e, c)
                    if c == 5:
                        evac(s, e, 0)
                evac(s, e + 1, 1)
            else:
                back = min(s.kc, 2)
                for c in range(s.nblk * s.kc):
                    hi(s, s.g0, 0, c)
                    b = c // s.kc - 1
                    if b >= 0 and c % s.kc == back - 1:
                        evac(s, b, b % 2)
                        if each:
                            each(b)
                evac(s, s.nblk - 1, (s.nblk - 1) % 2)
                if each:
                    each(s.nblk - 1)

        def acts_out(name, scale=None, bias=None, func=None, xh=XTH, f0=0):
            for j in range(NJ[name]):
                jj = J[name] + j
                bank_full(eng, jj)
                if scale is None:
                    eng.activation(xh[:, f0 + 2 * j:f0 + 2 * j + 2, :].rearrange("p a b -> p (a b)"), bank(jj),
                                   func or ACT.Copy).then_inc(S("tile_hi"), 1)
                    continue
                for e in range(2):
                    f = 2 * j + e
                    ins = eng.activation(xh[:, f0 + f, :], bank(jj)[:, e * T:(e + 1) * T], func or ACT.Identity,
                                         scale=scale(f), bias=bias(f) if bias else 0.0)
                ins.then_inc(S("tile_hi"), 1)

        def silu_c():
            eng.wait_ge(S("cols_in"), 16)
            ch.link(eng.activation(STAT[:, 0:32], COLS[:, 0:32], ACT.Silu))
            src = STAT[:, 0:32].rearrange("p (v k) -> p v k", v=2)
            eng.wait_ge(S("cond_zeroed"), 1)
            ch.add(eng.activation(CM[:, 0:64].rearrange("p (k v e) -> p e v k", v=2, e=2)[:, 0], src, ACT.Copy))
            ch.add(eng.activation(CF[:, :, :].rearrange("p k v -> p v k"), src, ACT.Copy))
            ch.done("cond_hi")

        def split_hi(src, ready, dst=None):
            ready()
            ch.add(eng.activation(XTH[:, :, :] if dst is None else dst, src, ACT.Copy))
            ch.done("acts_hi")

        def modulate(X, col, dma_sem):
            eng.wait_ge(S(dma_sem), 16)
            eng.wait_ge(S("mod0_ready"), 1)
            for k in range(KT):
                ch.add(eng.activation(X[:, k, :], X[:, k, :], ACT.Identity, scale=MODT[:, 16 + k, col:col + 1],
                                      bias=MODT[:, k, col:col + 1]))
            ch.done("modulated")

        roots = [0]

        def root(v):
            roots[0] += 1
            eng.wait_ge(S("square_in"), roots[0])
            ch.add(eng.activation(v, v, ACT.Sqrt))
            ch.done("root_out")

        def gate_logs(pre, LA, TMP):
            bank_full(eng, J[pre + "_rT"])
            free(eng.activation(RT[:, :], bank(J[pre + "_rT"])[0:64, 0:T], ACT.Copy), J[pre + "_rT"])
            for j in range(8):
                d, h, cb = j // 4, j // 2 % 2, j % 2
                jj = J[pre + "_z"] + j
                bank_full(eng, jj)
                free(eng.activation(LA[:, d, cb, h, :], bank(jj), ACT.Copy), jj)
            for d in range(2):
                eng.wait_ge(S("neg_abs"), (1 if pre == "ctx" else 3) + d)
                ch.link(eng.activation(TMP[:, :, :, :], TMP[:, :, :, :], ACT.Exp))
                ch.add(eng.activation(TMP[:, :, :, :], TMP[:, :, :, :], ACT.Ln, bias=1.0))
                ch.done("log1p")

        silu_c()
        stream(st["ada0"])
        modulate(XS, 1, "ctxT_in")
        split_hi(XS[:, :, :], lambda: ch.wait())
        stream(st["ctx_kv"])
        stream(st["ctx_r"])
        gate_logs("ctx", LA_C, TMP_C)
        for d in range(2):
            for j in range(4):
                jj = J[f"ctx_D{d}"] + j
                if j == 0:
                    if d == 0:
                        eng.wait_ge(S("ctx_la"), 1)
                    else:
                        eng.wait_ge(S("side_full%d" % ((J["ctx_S0"] + 3) % 4)), (J["ctx_S0"] + 3) // 4 + 1)
                bank_full(eng, jj)
                free(eng.activation(TMP_C[:, j % 2, j // 2, :], bank(jj), ACT.Exp), jj)
            for j in range(4):
                jj = J[f"ctx_S{d}"] + j
                bank_full(eng, jj)
                free(eng.activation(S0[:, d, j, :, :].rearrange("p a b -> p (a b)"), bank(jj), ACT.Copy), jj)
        modulate(XS2, 0, "xT_in")
        eng.wait_ge(chunk_used, st["ctx_r"].g0 + 4 + 2)
        split_hi(XS2[:, :, :], lambda: ch.wait())
        stream(st["lat_kv"])
        stream(st["lat_r"])
        stream(st["lat_rest"])
        eng.wait_ge(block_out, 4 + 2 * st["ada_plain"].b0)
        ch.add(eng.activation(NAT[:, 6:8, :, :], NAT[:, 6:8, :, :], ACT.Silu))
        ch.add(eng.activation(NAT[:, 14:16, :, :], NAT[:, 14:16, :, :], ACT.Silu))
        ch.done("silu_gates")
        gate_logs("lat", LA_L, TMP_L)
        for j in range(4):
            jj = J["G0"] + j
            bank_full(eng, jj)
            free(eng.activation(GF_[:, 2 * j:2 * j + 2, :].rearrange("p a b -> p (a b)"), bank(jj), ACT.Copy), jj)
        for j in range(4):
            jj = J["G1"] + j
            bank_full(eng, jj)
            free(eng.activation(GB_[:, 2 * j:2 * j + 2, :].rearrange("p a b -> p (a b)"), bank(jj), ACT.Copy), jj)
        eng.wait_ge(S("mixed_products"), 1)
        for j in range(4):
            jj = J["qT"] + j
            bank_full(eng, jj)
            free(eng.activation(QT[:, 2 * j:2 * j + 2, :].rearrange("p a b -> p (a b)"), bank(jj), ACT.Copy,
                                scale=DK ** -0.5), jj)
        for j in range(4):
            jj = J["kT"] + j
            bank_full(eng, jj)
            free(eng.activation(KTT[:, 2 * j:2 * j + 2, :].rearrange("p a b -> p (a b)"), bank(jj), ACT.Copy), jj)
        def plain_out(b):
            s = st["ada_plain"]
            eng.wait_ge(S("plain_used"), 4 * (b + 1))
            q = 32 * (b % 4)
            eng.activation(ADAR[q:q + 2, b // 4, :], BANKS[q:q + 2, ((s.b0 + b) % 2) * 2, :], ACT.Copy)\
               .then_inc(block_out, 2)

        for n in range(18):
            if 1 <= n < 17:
                plain_out(n - 1)
            Wn = (W0, W1)[n % 2]
            if n < 16:
                eng.wait_ge(S("decay_args"), n + 1)
                ch.add(eng.activation(Wn[:, :, :], Wn[:, :, :], ACT.Exp))
            else:
                if n == 16:
                    jobs_out(eng, "level1_6")
                else:
                    jobs_out(eng, "level1_7")
                ch.add(eng.activation(Wn[:, :, :], (GF_, GB_)[n - 16][:, :, :], ACT.Exp))
            ch.done("decay_exp")
        s = st["gla_o"]
        for B in range(2):
            eng.wait_ge(S("gla_o_full"), B + 1)
            for h in range(2):
                eng.activation(O[:, B, 2 * h:2 * h + 2, :].rearrange("p a b -> p (a b)"), acc(B, h), ACT.Copy)\
                   .then_inc(block_out, 1)
        eng.wait_ge(block_out, 4 + 2 * (s.b0 + 2))
        eng.sem_inc(S("gla_o_out"), 1)
        for h in range(2):
            for k in range(HEADS):
                ch.add(eng.activation(MTMP[:, 0:2, :].rearrange("p a b -> p (a b)"), O[:, h, k, :], ACT.Square,
                                      accum_out=STAT[:, h * 4 + k:h * 4 + k + 1]))
                ch.wait()
        ch.done("o_squares")
        root(STAT[:, 0:8])
        for name, dst in (("yT", None), ("p1T", P1T), ("p2T", P2T)):
            if dst is None:
                acts_out("yT")
                continue
            for j in range(4):
                jj = J[name] + j
                bank_full(eng, jj)
                free(eng.activation(dst[:, 2 * j:2 * j + 2, :].rearrange("p a b -> p (a b)"), bank(jj), ACT.Copy), jj)
        for q in range(2):
            eng.wait_ge(S("conv_done"), q + 1)
            ch.add(eng.activation(XTH[:, 8 + 4 * q:12 + 4 * q, :], XS[:, 8 + 4 * q:12 + 4 * q, :], ACT.Copy))
            ch.done("conv_hi")
        for j in range(4):
            jj = J["gt0"] + j
            bank_full(eng, jj)
            free(eng.activation(GTB[:, j, :], bank(jj), ACT.Copy), jj)
        stream(st["out_e"])
        root(STAT[:, 66:71:4])
        if stop == "x1":
            return

        def tiles_out(name, dst, n=T, scale=None, bias=None, func=None, f0=0):
            for j in range(NJ[name]):
                jj = J[name] + j
                bank_full(eng, jj)
                if scale is None:
                    free(eng.activation(dst[:, f0 + 2 * j:f0 + 2 * j + 2, :].rearrange("p a b -> p (a b)"), bank(jj),
                                        func or ACT.Copy), jj)
                    continue
                for e in range(2):
                    f = 2 * j + e
                    ins = eng.activation(dst[:, f0 + f, :], bank(jj)[:, e * T:(e + 1) * T], func or ACT.Identity,
                                         scale=scale(f), bias=bias(f) if bias else 0.0)
                free(ins, jj)

        def wait_jobs(*names):
            for n in names:
                jobs_out(eng, n)

        for j in range(4):
            jj = J["gt1"] + j
            bank_full(eng, jj)
            free(eng.activation(GTB1[:, j, :], bank(jj), ACT.Copy), jj)
        eng.wait_ge(S("norm_cols"), 1)
        norm_cols = dict(scale=lambda f: NORMC[:, 0, f:f + 1], bias=lambda f: NORMC[:, 1, f:f + 1])
        acts_out("x1T", **norm_cols)
        stream(st["in_o"])
        acts_out("zT")
        eng.wait_ge(block_out, 4 + 2 * st["pool"].b0)
        for q in range(4):
            ch.add(eng.activation(NATO[:, 4 + q:5 + q, :, :], NATO[:, 4 + q:5 + q, :, :], ACT.Silu))
            ch.done("silu_pool")
        stream(st["pool"])
        acts_out("pT", scale=lambda f: cols("pool_scale", f))
        stream(st["out_o"])
        root(STAT[:, 66:71:4])
        if stop == "x2":
            return

        NORMED = place("squares_scratch", 191.5, [P, 4, 2, NB])

        def rms_squares(src, c, scratch):
            for h in range(2):
                ch.link(eng.activation(scratch[:, :, h, :], src[:, :, h, :], ACT.Square,
                                       accum_out=STAT[:, 88 + h:89 + h]))
            ch.done("rms_squares")
            roots[0] += 1
            eng.wait_ge(S("square_in"), roots[0])
            ch.add(eng.activation(RSTD[:, c:c + 2], RSTD[:, c:c + 2], ACT.Sqrt))
            ch.done("root_out")
            rms_squares.n += 1
            eng.wait_ge(S("rstd_ready"), rms_squares.n)

        rms_squares.n = 0

        def softmax_rows(pre, units, SPb, PTb, dst, f0):
            def copies(u):
                pair, half = u // 2, u % 2
                jj = J[f"{pre}_p{u}"]
                if u >= 2:
                    bank_full(eng, J[f"{pre}_o{u - 2}"])
                bank_full(eng, jj)
                free(eng.activation(PTb[:, u % 2, :], bank(jj), ACT.Copy), jj)
                jj = J[f"{pre}_o{u}"]
                bank_full(eng, jj)
                free(eng.activation(dst[:, f0 + 2 * pair:f0 + 2 * pair + 2, half * P:(half + 1) * P],
                                    bank(jj)[:, 0:T].rearrange("p (a b) -> p a b", a=2), ACT.Copy), jj)

            for u in range(units):
                eng.wait_ge(S(pre + "_shifted"), u + 1)
                for e in range(2):
                    ch.add(eng.activation(SPb[:, u % 2, e, :], SPb[:, u % 2, e, :], ACT.Exp,
                                          bias=STAT[:, 64 + 4 * (u % 2) + e:65 + 4 * (u % 2) + e],
                                          accum_out=STAT[:, 66 + 4 * (u % 2) + e:67 + 4 * (u % 2) + e]))
                ch.done(pre + "_exp")
                if u >= 1:
                    copies(u - 1)
            copies(units - 1)

        eng.wait_ge(S("norm_cols"), 2)
        acts_out("x2T", **norm_cols)
        eng.wait_ge(S("x2_done"), 1)
        rms_squares(XN, 0, Y)
        for n in ("rkv", "lora", "att4", "att1", "kiwi"):
            stream(st[n])
        eng.wait_ge(S("angles"), 1)
        ch.add(eng.activation(ROPE[:, 0:2, :, :], ROPE[:, 2:4, :, :], ACT.Sin))
        ch.done("sines")
        tiles_out("aqT", QTA)
        jj = J["akT"]
        bank_full(eng, jj)
        free(eng.activation(KTA[:, :, :].rearrange("p a b -> p (a b)"), bank(jj), ACT.Copy), jj)
        tiles_out("aiT", QIT)
        jj = J["aiiT"]
        bank_full(eng, jj)
        free(eng.activation(KIT[:, :], bank(jj)[:, 0:T], ACT.Copy), jj)
        for j in range(16):
            jj = J["idx"] + j
            if j >= 2:
                eng.wait_ge(S("index_added"), j - 1)
            bank_full(eng, jj)
            free(eng.activation(RL[:, j % 2, :, :].rearrange("p a b -> p (a b)"), bank(jj), ACT.Relu), jj)
        softmax_rows("dsa", 8, SP, PT, XS, 8)
        tiles_out("rT", RTT)
        tiles_out("keyT", KTR)
        tiles_out("valT", VTR)
        for j, w in enumerate((P, P, 32)):
            jj = J["loraT"] + j
            bank_full(eng, jj)
            free(eng.activation(LT[0:w, j, :], bank(jj)[0:w, 0:T], ACT.Copy), jj)
        eng.wait_ge(S("lora_mixed"), 1)
        ch.add(eng.activation(LT[0:64, 0, :], LT[0:64, 0, :], ACT.Tanh))
        ch.add(eng.activation(LT[:, 1, :], LT[:, 1, :], ACT.Sigmoid))
        ch.add(eng.activation(LT[0:32, 2, :], LT[0:32, 2, :], ACT.Sigmoid))
        ch.done("lora_acts")
        tiles_out("decay", SIG, scale=lambda f: 1.0, bias=lambda f: cols("w_decay0_2", f), func=ACT.Sigmoid)
        tiles_out("rate", AT, scale=lambda f: 1.0, bias=lambda f: cols("a0_2", f), func=ACT.Sigmoid)
        tiles_out("dgate", GT)

        def natural_out(name, dst):
            for j in range(4):
                jj = J[name] + j
                bank_full(eng, jj)
                free(eng.activation(dst[:, j // 2, (j % 2) * NB:(j % 2 + 1) * NB], bank(jj), ACT.Copy), jj)

        natural_out("valN", VN)
        tiles_out("kknorm", NRM, func=ACT.Sqrt)
        DEC = float(np.exp(-0.5))
        eng.wait_ge(S("cum_ready"), 1)
        ch.add(eng.activation(NRM[:, :, :], LG[:, :, :], ACT.Exp, scale=DEC))
        ch.add(eng.activation(SIG[:, :, :], SIG[:, :, :], ACT.Exp, scale=-DEC))
        ch.done("inv_decay")
        eng.wait_ge(S("cum_read"), 1)
        ch.wait()
        ch.add(eng.activation(LG[:, :, :], LG[:, :, :], ACT.Exp, scale=-DEC))
        ch.done("decays")
        natural_out("bN", BN)
        natural_out("keyN", KN)
        for c in range(8):
            half, r = c // 4, slice(C * (c % 4), C * (c % 4) + C)
            for name, dst in ((f"chunkR{c}", RS), (f"chunkU{c}", U)):
                jj = J[name]
                bank_full(eng, jj)
                free(eng.activation(dst[r, half, 0:NB], bank(jj)[r, :], ACT.Copy), jj)
        s = st["delta_y"]
        eng.wait_ge(S("delta_y_full"), 1)
        for q in range(4):
            eng.activation(YT[:, 2 * q:2 * q + 2, :].rearrange("p a b -> p (a b)"), BANKS[:, q, :], ACT.Copy)\
               .then_inc(block_out, 1)
        eng.wait_ge(S("y_centred"), 1)
        ch.add(eng.activation(SQ[:, :, :], YT[:, :, :], ACT.Square))
        ch.done("y_squares")
        eng.wait_ge(S("y_var"), 1)
        ch.add(eng.activation(VAR[:, :, :], VAR[:, :, :], ACT.Sqrt))
        ch.done("y_std")
        split_hi(XS[:, :, :], lambda: eng.wait_ge(S("y_delta"), 1) or wait_jobs("dsa_o7"))
        stream(st["mix"])
        acts_out("memT", scale=lambda f: cols("norm_mem_2", f))
        rms_squares(MEMN, 2, NORMED)
        stream(st["cross_kv"])
        acts_out("x3T", scale=lambda f: cols("norm_cross_2", f))
        rms_squares(XN, 4, Y)
        stream(st["cross_q"])
        tiles_out("ckT", CKT)
        tiles_out("cqT", CQT)
        softmax_rows("cross", 4, CSP, CPT, XS, 0)
        split_hi(XS[:, 0:4, :], lambda: wait_jobs("cross_o3"), XTH[:, 0:4, :])
        stream(st["cross_o"])
        acts_out("x4T", scale=lambda f: cols("norm_mlp_2", f))
        rms_squares(XN, 6, Y)
        stream(st["up0"])
        acts_out("h0T", xh=XTH2)
        stream(st["up1"])
        for q in range(FF):
            stream(st[f"down{q}"])
            if q + 1 < FF:
                acts_out(f"h{q + 1}T", xh=XTH2)
            if q + 2 < FF:
                stream(st[f"up{q + 2}"])
        eng.wait_ge(S("h_summed"), 1 + FF)
        rms_squares(XN, 6, UPN)

    @block.vector
    def _(eng):
        ch = Chain(eng, "dve_steps")

        def lo(s, g0, i, c):
            n = s.n
            eng.wait_ge(hi_ready, g0 + 4 * i + c + 1)
            eng.tensor_tensor(WLO[:, c % 2, :, 0:n], RAW[:, c % 4, :, 0:n], WHI[:, c % 2, :, 0:n].bitcast(F32),
                              ALU.subtract).then_inc(lo_ready, 1)

        def stream(s, each=None):
            if s.loop and each is None:
                with eng.Fori(0, s.nblk) as i:
                    for c in range(4):
                        lo(s, s.g0, i, c)
            else:
                for c in range(s.nblk * s.kc):
                    lo(s, s.g0, 0, c)
                    b = c // s.kc - 1
                    if each and b >= 0 and c % s.kc == min(s.kc, 3) - 1:
                        eng.wait_ge(block_out, 4 + 2 * (s.b0 + b + 1))
                        each(b)
                if each:
                    eng.wait_ge(block_out, 4 + 2 * (s.b0 + s.nblk))
                    each(s.nblk - 1)

        def acts_in(name, scale=None, bias=None, xh=XTH, xl=XTL, f0=0):
            for j in range(NJ[name]):
                jj = J[name] + j
                eng.wait_ge(S("tile_hi"), CUT[name] + j + 1)
                bank_full(eng, jj)
                if scale is None:
                    both = [t[:, f0 + 2 * j:f0 + 2 * j + 2, :].rearrange("p a b -> p (a b)") for t in (xl, xh)]
                    free(eng.tensor_tensor(both[0], bank(jj), both[1].bitcast(F32), ALU.subtract), jj)
                    continue
                for e in range(2):
                    f = 2 * j + e
                    src = bank(jj)[:, e * T:(e + 1) * T]
                    if bias is None:
                        ins = eng.scalar_tensor_tensor(out=xl[:, f, :], in0=src, scalar=scale(f),
                                                       in1=xh[:, f, :].bitcast(F32), op0=ALU.mult, op1=ALU.subtract)
                    else:
                        ch.link(eng.tensor_scalar(TILE[:, e, :], src, scale(f), bias(f), ALU.mult, ALU.add))
                        ins = eng.tensor_tensor(xl[:, f, :], TILE[:, e, :], xh[:, f, :].bitcast(F32), ALU.subtract)
                free(ins, jj)

        def split_lo(src, n, hi_=None, lo_=None):
            hi_ = XTH[:, :, :] if hi_ is None else hi_
            lo_ = XTL[:, :, :] if lo_ is None else lo_
            eng.wait_ge(S("acts_hi"), n)
            ch.add(eng.tensor_tensor(lo_, src, hi_.bitcast(F32), ALU.subtract))
            ch.done("acts_lo")

        roots = [0]

        def rsqrt(v):
            roots[0] += 1
            ch.done("square_in")
            eng.wait_ge(S("root_out"), roots[0])
            ch.link(eng.reciprocal(v, v))

        def gate_logs(pre, LA, TMP):
            jobs_out(eng, pre + "_z")
            for d in range(2):
                z = LA[:, d, :, :, :].rearrange("p a b c -> p (a b c)")
                t = TMP[:, :, :, :].rearrange("p a b c -> p (a b c)")
                ch.add(eng.scalar_tensor_tensor(out=t, in0=z, scalar=-1.0, in1=z, op0=ALU.mult, op1=ALU.min))
                ch.done("neg_abs")
                eng.wait_ge(S("log1p"), (1 if pre == "ctx" else 3) + d)
                ch.link(eng.scalar_tensor_tensor(out=z, in0=z, scalar=0.0, in1=t, op0=ALU.min, op1=ALU.subtract))
            ch.done(pre + "_la")

        eng.memset(CM[:, :].bitcast(F32), 0.0).then_inc(S("cond_zeroed"), 1)
        eng.sem_inc(block_out, 4)
        eng.wait_ge(S("cond_hi"), 1)
        e2 = CM[:, 0:64].rearrange("p (k v e) -> p e v k", v=2, e=2)
        ch.add(eng.tensor_tensor(e2[:, 1], STAT[:, 0:32].rearrange("p (v k) -> p v k", v=2), e2[:, 0].bitcast(F32),
                                 ALU.subtract))
        ch.done("cond_lo")
        stream(st["ada0"])
        jm = J["mod0"]
        bank_full(eng, jm)
        ch.add(eng.tensor_copy(MODT[:, 0:16, :].rearrange("p a b -> p (a b)"), bank(jm)[:, 0:32]))
        free(eng.tensor_scalar(MODT[:, 16:32, :].rearrange("p a b -> p (a b)"), bank(jm)[:, 32:64], 1.0, None,
                               ALU.add), jm)
        jobs_out(eng, "mod0")
        ch.done("mod0_ready")
        split_lo(XS[:, :, :], 1)
        stream(st["ctx_kv"])
        stream(st["ctx_r"])
        gate_logs("ctx", LA_C, TMP_C)
        for d in range(2):
            jobs_out(eng, f"ctx_D{d}")
            ch.add(eng.tensor_tensor(TMP_C[:, :, :, :].rearrange("p a b c -> p (a b c)"),
                                     TMP_C[:, :, :, :].rearrange("p a b c -> p (a b c)"),
                                     NAT[:, 0:2, :, :].rearrange("p a b c -> p (a b c)"), ALU.mult))
            ch.done("ctx_kd")
        split_lo(XS2[:, :, :], 2)
        stream(st["lat_kv"])
        stream(st["lat_r"])
        stream(st["lat_rest"])
        eng.wait_ge(S("silu_gates"), 1)
        ch.add(eng.tensor_tensor(NAT[:, 10:12, :, :].rearrange("p a b c -> p (a b c)"),
                                 NAT[:, 10:12, :, :].rearrange("p a b c -> p (a b c)"),
                                 NAT[:, 12:14, :, :].rearrange("p a b c -> p (a b c)"), ALU.mult))
        ch.add(eng.tensor_tensor(NAT[:, 8:10, :, :].rearrange("p a b c -> p (a b c)"),
                                 NAT[:, 8:10, :, :].rearrange("p a b c -> p (a b c)"),
                                 NAT[:, 14:16, :, :].rearrange("p a b c -> p (a b c)"), ALU.mult))
        ch.done("mixed_products")
        gate_logs("lat", LA_L, TMP_L)
        jobs_out(eng, "kT")
        steps = [(d, l) for d in range(2) for l in range(8)]

        def pairs(t, b):
            return t[:, :, :].rearrange("p f t -> p (f t)").rearrange("p (m two b) -> p two m b", two=2, b=b)

        def args(n):
            d, l = steps[n]
            b = 1 << l
            Wv, Gv = pairs((W0, W1)[n % 2], b), pairs((GF_, GB_)[d], b)
            m = 8 * T // (2 * b)
            if n >= 2:
                dd, ll = steps[n - 2]
                jobs_out(eng, f"level{dd}_{ll}")
            if d == 0:
                ref = Gv[:, 0, :, b - 1:b].to_broadcast([P, m, b])
                ch.add(eng.tensor_tensor(Wv[:, 0], ref, Gv[:, 0], ALU.subtract))
                ch.add(eng.tensor_tensor(Wv[:, 1], Gv[:, 1], ref, ALU.subtract))
            else:
                ref = Gv[:, 1, :, 0:1].to_broadcast([P, m, b])
                ch.add(eng.tensor_tensor(Wv[:, 0], Gv[:, 0], ref, ALU.subtract))
                ch.add(eng.tensor_tensor(Wv[:, 1], ref, Gv[:, 1], ALU.subtract))
            ch.done("decay_args")

        def factors(n):
            d, l = steps[n]
            b = 1 << l
            Wv = pairs((W0, W1)[n % 2], b)
            first, second = ((KTT, QT), (QT, KTT))[d]
            eng.wait_ge(S("decay_exp"), n + 1)
            ch.add(eng.tensor_tensor(Wv[:, 0], Wv[:, 0], pairs(first, b)[:, 0], ALU.mult))
            ch.add(eng.tensor_tensor(Wv[:, 1], Wv[:, 1], pairs(second, b)[:, 1], ALU.mult))
            ch.done("factors")

        def collect(n):
            d, l = steps[n]
            name = f"level{d}_{l}"
            if l == 7:
                jj = J[name]
                bank_full(eng, jj)
                free(eng.tensor_copy(ACCX[:, :, d, :], bank(jj).rearrange("p (a b) -> p a b", a=4)), jj)
                return
            for j in range(2):
                jj = J[name] + j
                bank_full(eng, jj)
                mask = const(f"mask{d}_{l}").rearrange("p (a b) -> p a b", a=1).to_broadcast([P, 4, P])
                ch.wait()
                free(eng.tensor_tensor(MTMP[:, :, :], bank(jj).rearrange("p (a b) -> p a b", a=4), mask, ALU.mult), jj)
                eng.wait_ge(S(f"side_free{jj % 4}"), jj // 4 + 1)
                dst = ACCD[:, 2 * j:2 * j + 2, :, :].rearrange("p a b c -> p (a b c)")
                ch.link(eng.tensor_tensor(dst, dst, MTMP[:, :, :].rearrange("p a b -> p (a b)"), ALU.add))

        for j in range(2):
            jj = J["diag"] + j
            bank_full(eng, jj)
            free(eng.scalar_tensor_tensor(out=ACCD[:, 2 * j:2 * j + 2, :, :].rearrange("p a b c -> p (a b) c"),
                                          in0=bank(jj).rearrange("p (a b) -> p a b", a=4), scalar=2.0,
                                          in1=ident.rearrange("p (a b) -> p a b", a=1).to_broadcast([P, 4, P]),
                                          op0=ALU.mult, op1=ALU.mult), jj)
        jobs_out(eng, "diag")
        args(0)
        for n in range(16):
            factors(n)
            if n >= 1:
                collect(n - 1)
            if n + 1 < 16:
                args(n + 1)
        collect(15)
        for n in (16, 17):
            eng.wait_ge(S("decay_exp"), n + 1)
            Wn = (W0, W1)[n % 2]
            ch.add(eng.tensor_tensor(Wn[:, :, :], Wn[:, :, :], QT[:, :, :], ALU.mult))
            ch.wait()
        jobs_out(eng, "level1_7")
        ch.done("state_factors")
        eng.wait_ge(S("o_squares"), 1)
        ch.link(eng.tensor_scalar(STAT[:, 0:8], STAT[:, 0:8], 1.0 / DK, EPS, ALU.mult, ALU.add))
        rsqrt(STAT[:, 0:8])
        eng.wait_ge(S("gnw_in"), 16)
        for h in range(2):
            for k in range(HEADS):
                ch.link(eng.scalar_tensor_tensor(out=O[:, h, k, :], in0=O[:, h, k, :],
                                                 scalar=STAT[:, h * 4 + k:h * 4 + k + 1], in1=GNW[:, :],
                                                 op0=ALU.mult, op1=ALU.mult))
        for h in range(2):
            ch.add(eng.tensor_tensor(O[:, h, :, :].rearrange("p (c k) v -> p c (k v)", c=2),
                                     O[:, h, :, :].rearrange("p (c k) v -> p c (k v)", c=2),
                                     NAT[:, 6:8, h, :], ALU.mult))
        ch.done("y_b")
        eng.sem_inc(S("scores_read"), 1)
        acts_in("yT")
        jobs_out(eng, "p2T")
        for f in range(8):
            x4 = P1T[:, f, :].rearrange("p (r c) -> p r c", c=ROW)
            o4 = CV[:, f, :].rearrange("p (r c) -> p r c", c=ROW)
            ch.link(eng.tensor_scalar(CV[:, f, :], P1T[:, f, :], cols("conv_w1", f), None, ALU.mult))
            ch.link(eng.scalar_tensor_tensor(out=o4[:, :, 1:ROW], in0=x4[:, :, 0:ROW - 1], scalar=cols("conv_w0", f),
                                             in1=o4[:, :, 1:ROW], op0=ALU.mult, op1=ALU.add))
            ch.link(eng.scalar_tensor_tensor(out=o4[:, :, 0:ROW - 1], in0=x4[:, :, 1:ROW], scalar=cols("conv_w2", f),
                                             in1=o4[:, :, 0:ROW - 1], op0=ALU.mult, op1=ALU.add))
            ch.link(eng.tensor_tensor(XS[:, 8 + f, :], CV[:, f, :], P2T[:, f, :], ALU.mult))
            if f % 4 == 3:
                eng.sem_inc(S("conv_done"), 1)
        for q in range(2):
            eng.wait_ge(S("conv_hi"), q + 1)
            r = slice(8 + 4 * q, 12 + 4 * q)
            ch.add(eng.tensor_tensor(XTL[:, r, :], XS[:, r, :], XTH[:, r, :].bitcast(F32), ALU.subtract))
            ch.done("conv_lo")

        def residual_norm(name, s, G, natural_gain):
            jobs_out(eng, name)

            def each(b):
                for h in range(2):
                    ch.add(eng.tensor_tensor(Y[:, b, h, :], Y[:, b, h, :], G[:, b, :], ALU.mult))
                ch.wait()
                ch.link(eng.scalar_tensor_tensor(out=XN[:, b, :, :].rearrange("p b c -> p (b c)"),
                                                 in0=XN[:, b, :, :].rearrange("p b c -> p (b c)"), scalar=ALPHA,
                                                 in1=Y[:, b, :, :].rearrange("p b c -> p (b c)"),
                                                 op0=ALU.mult, op1=ALU.add))
                for h in range(2):
                    ch.add(eng.bn_stats(STAT[:, h * 32 + 6 * b:h * 32 + 6 * b + 6], XN[:, b, h, :]))

            stream(s, each)
            ch.wait()
            for h in range(2):
                ch.add(eng.bn_aggr(STAT[:, 64 + 4 * h:66 + 4 * h], STAT[:, h * 32:h * 32 + 24]))
            ch.wait()
            for h in range(2):
                ch.add(eng.tensor_scalar(STAT[:, 66 + 4 * h:67 + 4 * h], STAT[:, 65 + 4 * h:66 + 4 * h], EPS, None,
                                         ALU.add))
            rsqrt(STAT[:, 66:71:4])
            for b in range(4):
                for h in range(2):
                    ch.add(eng.tensor_scalar(XN[:, b, h, :], XN[:, b, h, :], STAT[:, 64 + 4 * h:65 + 4 * h],
                                             STAT[:, 66 + 4 * h:67 + 4 * h], ALU.subtract, ALU.mult))
                ch.done("block_normed")

        def gain_bias(sem_value):
            eng.wait_ge(S("ln_in"), sem_value)
            for h in range(2):
                ch.add(eng.tensor_tensor(XN[:, :, h, :], XN[:, :, h, :], LNG[:, :, :], ALU.mult))
            ch.wait()
            for h in range(2):
                ch.add(eng.tensor_tensor(XN[:, :, h, :], XN[:, :, h, :], LNB[:, :, :], ALU.add))

        norm_cols = dict(scale=lambda f: NORMC[:, 0, f:f + 1], bias=lambda f: NORMC[:, 1, f:f + 1])
        eng.wait_ge(S("x_in"), 32)
        residual_norm("gt0", st["out_e"], GTB, None)
        g0, b0 = COL_AT["ln_g0"], COL_AT["ln_b0"]
        for j in range(4):
            jm = J["mod1"] + j
            bank_full(eng, jm)
            sh, sc = slice(4 * j, 4 * j + 4), slice(KT + 4 * j, KT + 4 * j + 4)
            ch.add(eng.tensor_copy(MODT[:, sh, 0:1].rearrange("p a b -> p (a b)"), bank(jm)[:, sh]))
            free(eng.tensor_scalar(MODT[:, sc, 0:1].rearrange("p a b -> p (a b)"), bank(jm)[:, sc], 1.0, None,
                                   ALU.add), jm)
        jobs_out(eng, "mod1")
        ch.wait()
        sc1 = MODT[:, 16:32, 0:1].rearrange("p a b -> p (a b)")
        ch.add(eng.tensor_tensor(NORMC[:, 0, :], COLS[:, g0:g0 + KT], sc1, ALU.mult))
        ch.link(eng.tensor_tensor(NORMC[:, 1, :], COLS[:, b0:b0 + KT], sc1, ALU.mult))
        ch.add(eng.tensor_tensor(NORMC[:, 1, :], NORMC[:, 1, :], MODT[:, 0:16, 0:1].rearrange("p a b -> p (a b)"),
                                 ALU.add))
        ch.done("norm_cols")
        if stop == "x1":
            gain_bias(32)
            ch.done("x1_done")
            return

        def flat(t):
            return t.rearrange("p a b c -> p (a b c)")

        acts_in("x1T", **norm_cols)
        gain_bias(32)
        ch.done("x1_done")
        stream(st["in_o"])
        acts_in("zT")

        def gate_z(b):
            eng.wait_ge(S("silu_pool"), b + 1)
            ch.add(eng.tensor_tensor(Y[:, b, :, :], Y[:, b, :, :], NATO[:, 4 + b, :, :], ALU.mult))
            ch.done("gated_z")

        stream(st["pool"], gate_z)
        acts_in("pT", scale=lambda f: cols("pool_scale", f))
        g0, b0, m0 = COL_AT["ln_g1"], COL_AT["ln_b1"], COL_AT["norm_mix_2"]
        jobs_out(eng, "x1T")
        ch.add(eng.tensor_tensor(NORMC[:, 0, :], COLS[:, g0:g0 + KT], COLS[:, m0:m0 + KT], ALU.mult))
        ch.add(eng.tensor_tensor(NORMC[:, 1, :], COLS[:, b0:b0 + KT], COLS[:, m0:m0 + KT], ALU.mult))
        ch.done("norm_cols")
        residual_norm("gt1", st["out_o"], GTB1, None)
        if not stop:
            acts_in("x2T", **norm_cols)
        gain_bias(64)
        ch.done("x2_done")
        if stop == "x2":
            return

        def inverse_rms(c):
            inverse_rms.n += 1
            eng.wait_ge(S("rms_squares"), inverse_rms.n)
            ch.link(eng.tensor_scalar(RSTD[:, c:c + 2], STAT[:, 88:90], 1.0 / D, EPS, ALU.mult, ALU.add))
            rsqrt(RSTD[:, c:c + 2])
            eng.sem_inc(S("rstd_ready"), 1)

        inverse_rms.n = 0

        def softmax_rows(pre, units, SPb, scale, bias):
            for u in range(units):
                half = u % 2
                m, z = 64 + 4 * (u % 2), 66 + 4 * (u % 2)
                if u >= 2:
                    bank_full(eng, J[f"{pre}_p{u - 2}"])
                jj = J[f"{pre}_s{u}"]
                bank_full(eng, jj)
                sc = bank(jj).rearrange("p (a b) -> p a b", a=2)
                if bias is None:
                    free(eng.tensor_scalar(SPb[:, u % 2], sc, scale, None, ALU.mult), jj)
                else:
                    b = bias[:, half, :].rearrange("p (a b) -> p a b", a=1).to_broadcast([P, 2, T])
                    free(eng.scalar_tensor_tensor(out=SPb[:, u % 2], in0=sc, scalar=scale, in1=b, op0=ALU.mult,
                                                  op1=ALU.add), jj)
                copied(eng, jj)
                ch.link(eng.tensor_reduce(STAT[:, m:m + 2], SPb[:, u % 2], AX.X, ALU.max))
                ch.add(eng.tensor_scalar(STAT[:, m:m + 2], STAT[:, m:m + 2], -1.0, None, ALU.mult))
                ch.done(pre + "_shifted")
                eng.wait_ge(S(pre + "_exp"), u + 1)
                ch.link(eng.reciprocal(STAT[:, z:z + 2], STAT[:, z:z + 2]))
                for e in range(2):
                    ch.add(eng.tensor_scalar(SPb[:, u % 2, e, :], SPb[:, u % 2, e, :], STAT[:, z + e:z + e + 1], None,
                                             ALU.mult))
                ch.done(pre + "_probs")

        inverse_rms(0)
        for n in ("rkv", "lora", "att4", "att1", "kiwi"):
            stream(st[n])
        eng.wait_ge(S("positions_in"), 16)
        eng.wait_ge(S("second_consts_in"), 16)
        ch.link(eng.tensor_copy(ROPE[:, 6, 0, 0:2], ROPE[:, 7, 0, 0:2].bitcast(I32)))
        for h in range(2):
            ch.add(eng.tensor_scalar(ROPE[:, 2, h, :], const("inv_freq"), ROPE[:, 6, 0, h:h + 1], None, ALU.mult))
        ch.wait()
        magic = 1.5 * 2.0 ** 23
        ch.link(eng.tensor_scalar(ROPE[:, 4], ROPE[:, 2], float(1 / (2 * np.pi)), magic, ALU.mult, ALU.add))
        ch.link(eng.tensor_scalar(ROPE[:, 4], ROPE[:, 4], magic, None, ALU.subtract))
        for part in (-6.28125, -0.0019350051879882812, -3.019916050e-07):
            ch.link(eng.scalar_tensor_tensor(out=ROPE[:, 2], in0=ROPE[:, 4], scalar=part, in1=ROPE[:, 2],
                                             op0=ALU.mult, op1=ALU.add))
        ch.link(eng.tensor_scalar(ROPE[:, 3], ROPE[:, 2], float(np.pi / 2), None, ALU.add))
        ch.link(eng.tensor_scalar(ROPE[:, 4], ROPE[:, 3], float(np.pi), -float(2 * np.pi), ALU.is_gt, ALU.mult))
        ch.link(eng.tensor_tensor(ROPE[:, 3], ROPE[:, 3], ROPE[:, 4], ALU.add))
        ch.add(eng.tensor_scalar(ROPE[:, 2:4], ROPE[:, 2:4], 3.1415925, -3.1415925, ALU.min, ALU.max))
        ch.done("angles")
        eng.wait_ge(S("sines"), 1)
        eng.wait_ge(block_out, 4 + 2 * st["delta_y"].b0)

        def rope(x, heads, width, half, step):
            sin = ROPE[:, 0, rope.h, 0:16:step].rearrange("p (a b) -> p a b", a=1).to_broadcast([P, heads, half])
            cos = ROPE[:, 1, rope.h, 0:16:step].rearrange("p (a b) -> p a b", a=1).to_broadcast([P, heads, half])
            x1, x2 = x[:, :, 0:half], x[:, :, half:2 * half]
            t = [ROT[:, k, 0:heads * half].rearrange("p (a b) -> p a b", a=heads) for k in range(4)]
            ch.add(eng.tensor_tensor(t[0], x1, cos, ALU.mult))
            ch.add(eng.tensor_tensor(t[1], x2, sin, ALU.mult))
            ch.add(eng.tensor_tensor(t[2], x2, cos, ALU.mult))
            ch.link(eng.tensor_tensor(t[3], x1, sin, ALU.mult))
            ch.add(eng.tensor_tensor(x1, t[0], t[1], ALU.subtract))
            ch.link(eng.tensor_tensor(x2, t[2], t[3], ALU.add))

        for h in range(2):
            rope.h = h
            for b in range(2):
                rope(NA[:, b, h, :].rearrange("p (c d) -> p c d", d=128), 4, 128, 16, 1)
            rope(NA[:, 2, h, 0:256].rearrange("p (c d) -> p c d", d=128), 2, 128, 16, 1)
            for b in (3, 4):
                rope(NA[:, b, h, :].rearrange("p (c d) -> p c d", d=64), 8, 64, 8, 2)
            rope(KIWI[:, h, 0:64].rearrange("p (c d) -> p c d", d=64), 1, 64, 8, 2)
            for e in range(2):
                ch.add(eng.tensor_copy(KI2[:, h, e * 64:(e + 1) * 64], KIWI[:, h, 0:64]))
            ch.add(eng.tensor_scalar(KIWI[:, h, 64:80], KIWI[:, h, 64:80], 1.0 / 32.0, None, ALU.mult))
        ch.done("roped")
        ch.link(eng.memset(SC[:, :, :], 0.0))
        for j in range(16):
            half = j // 8
            jj = J["idx"] + j
            copied(eng, jj)
            for e in range(2):
                hd = index_head(j, e)
                ch.link(eng.scalar_tensor_tensor(out=SC[:, half, :], in0=RL[:, j % 2, e, :],
                                                 scalar=KIWI[:, half, 64 + hd:65 + hd], in1=SC[:, half, :],
                                                 op0=ALU.mult, op1=ALU.add))
            eng.sem_inc(S("index_added"), 1)
        for h in range(2):
            ch.link(eng.tensor_tensor(SC[:, h, :], SC[:, h, :], const(f"causal_{h}"), ALU.add))
        for r in range(8):
            for h in range(2):
                ch.add(eng.max(STAT[:, 72 + 8 * h:80 + 8 * h], SC[:, h, :]))
            ch.wait()
            for h in range(2):
                ch.add(eng.match_replace(SC[:, h, :], STAT[:, 72 + 8 * h:80 + 8 * h], SC[:, h, :], -3e38))
            ch.wait()
        ch.link(eng.tensor_scalar(BIAS[:, :, :], SC[:, :, :], -2e38, -1e30, ALU.is_ge, ALU.mult))
        for h in range(2):
            ch.add(eng.tensor_tensor(BIAS[:, h, :], BIAS[:, h, :], const(f"causal_{h}"), ALU.min))
        ch.wait()
        softmax_rows("dsa", 8, SP, 128.0 ** -0.5, BIAS)

        def mix(t, name, tile0, ntiles, rows=P, mu=None):
            d = TMPX[0:rows, 0:ntiles, :]
            x = t[0:rows, tile0:tile0 + ntiles, :]
            ch.add(eng.tensor_tensor(d[:, :, 1:T], x[:, :, 0:T - 1], x[:, :, 1:T], ALU.subtract))
            ch.link(eng.tensor_scalar(d[:, :, 0:1], x[:, :, 0:1], -1.0, None, ALU.mult))
            for f in range(ntiles):
                ch.add(eng.scalar_tensor_tensor(out=x[:, f, :], in0=d[:, f, :], scalar=mu(f)[0:rows, :],
                                                in1=x[:, f, :], op0=ALU.mult, op1=ALU.add))
            ch.wait()

        TMPX = KK
        jobs_out(eng, "dsa_o7")
        jobs_out(eng, "loraT")
        mix(LT, "lora", 0, 2, mu=lambda f: cols("mu_lora", f))
        mix(LT, "lora", 2, 1, 32, mu=lambda f: cols("mu_lora", 2))
        ch.done("lora_mixed")
        for t, name in ((VTR, "mu_v"), (KTR, "mu_k"), (RTT, "mu_r")):
            mix(t, name, 0, 8, mu=lambda f: cols(name, f))
            ch.done("mixed")

        def tt(o, x, y, op):
            ch.link(eng.tensor_tensor(o[:, :, :], x[:, :, :], y[:, :, :], op))

        for f in range(8):
            ch.add(eng.tensor_scalar(KK[:, f, :], KTR[:, f, :], cols("k_k_2", f), None, ALU.mult))
        ch.wait()
        jobs_out(eng, "rate")
        tt(TMPR, KK, KK, ALU.mult)
        ch.done("kk_squares")
        jobs_out(eng, "kknorm")
        ch.link(eng.tensor_scalar(NRM[:, :, :], NRM[:, :, :], 1e-12, None, ALU.max))
        ch.link(eng.reciprocal(NRM[:, :, :], NRM[:, :, :]))
        tt(KK, KK, NRM, ALU.mult)
        for f in range(8):
            ch.add(eng.tensor_scalar(TMPR[:, f, :], AT[:, f, :], -1.0, cols("k_a_2", f), ALU.add, ALU.mult))
        ch.wait()
        ch.link(eng.scalar_tensor_tensor(out=KTR[:, :, :], in0=TMPR[:, :, :], scalar=1.0, in1=KTR[:, :, :],
                                         op0=ALU.add, op1=ALU.mult))
        for f in range(8):
            ch.add(eng.scalar_tensor_tensor(out=TMPR[:, f, :], in0=RTT[:, f, :], scalar=cols("r_k_2", f),
                                            in1=KTR[:, f, :], op0=ALU.mult, op1=ALU.mult))
        ch.done("bonus_in")
        tt(AT, KK, AT, ALU.mult)
        for f in range(8):
            ch.add(eng.tensor_tensor_scan(LG[:, f, :], const("restart"), SIG[:, f, :], 0.0, ALU.mult, ALU.add))
        ch.wait()
        tt(SIG, LG, SIG, ALU.subtract)
        ch.done("cum_ready")
        eng.wait_ge(S("inv_decay"), 1)
        tt(KTR, KTR, NRM, ALU.mult)
        tt(AT, AT, NRM, ALU.mult)
        ch.link(eng.scalar_tensor_tensor(out=KK[:, :, :], in0=KK[:, :, :], scalar=-1.0, in1=SIG[:, :, :],
                                         op0=ALU.mult, op1=ALU.mult))
        ch.done("cum_read")
        eng.wait_ge(S("decays"), 1)
        tt(RTT, RTT, LG, ALU.mult)
        ch.link(eng.tensor_copy(GE[:, :, :], LG[:, :, C - 1:T:C]))
        ch.done("scaled")
        for j in range(4):
            jj = J["bonus"] + j
            bank_full(eng, jj)
            v = VTR[:, 2 * j:2 * j + 2, :].rearrange("p a b -> p (a b)")
            free(eng.tensor_tensor(v, v, bank(jj), ALU.mult), jj)

        def collect(name, dst, mask):
            for j in range(8):
                jj = J[name] + j
                bank_full(eng, jj)
                for c in range(4):
                    r = slice(C * c, C * (c + 1))
                    ins = eng.tensor_tensor(dst[r, 4 * j:4 * j + 4, :],
                                            bank(jj)[r, :].rearrange("p (u q) -> p u q", u=4)[:, :, C * c:C * (c + 1)],
                                            const(mask)[r, :].rearrange("p (a b) -> p a b", a=1)
                                            .to_broadcast([C, 4, C]), ALU.mult)
                free(ins, jj)

        jobs_out(eng, "keyN")
        collect("Aab", AAB, "below")
        jobs_out(eng, "Aab")
        eng.sem_inc(S("a_ab_ready"), 1)
        collect("Aak", AAK, "above")
        collect("Arb", ARB, "above_eq")
        collect("Ark", ARK, "above_eq")
        eng.wait_ge(S("a_by_chunk_in"), 16)
        jobs_out(eng, "Ark")
        ch.link(eng.tensor_copy(TC[:, :, :].rearrange("p a b -> p (a b)"), const("eye32")))
        for t in range(1, C):
            prod = TMPC[:, 0:t * t].rearrange("p (s r) -> p s r", s=t)
            ch.link(eng.tensor_tensor(prod, TC[:, 0:t, 0:t], AC[:, t:t + 1, 0:t].to_broadcast([P, t, t]), ALU.mult))
            ch.link(eng.tensor_reduce(TC[:, 0:t, t:t + 1], prod, AX.X, ALU.add))
        ch.done("inverse_ready")
        eng.wait_ge(S("a_by_chunk_in"), 16)
        ch.link(eng.memset(ST[:, :, :], 0.0))
        ch.done("state_ready")
        for c in range(8):
            half, r = c // 4, slice(C * (c % 4), C * (c % 4) + C)
            for name, dst in ((f"chunkR{c}", RS), (f"chunkU{c}", U)):
                jj = J[name] + 1
                bank_full(eng, jj)
                free(eng.tensor_copy(dst[r, half, NB:2 * NB], bank(jj)[r, :]), jj)
            if c == 7:
                break
            for b in range(2):
                jj = J[f"chunkS{c}"] + b
                bank_full(eng, jj)
                for p in range(2):
                    q = slice(RN * p, RN * (p + 1))
                    dst = ST[q, 4 * b:4 * b + 4, RN * p:RN * (p + 1)]
                    src = bank(jj)[q, :].rearrange("p (f v) -> p f v", f=4)[:, :, RN * p:RN * (p + 1)]
                    ins = eng.tensor_tensor(dst, dst, src, ALU.add)
                free(ins, jj)
            jobs_out(eng, f"chunkS{c}")
            for p in range(2):
                q = slice(RN * p, RN * (p + 1))
                dst = ST[q, :, RN * p:RN * (p + 1)]
                ch.add(eng.tensor_tensor(dst, dst, GE[q, :, c:c + 1].to_broadcast([RN, 8, RN]), ALU.mult))
            ch.done("state_ready")
        eng.wait_ge(block_out, 4 + 2 * (st["delta_y"].b0 + 2))
        for j in range(4):
            jj = J["ymean"] + j
            bank_full(eng, jj)
            y = YT[:, 2 * j:2 * j + 2, :].rearrange("p a b -> p (a b)")
            free(eng.tensor_tensor(y, y, bank(jj), ALU.subtract), jj)
        jobs_out(eng, "ymean")
        eng.sem_inc(S("y_centred"), 1)
        for j in range(4):
            jj = J["yvar"] + j
            bank_full(eng, jj)
            free(eng.tensor_scalar(VAR[:, 2 * j:2 * j + 2, :].rearrange("p a b -> p (a b)"), bank(jj), 64e-5, None,
                                   ALU.add), jj)
        jobs_out(eng, "yvar")
        eng.sem_inc(S("y_var"), 1)
        eng.wait_ge(S("y_std"), 1)
        ch.link(eng.reciprocal(VAR[:, :, :], VAR[:, :, :]))
        tt(YT, YT, VAR, ALU.mult)
        for f in range(8):
            ch.add(eng.tensor_scalar(YT[:, f, :], YT[:, f, :], cols("lnx_w_2", f), cols("lnx_b_2", f), ALU.mult,
                                     ALU.add))
        ch.wait()
        tt(YT, YT, VTR, ALU.add)
        tt(XS[:, 0:8], YT, GT, ALU.mult)
        ch.done("y_delta")
        split_lo(XS[:, :, :], ACTS["mix"])

        def add_residual(buf, s, sem=None):
            def each(b):
                ch.add(eng.tensor_tensor(XN[:, b, :, :], XN[:, b, :, :], buf[:, b, :, :], ALU.add))
                if sem:
                    ch.done(sem)
            stream(s, each)
            ch.wait()

        add_residual(Y, st["mix"], "h_block")
        acts_in("memT", scale=lambda f: cols("norm_mem_2", f))
        inverse_rms(2)
        stream(st["cross_kv"])
        acts_in("x3T", scale=lambda f: cols("norm_cross_2", f))
        inverse_rms(4)
        stream(st["cross_q"])
        softmax_rows("cross", 4, CSP, 128.0 ** -0.5, None)
        split_lo(XS[:, 0:4, :], ACTS["cross_o"], XTH[:, 0:4, :], XTL[:, 0:4, :])
        add_residual(Y, st["cross_o"], "h_block")
        ch.done("h_summed")
        acts_in("x4T", scale=lambda f: cols("norm_mlp_2", f))
        inverse_rms(6)

        def square(b):
            ch.add(eng.tensor_tensor(UPN[:, b, :, :], UPN[:, b, :, :], UPN[:, b, :, :], ALU.mult))
            ch.done("hidden_squared")

        stream(st["up0"], square)
        acts_in("h0T", xh=XTH2, xl=XTL2)
        stream(st["up1"], square)
        for q in range(FF):
            add_residual(Y3, st[f"down{q}"])
            ch.done("h_summed")
            if q + 1 < FF:
                acts_in(f"h{q + 1}T", xh=XTH2, xl=XTL2)
            if q + 2 < FF:
                stream(st[f"up{q + 2}"], square)
        inverse_rms(6)
        eng.wait_ge(S("final_gain_in"), 16)
        for h in range(2):
            ch.add(eng.scalar_tensor_tensor(out=XN[:, :, h, :], in0=XN[:, :, h, :], scalar=RSTD[:, 6 + h:7 + h],
                                            in1=NFB[:, :, :], op0=ALU.mult, op1=ALU.mult))
        ch.done("out_ready")

    @block.tensor
    def _(eng):
        def chunk(s, B, par, kc, c, g, kt, nk):
            eng.wait_ge(lo_ready, g + 1)
            for k in range(4):
                t = kt + k
                if s.rows_only:
                    for m, w in enumerate((WHI, WLO)):
                        ins = eng.matmul(BANKS[:, par * 2, 0:s.n], CM[:, 4 * t:4 * t + P], w[:, c % 2, k, 0:s.n],
                                         start=(kc == 0 and k == 0 and m == 0),
                                         stop=(kc == nk - 1 and k == 3 and m == 1))
                    continue
                for h in range(2):
                    xh, xl = s.x or (XTH, XTL)
                    for m, (x, w) in enumerate(((xh, WHI), (xh, WLO), (xl, WHI))):
                        ins = eng.matmul(BANKS[:, par * 2 + h, 0:s.n], x[:, t, h * P:(h + 1) * P],
                                         w[:, c % 2, k, 0:s.n], start=(kc == 0 and k == 0 and m == 0),
                                         stop=(kc == nk - 1 and k == 3 and m == 2))
            ins.then_inc(chunk_used, 1)

        def acts_ready(s, kt):
            if s.acts == "y":
                if kt < 8:
                    copied(eng, J["yT"] + kt // 2)
                    copied(eng, J["yT"] + kt // 2 + 1)
                else:
                    eng.wait_ge(S("conv_lo"), kt // 4 - 1)
            elif s.acts:
                copied(eng, J[s.acts] + kt // 2)
                copied(eng, J[s.acts] + kt // 2 + 1)

        def stream(s):
            if s.loop:
                with eng.Fori(0, s.nblk // 2) as i:
                    for b in range(2):
                        eng.wait_ge(block_out, 2 * s.b0 + 4 * i + 2 * b + 2)
                        for kc in range(4):
                            if b == 0:
                                acts_ready(s, 4 * kc)
                            chunk(s, None, b, kc, kc, s.g0 + 8 * i + 4 * b + kc, 4 * kc, 4)
            else:
                for b in range(s.nblk):
                    eng.wait_ge(block_out, 2 * (s.b0 + b) + 2)
                    for kc in range(s.kc):
                        g = s.g0 + b * s.kc + kc
                        acts_ready(s, s.kt0(b) + 4 * kc)
                        chunk(s, None, b % 2, kc, g, g, s.kt0(b) + 4 * kc, s.kc)

        def gate_logs(pre):
            eng.wait_ge(block_out, 4 + 2 * (st[pre + "_r"].b0 + 2))
            jj = J[pre + "_rT"]
            bank_free(eng, jj)
            for h in range(2):
                ins = eng.transpose(bank(jj)[0:64, h * P:(h + 1) * P], RN2[:, h, :], ident)
            full(ins, jj)
            jobs_out(eng, pre + "_rT")
            eng.wait_ge(S("gate_w_in"), 64)
            for j in range(8):
                d, h, cb = j // 4, j // 2 % 2, j % 2
                jj = J[pre + "_z"] + j
                bank_free(eng, jj)
                full(eng.matmul(bank(jj), RT[32 * d:32 * d + 17, h * P:(h + 1) * P],
                                WG[32 * d:32 * d + 17, cb * NB:(cb + 1) * NB], start=True, stop=True), jj)

        def transposes(name, src, ready=None):
            for j in range(NJ[name]):
                if ready and j % 2 == 0:
                    eng.wait_ge(S(ready[0]), ready[1] + j // 2 + 1)
                jj = J[name] + j
                bank_free(eng, jj)
                for f in (2 * j, 2 * j + 1):
                    for h in range(2):
                        ins = eng.transpose(bank(jj)[:, (f % 2) * T + h * P:(f % 2) * T + (h + 1) * P], src(f, h), ident)
                full(ins, jj)

        eng.sem_inc(chunk_used, 2)
        eng.wait_ge(S("cond_lo"), 1)
        stream(st["ada0"])
        eng.wait_ge(block_out, 4 + 16)
        eng.wait_ge(S("ada0_bias_in"), 16)
        eng.wait_ge(S("consts_in"), 32)
        jj = J["mod0"]
        for f in range(32):
            ins = eng.matmul(bank(jj)[:, 2 * f:2 * f + 2], ADAROW[:, f * P:(f + 1) * P], const("comb", 5),
                             start=True, stop=True)
        full(ins, jj)
        eng.wait_ge(S("acts_lo"), 1)
        stream(st["ctx_kv"])
        stream(st["ctx_r"])
        eng.wait_ge(S("rank_zeroed"), 3)
        gate_logs("ctx")
        eng.wait_ge(S("ctx_la"), 1)
        for d in range(2):
            for j in range(4):
                th, cb = j // 2, j % 2
                jj = J[f"ctx_D{d}"] + j
                terms = [(th, "gt" if d == 0 else "lt")]
                if th == d:
                    terms.append((1 - d, "ones16"))
                bank_free(eng, jj)
                for n, (sh, m) in enumerate(terms):
                    ins = eng.matmul(bank(jj), const(m), LA_C[:, d, cb, sh, :], start=(n == 0),
                                     stop=(n == len(terms) - 1))
                full(ins, jj)
            eng.wait_ge(S("ctx_kd"), d + 1)
            for j in range(4):
                jj = J[f"ctx_S{d}"] + j
                bank_free(eng, jj)
                for k2 in range(2):
                    for h in range(2):
                        c0 = j * DK + k2 * P
                        v0 = j * DK
                        ins = eng.matmul(bank(jj)[:, k2 * DK:(k2 + 1) * DK],
                                         TMP_C[:, c0 // NB, h, c0 % NB:c0 % NB + P],
                                         NAT[:, 2 + v0 // NB, h, v0 % NB:v0 % NB + DK], start=(h == 0), stop=(h == 1))
                full(ins, jj)
        eng.wait_ge(S("acts_lo"), 2)
        stream(st["lat_kv"])
        stream(st["lat_r"])
        stream(st["lat_rest"])
        gate_logs("lat")
        eng.wait_ge(S("lat_la"), 1)
        for d in range(2):
            for j in range(4):
                jj = J[f"G{d}"] + j
                bank_free(eng, jj)
                for f in (2 * j, 2 * j + 1):
                    o0 = (f % 2) * T
                    la = [LA_L[:, d, f // 4, h, (f % 4) * P:(f % 4 + 1) * P] for h in range(2)]
                    o, _ = c_at["le" if d == 0 else "ones16"]
                    eng.matmul(bank(jj)[:, o0:o0 + T], la[d], CONST[:, o:o + T], start=True, stop=False,
                               skip_group_check=True)
                    ins = eng.matmul(bank(jj)[:, o0 + (1 - d) * P:o0 + (2 - d) * P], la[1 - d],
                                     const("le" if d == 0 else "ge"), start=False, stop=True, skip_group_check=True)
                full(ins, jj)
        transposes("qT", lambda f, h: NAT[:, 4 + f // 4, h, (f % 4) * P:(f % 4 + 1) * P])
        transposes("kT", lambda f, h: NAT[:, 0 + f // 4, h, (f % 4) * P:(f % 4 + 1) * P])
        jobs_out(eng, "kT")

        def scores(name, A, B):
            for j in range(2):
                jj = J[name] + j
                bank_free(eng, jj)
                for hd in (2 * j, 2 * j + 1):
                    for h in range(2):
                        for k2 in range(2):
                            o0 = (hd % 2) * T + h * P
                            ins = eng.matmul(bank(jj)[:, o0:o0 + P], A[:, 2 * hd + k2, h * P:(h + 1) * P],
                                             B[:, 2 * hd + k2, h * P:(h + 1) * P], start=(k2 == 0), stop=(k2 == 1))
                full(ins, jj)

        def plain_block(b):
            s = st["ada_plain"]
            q = 32 * (b % 4)
            eng.wait_ge(block_out, 2 * (s.b0 + b) + 2)
            for kc in range(4):
                eng.wait_ge(landed[kc], 16 * (s.ring0 // 4 + b + 1))
                for k in range(4):
                    ins = eng.matmul(BANKS[q:q + 2, ((s.b0 + b) % 2) * 2, :], CF[:, 4 * kc + k, :], RAW[:, kc, k, :],
                                     start=(kc == 0 and k == 0), stop=(kc == 3 and k == 3))
                ins.then_inc(S("plain_used"), 1)

        scores("diag", KTT, QT)
        n = 0
        for d in range(2):
            for l in range(8):
                Wn = (W0, W1)[n % 2]
                n += 1
                eng.wait_ge(S("factors"), n)
                if l < 7:
                    scores(f"level{d}_{l}", Wn, Wn)
                    plain_block(n - 1)
                    continue
                jj = J[f"level{d}_7"]
                bank_free(eng, jj)
                for hd in range(HEADS):
                    for k2 in range(2):
                        ins = eng.matmul(bank(jj)[:, hd * P:(hd + 1) * P], Wn[:, 2 * hd + k2, d * P:(d + 1) * P],
                                         Wn[:, 2 * hd + k2, (1 - d) * P:(2 - d) * P], start=(k2 == 0), stop=(k2 == 1))
                full(ins, jj)
                plain_block(n - 1)
        eng.wait_ge(S("state_factors"), 1)
        s = st["gla_o"]
        for B in range(2):
            eng.wait_ge(block_out, 2 * (s.b0 + B) + 2)
            for hd in range(HEADS):
                dst = acc(B, hd // 2)[:, (hd % 2) * DK:(hd % 2 + 1) * DK]
                terms = [(ACCD[:, hd, B, :], B), (ACCX[:, hd, 1 - B, :], 1 - B)]
                v0 = hd * DK
                for n, (sc, jh) in enumerate(terms):
                    eng.matmul(dst, sc, NAT[:, 2 + v0 // NB, jh, v0 % NB:v0 % NB + DK], start=(n == 0), stop=False)
                for d in range(2):
                    for k2 in range(2):
                        ins = eng.matmul(dst, (W0, W1)[d][:, 2 * hd + k2, B * P:(B + 1) * P], S0[:, d, hd, k2, :],
                                         start=False, stop=(d == 1 and k2 == 1))
            ins.then_inc(S("gla_o_full"), 1)
        eng.wait_ge(S("y_b"), 1)
        transposes("yT", lambda f, h: O[:, h, f // 2, (f % 2) * P:(f % 2 + 1) * P])
        transposes("p1T", lambda f, h: NAT[:, 10 + f // 4, h, (f % 4) * P:(f % 4 + 1) * P])
        transposes("p2T", lambda f, h: NAT[:, 8 + f // 4, h, (f % 4) * P:(f % 4 + 1) * P])
        def gate_bcast(name, b0):
            for j in range(4):
                b = b0 + j
                q = 32 * (b % 4)
                jj = J[name] + j
                bank_free(eng, jj)
                full(eng.matmul(bank(jj), const("comb_wide3")[q:q + 3, :], ADAR[q:q + 3, b // 4, :], start=True,
                                stop=True), jj)

        eng.wait_ge(S("plain_bias_in"), 256)
        gate_bcast("gt0", 0)
        stream(st["out_e"])
        for j in range(4):
            jj = J["mod1"] + j
            bank_free(eng, jj)
            q = 32 * j
            for f in [4 * j + k for k in range(4)] + [KT + 4 * j + k for k in range(4)]:
                ins = eng.matmul(bank(jj)[:, f:f + 1], ADAR[q:q + 3, 1 + f // KT, (f % 4) * P:(f % 4 + 1) * P],
                                 const("comb3")[q:q + 3, 0:1], start=True, stop=True)
            full(ins, jj)
        if stop == "x1":
            return

        gate_bcast("gt1", 12)

        def natural(buf):
            return lambda f, h: buf[:, f // 4, h, (f % 4) * P:(f % 4 + 1) * P]

        transposes("x1T", natural(XN), ("block_normed", 0))
        stream(st["in_o"])
        eng.wait_ge(block_out, 4 + 2 * st["pool"].b0)
        eng.wait_ge(S("pool_consts_in"), 16)
        for j in range(8):
            jj = J["zT"] + j
            bank_free(eng, jj)
            for f in (2 * j, 2 * j + 1):
                w = (2, 4, 8, 8)[f // 4]
                for h in range(2):
                    ins = eng.matmul(bank(jj)[:, (f % 2) * T:(f % 2 + 1) * T],
                                     NATO[:, f // 4, h, (f % 4) * P:(f % 4 + 1) * P], const(f"pool{w}_{h}"),
                                     start=(h == 0), stop=(h == 1))
            full(ins, jj)
        stream(st["pool"])
        transposes("pT", natural(Y), ("gated_z", 0))
        stream(st["out_o"])
        if stop == "x2":
            return

        def attention(pre, units, q_T, k_T, kv, V, SPb, PTb):
            def values(u):
                pair, half = u // 2, u % 2
                eng.wait_ge(S(pre + "_probs"), u + 1)
                jj = J[f"{pre}_p{u}"]
                bank_free(eng, jj)
                for e in range(2):
                    for sh in range(2):
                        ins = eng.transpose(bank(jj)[:, (2 * e + sh) * P:(2 * e + sh + 1) * P],
                                            SPb[:, u % 2, e, sh * P:(sh + 1) * P], ident)
                full(ins, jj)
                copied(eng, jj)
                jj = J[f"{pre}_o{u}"]
                bank_free(eng, jj)
                for e in range(2):
                    for sh in range(2):
                        ins = eng.matmul(bank(jj)[:, e * P:(e + 1) * P], V(kv(2 * pair + e), sh),
                                         PTb[:, u % 2, (2 * e + sh) * P:(2 * e + sh + 1) * P], start=(sh == 0),
                                         stop=(sh == 1))
                full(ins, jj)

            for u in range(units):
                pair, half = u // 2, u % 2
                jj = J[f"{pre}_s{u}"]
                bank_free(eng, jj)
                for e in range(2):
                    ins = eng.matmul(bank(jj)[:, e * T:(e + 1) * T], q_T[:, 2 * pair + e, half * P:(half + 1) * P],
                                     k_T[:, kv(2 * pair + e), :], start=True, stop=True)
                full(ins, jj)
                if u >= 1:
                    values(u - 1)
            values(units - 1)

        transposes("x2T", natural(XN), ("block_normed", 4))
        for n in ("rkv", "lora", "att4", "att1", "kiwi"):
            stream(st[n])
        eng.wait_ge(S("roped"), 1)
        transposes("aqT", natural(NA))
        transposes("akT", lambda f, h: NA[:, 2, h, f * P:(f + 1) * P])
        transposes("aiT", lambda f, h: NA[:, 3 + f // 4, h, (f % 4) * P:(f % 4 + 1) * P])
        jj = J["aiiT"]
        bank_free(eng, jj)
        for h in range(2):
            ins = eng.transpose(bank(jj)[:, h * P:(h + 1) * P], KI2[:, h, :], ident)
        full(ins, jj)
        jobs_out(eng, "aiiT")
        for j in range(16):
            half = j // 8
            jj = J["idx"] + j
            bank_free(eng, jj)
            for e in range(2):
                hd = index_head(j, e)
                r = slice(64 * (hd % 2), 64 * (hd % 2) + 64)
                ins = eng.matmul(bank(jj)[:, e * T:(e + 1) * T], QIT[r, hd // 2, half * P:(half + 1) * P], KIT[r, :],
                                 start=True, stop=True)
            full(ins, jj)
        attention("dsa", 8, QTA, KTA, lambda hd: hd // 4,
                  lambda g, sh: NA[:, 2, sh, 256 + g * P:256 + (g + 1) * P], SP, PT)
        transposes("rT", lambda f, h: NR[:, f // 4, h, (f % 4) * P:(f % 4 + 1) * P])
        transposes("keyT", lambda f, h: NR[:, 2 + f // 4, h, (f % 4) * P:(f % 4 + 1) * P])
        transposes("valT", lambda f, h: NR[:, 4 + f // 4, h, (f % 4) * P:(f % 4 + 1) * P])
        for j, (c0, w) in enumerate(((0, P), (P, P), (2 * P, 32))):
            jj = J["loraT"] + j
            bank_free(eng, jj)
            for h in range(2):
                ins = eng.transpose(bank(jj)[0:w, h * P:(h + 1) * P], LORA[:, h, c0:c0 + w], ident)
            full(ins, jj)
        eng.wait_ge(S("lora_acts"), 1)
        eng.wait_ge(S("ups_in"), 64)

        def feature_jobs(name, terms):
            for j in range(4):
                jj = J[name] + j
                bank_free(eng, jj)
                for f in (2 * j, 2 * j + 1):
                    for n, (lhs, rhs) in enumerate(terms):
                        ins = eng.matmul(bank(jj)[:, (f % 2) * T:(f % 2 + 1) * T], lhs(f), rhs(f), start=(n == 0),
                                         stop=(n == len(terms) - 1))
                full(ins, jj)

        feature_jobs("decay", [(lambda f: WDU[0:64, f * P:(f + 1) * P], lambda f: LT[0:64, 0, :])])
        feature_jobs("rate", [(lambda f: WDU[64:128, f * P:(f + 1) * P], lambda f: LT[64:128, 0, :])])
        feature_jobs("dgate", [(lambda f: GU[:, 0, f * P:(f + 1) * P], lambda f: LT[:, 1, :]),
                               (lambda f: GU[0:32, 1, f * P:(f + 1) * P], lambda f: LT[0:32, 2, :])])

        def token_jobs(name, src):
            for j in range(4):
                jj = J[name] + j
                bank_free(eng, jj)
                h = j // 2
                for q in range(4):
                    ins = eng.transpose(bank(jj)[:, q * P:(q + 1) * P], src[:, (j % 2) * 4 + q, h * P:(h + 1) * P],
                                        ident)
                full(ins, jj)

        eng.wait_ge(S("mixed"), 1)
        token_jobs("valN", VTR)
        eng.wait_ge(S("kk_squares"), 1)
        feature_jobs("kknorm", [(lambda f: const("head_ones"), lambda f: TMPR[:, f, :])])
        eng.wait_ge(S("bonus_in"), 1)
        feature_jobs("bonus", [(lambda f: const("head_ones"), lambda f: TMPR[:, f, :])])
        eng.wait_ge(S("scaled"), 1)
        token_jobs("bN", AT)
        token_jobs("keyN", KTR)

        def unit(half, hd):
            return half * 16 + (hd % 2) * 8 + hd // 2

        def chunk_matrices(name, A, B):
            for j in range(8):
                jj = J[name] + j
                bank_free(eng, jj)
                half, par = j // 4, j // 2 % 2
                for q in range(4):
                    f = (j % 2) * 4 + q
                    r = slice(RN * par, RN * (par + 1))
                    ins = eng.matmul(bank(jj)[:, q * P:(q + 1) * P], A[r, f, half * P:(half + 1) * P],
                                     B[r, f, half * P:(half + 1) * P], start=True, stop=True)
                full(ins, jj)

        chunk_matrices("Aab", KK, AT)
        chunk_matrices("Aak", KTR, KK)
        chunk_matrices("Arb", AT, RTT)
        chunk_matrices("Ark", KTR, RTT)
        jobs_out(eng, "Ark")
        s = st["delta_y"]
        eng.wait_ge(block_out, 2 * (s.b0 + 1) + 2)
        for c in range(8):
            half, r = c // 4, slice(C * (c % 4), C * (c % 4) + C)
            tok = slice(C * c, C * (c + 1))
            eng.wait_ge(S("state_ready"), c + 1)
            for b in range(2):
                jj = J[f"chunkR{c}"] + b
                bank_free(eng, jj)
                for q in range(4):
                    f = 4 * b + q
                    eng.matmul(bank(jj)[r, q * P:(q + 1) * P], KK[:, f, tok], ST[:, f, :], start=True, stop=True,
                               skip_group_check=True)
                    for p in range(2):
                        hd = 2 * f + p
                        ins = eng.matmul(bank(jj)[r, q * P + RN * p:q * P + RN * (p + 1)], AAK[r, unit(half, hd), :],
                                         VN[r, half, hd * RN:(hd + 1) * RN], start=False, stop=True,
                                         skip_group_check=True)
                full(ins, jj)
            if c == 0:
                eng.wait_ge(S("inverse_in"), 64)
            for b in range(2):
                copied(eng, J[f"chunkR{c}"] + b)
            for b in range(2):
                jj = J[f"chunkU{c}"] + b
                bank_free(eng, jj)
                for q in range(8):
                    hd = 8 * b + q
                    ins = eng.matmul(bank(jj)[r, q * RN:(q + 1) * RN], TT[r, unit(half, hd), :],
                                     RS[r, half, hd * RN:(hd + 1) * RN], start=True, stop=True)
                full(ins, jj)
            for f in range(8):
                eng.matmul(BANKS[:, f // 2, (f % 2) * T + C * c:(f % 2) * T + C * (c + 1)], ST[:, f, :],
                           RTT[:, f, tok], start=(c == 0 and f % 2 == 0), stop=False, skip_group_check=True)
            for b in range(2):
                copied(eng, J[f"chunkU{c}"] + b)
            if c < 7:
                for b in range(2):
                    jj = J[f"chunkS{c}"] + b
                    bank_free(eng, jj)
                    for q in range(4):
                        for p in range(2):
                            hd = 2 * (4 * b + q) + p
                            dst = bank(jj)[RN * p:RN * (p + 1), q * P + RN * p:q * P + RN * (p + 1)]
                            v = slice(hd * RN, (hd + 1) * RN)
                            eng.matmul(dst, BN[r, half, v], U[r, half, v], start=True, stop=False)
                            ins = eng.matmul(dst, KN[r, half, v], VN[r, half, v], start=False, stop=True)
                    full(ins, jj)
            for hd in range(RH):
                f, p = hd // 2, hd % 2
                dst = BANKS[RN * p:RN * (p + 1), f // 2, (f % 2) * T + C * c:(f % 2) * T + C * (c + 1)]
                v = slice(hd * RN, (hd + 1) * RN)
                eng.matmul(dst, U[r, half, v], ARB[r, unit(half, hd), :], start=False, stop=False,
                           skip_group_check=True)
                ins = eng.matmul(dst, VN[r, half, v], ARK[r, unit(half, hd), :], start=False, stop=(c == 7),
                                 skip_group_check=True)
            if c == 7:
                ins.then_inc(S("delta_y_full"), 1)
        eng.wait_ge(block_out, 4 + 2 * (s.b0 + 2))
        feature_jobs("ymean", [(lambda f: const("head_mean"), lambda f: YT[:, f, :])])
        eng.wait_ge(S("y_squares"), 1)
        feature_jobs("yvar", [(lambda f: const("head_mean"), lambda f: SQ[:, f, :])])
        eng.wait_ge(S("acts_lo"), ACTS["mix"])
        stream(st["mix"])
        eng.wait_ge(S("mem_in"), 32)
        transposes("memT", natural(MEMN))
        stream(st["cross_kv"])
        transposes("x3T", natural(XN), ("h_block", 0))
        stream(st["cross_q"])
        eng.wait_ge(block_out, 4 + 2 * st["cross_o"].b0)
        transposes("ckT", natural(CKV))
        transposes("cqT", natural(CQ))
        jobs_out(eng, "cqT")
        attention("cross", 4, CQT, CKT, lambda hd: hd, lambda g, sh: CKV[:, 1, sh, g * P:(g + 1) * P], CSP, CPT)
        eng.wait_ge(S("acts_lo"), ACTS["cross_o"])
        stream(st["cross_o"])
        transposes("x4T", natural(XN), ("h_block", 4))

        stream(st["up0"])
        transposes("h0T", natural(UPN), ("hidden_squared", 0))
        stream(st["up1"])
        for q in range(FF):
            stream(st[f"down{q}"])
            if q + 1 < FF:
                transposes(f"h{q + 1}T", natural(UPN), ("hidden_squared", 4 * (q + 1)))
            if q + 2 < FF:
                stream(st[f"up{q + 2}"])

    ctx.close()


def columns(v):
    return np.ascontiguousarray(v.reshape(-1, P).T)


def transposed(x):
    return np.ascontiguousarray(x.T.reshape(-1, P, x.shape[0]).transpose(1, 0, 2))


def kernel(**inputs):
    import concourse.bacc as bacc
    from concourse.bass_utils import run_bass_kernel_spmd as run

    v = {k: np.ascontiguousarray(x) for k, x in inputs.items()}
    mu = v["rwkv_mu_2"][0]
    col = {
        "c": v["c"][0], "c_ctx": v["c_ctx"], "conv_w0": v["conv_w"][0, 0], "conv_w1": v["conv_w"][0, 1],
        "conv_w2": v["conv_w"][0, 2], "pool_scale": v["pool_scale"][0], "norm_mix_2": v["norm_mix_2"][0],
        "norm_cross_2": v["norm_cross_2"][0], "norm_mem_2": v["norm_mem_2"][0], "norm_mlp_2": v["norm_mlp_2"][0],
        "ln_g0": v["ln_g"][0], "ln_b0": v["ln_b"][0], "ln_g1": v["ln_g"][1], "ln_b1": v["ln_b"][1],
        "mu_lora": np.concatenate([mu[3072:3360], np.zeros(96, np.float32)]),
        "mu_r": mu[0:1024], "mu_k": mu[1024:2048], "mu_v": mu[2048:3072],
    }
    for n in ("w_decay0_2", "a0_2", "k_k_2", "k_a_2", "r_k_2", "lnx_w_2", "lnx_b_2"):
        col[n] = v[n][0].reshape(-1)
    arrays = {"cols": np.concatenate([columns(col[n]) for n in COL_NAMES], 1),
              "common_consts": common_constants()[1], "gla_consts": gla_constants()[1],
              "pool_consts": pool_constants()[1], "second_consts": second_constants()[1],
              "mem": v["mem_2"], "positions": np.ascontiguousarray(v["positions_2"].reshape(2, P).T),
              "ctxT": transposed(v["ctx"][0]), "xT": transposed(v["x"][0])}
    for n in ("x", "w_ada", "b_ada", "ln_g", "ln_b", "w_in_e", "w_gate_f", "b_gate_f", "w_gate_b", "b_gate_b",
              "gla_norm_w", "w_out_e", "w_in_o", "w_pool", "w_out_o", "norm_final_2"):
        arrays[n] = v[n]
    for n in ("w_in", "w_mix_out", "w_q_cross", "w_kv_cross", "w_o_cross", "w_up", "w_down"):
        arrays[n if n != "w_in" else "w_in_2"] = v[n + "_2"]
    for n in ("w_decay_up_2", "a_up_2", "g_up_2"):
        arrays[n] = v[n]
    nc = bacc.Bacc("TRN2", target_bir_lowering=False, num_devices=1)
    args = {n: nc.dram_tensor("in_" + n, x.shape, mybir.dt.from_np(x.dtype), kind="ExternalInput").ap()
            for n, x in arrays.items()}
    for n in ("scratch_a", "scratch_t"):
        args[n] = nc.dram_tensor(n, (P, C, C), F32, kind="Internal").ap()
    out = nc.dram_tensor("out", (1, T, D), F32, kind="ExternalOutput").ap()
    build(nc, args, out, STOP)
    r = run(nc, [{"in_" + n: x for n, x in arrays.items()}], core_ids=[0])
    return r.results[0]["out"]
```

```python
from contextlib import ExitStack

import numpy as np

import concourse.bass as bass
from concourse import mybir

F32 = mybir.dt.float32
F32R = mybir.dt.float32r
I32 = mybir.dt.int32
ALU = mybir.AluOpType
ACT = mybir.ActivationFunctionType
AX = mybir.AxisListType

STOP = None
P = 128
T = 256
D = 2048
NB = 512
KT = D // P
HEADS, DK = 4, 256
ROW = 64
EPS = 1e-5
ALPHA = 4.0 ** 0.25


def packed(parts, first=0):
    at, n = {}, first
    for name, m in parts:
        at[name] = (n, m.shape[1])
        n += m.shape[1]
    return at, np.concatenate([m for _, m in parts], 1).astype(np.float32)


J_ = np.arange(P)[:, None]
I_ = np.arange(P)[None, :]


def common_constants():
    comb = np.zeros((P, 2))
    comb[[0, 1, 4], 0] = 1
    comb[[2, 3, 4], 1] = 1
    comb3 = np.stack([(J_[:, 0] % 32 == 0) | (J_[:, 0] % 32 == 2), (J_[:, 0] % 32 == 1) | (J_[:, 0] % 32 == 2)], 1)
    wide3 = np.broadcast_to((J_ % 32 == 0) | (J_ % 32 == 2), (P, P))
    return packed([("ident", (J_ == I_) * 1.0), ("comb", comb), ("comb3", comb3 * 1.0), ("comb_wide3", wide3 * 1.0)])


COMMON = P + 4 + P


def gla_constants():
    tau = 1.0 / 16.0
    parts = [("le", (J_ <= I_) * tau), ("ones16", np.full((P, P), tau)), ("ge", (J_ >= I_) * tau),
             ("gt", (J_ > I_) * tau), ("lt", (J_ < I_) * tau)]
    for d in range(2):
        for l in range(7):
            b = 1 << l
            m = (J_ // (2 * b) == I_ // (2 * b)) & (J_ // b % 2 == d) & (I_ // b % 2 == 1 - d)
            parts.append((f"mask{d}_{l}", m * 1.0))
    return packed(parts, COMMON)


def pool_constants():
    t = np.arange(T)
    parts = []
    rows = T // ROW
    for w in (2, 4, 8):
        m = np.zeros((T, T))
        for r in range(rows):
            lo, hi = max(r - w // 2, 0), min(r + w - w // 2, rows)
            for q in range(lo, hi):
                m[(q * ROW + np.arange(ROW)), (r * ROW + np.arange(ROW))] = np.float32(1.0 / (hi - lo))
        m[t, t] -= 1.0
        for h in range(2):
            parts.append((f"pool{w}_{h}", m[h * P:(h + 1) * P]))
    return packed(parts, COMMON)


C = 32
RH, RN = 16, 64


def second_constants():
    c = np.arange(C)[None, :]
    p = np.arange(P)[:, None]
    key = np.arange(T)[None, :]
    inv = 500000.0 ** (-np.arange(16, dtype=np.float32) / np.float32(16))
    parts = [("head_ones", (J_ // RN == I_ // RN) * 1.0), ("head_mean", (J_ // RN == I_ // RN) / RN),
             ("below", (c < p % C) * 1.0), ("above", (p % C < c) * 1.0), ("above_eq", (p % C <= c) * 1.0),
             ("restart", np.broadcast_to(np.arange(T) % C != 0, (P, T)) * 1.0),
             ("inv_freq", np.broadcast_to(inv, (P, 16)))]
    for h in range(2):
        parts.append((f"causal_{h}", np.where(key <= p + h * P, 0.0, -1e30)))
    parts.append(("eye32", np.broadcast_to(np.eye(C).reshape(1, -1), (P, C * C))))
    return packed(parts, COMMON)


COL_NAMES = ["c", "c_ctx", "conv_w0", "conv_w1", "conv_w2", "pool_scale", "norm_mix_2", "norm_cross_2",
             "norm_mem_2", "norm_mlp_2", "mu_r", "mu_k", "mu_v", "mu_lora", "w_decay0_2", "a0_2", "k_k_2", "k_a_2", "r_k_2",
             "lnx_w_2", "lnx_b_2", "ln_g0", "ln_b0", "ln_g1", "ln_b1"]
COL_TILES = [16, 16, 8, 8, 8, 16, 16, 16, 16, 16, 8, 8, 8, 3] + [8] * 7 + [16] * 4
COL_AT = {n: sum(COL_TILES[:k]) for k, n in enumerate(COL_NAMES)}
NCOLS = sum(COL_TILES)


class Stage:

    def __init__(self, name, view, nblk, n=NB, kc=4, loop=True, rows_only=False, dest=None, kt0=None, func=None,
                 x=None, acts=None, plain=False, scale=None, summed=False):
        self.name, self.view, self.nblk, self.n, self.kc = name, view, nblk, n, kc
        self.loop, self.rows_only, self.dest = loop, rows_only, dest
        self.kt0 = kt0 or (lambda blk: 0)
        self.func = func
        self.x, self.acts, self.plain, self.scale = x, acts, plain, scale
        self.summed = summed


def build(nc, a, out, stop=None):
    ctx = ExitStack()
    BASE = 16512

    def place(name, kb, shape, dt=F32):
        assert kb * 1024 + int(np.prod(shape[1:])) * 4 <= 207.8 * 1024, name
        return nc.alloc_sbuf_tensor_at(name, shape, dt, offset=BASE + int(kb * 1024))

    sems = {}

    def S(name):
        if name not in sems:
            sems[name] = ctx.enter_context(nc.semaphore(name))
        return sems[name]

    RAW = place("weights_raw", 0, [P, 4, 4, NB])
    WHI = place("weights_hi", 32, [P, 2, 4, NB], F32R)
    WLO = place("weights_lo", 48, [P, 2, 4, NB], F32R)
    CM = place("cond_parts", 64, [P, 192], F32R)
    TILE = place("shifted_tile", 205.5, [P, 2, T])
    RSTD = place("inverse_rms", 68.625, [P, 8])
    NORMC = place("norm_cols", 65.25, [P, 2, KT])
    STAT = place("stats", 64.75, [P, 128])
    RN2 = place("gate_rank_rows", 65.25, [P, 2, 64])
    RT = place("gate_rank_T", 65.75, [64, T])
    MODT = place("modulation_cols", 66.75, [P, 48, 2])
    COLS = place("feature_cols", 67.25, [P, NCOLS])
    CONST = place("constants", 68.75, [P, 2752])
    XTH = place("acts_hi", 79.5, [P, KT, T], F32R)
    XTL = place("acts_lo", 95.5, [P, KT, T], F32R)
    NAT = place("natural_blocks", 111.5, [P, 16, 2, NB])
    XS = place("acts_T", 111.5, [P, KT, T])
    XS2 = place("acts_T_latent", 143.5, [P, KT, T])
    S0 = place("context_states", 175.5, [P, 2, HEADS, 2, DK])
    ADAROW = place("modulation_rows", 191.5, [5, 8 * NB])
    WG = place("gate_weights", 191.5, [64, 1024])
    W0 = place("decayed_a", 191.5, [P, 8, T])
    ACCD = place("scores_diag", 199.5, [P, HEADS, 2, P])
    ACCX = place("scores_cross", 203.5, [P, HEADS, 2, P])
    LA_C = place("log_decay_ctx", 127.5, [P, 2, 2, 2, NB])
    TMP_C = place("decay_ctx", 159.5, [P, 2, 2, NB])
    LA_L = place("log_decay", 79.5, [P, 2, 2, 2, NB])
    TMP_L = place("gate_tmp", 95.5, [P, 2, 2, NB])
    GB_ = place("cum_decay_b", 95.5, [P, 8, T])
    GF_ = place("cum_decay_f", 103.5, [P, 8, T])
    W1 = place("decayed_b", 79.5, [P, 8, T])
    MTMP = place("masked_scores", 87.5, [P, 4, P])
    QT = place("q_T", 159.5, [P, 8, T])
    KTT = place("k_T", 167.5, [P, 8, T])
    O = place("gla_out", 127.5, [P, 2, HEADS, DK])
    GNW = place("gla_norm_row", 91.5, [P, DK])
    P1T = place("conv_in_T", 159.5, [P, 8, T])
    P2T = place("conv_gate_T", 167.5, [P, 8, T])
    CV = place("conv_out_T", 199.5, [P, 8, T])
    XN = place("residual", 127.5, [P, 4, 2, NB])
    Y = place("projected", 143.5, [P, 4, 2, NB])
    GTB = place("gate_bcast", 159.5, [P, 4, NB])
    CF = place("cond", 68.5, [P, KT, 2])
    ADAR = place("modulation_rows_plain", 111.5, [P, 4, NB])
    LNG = place("ln_gain_bcast", 183.5, [P, 4, NB])
    LNB = place("ln_bias_bcast", 191.5, [P, 4, NB])

    GTB1 = place("gate_bcast_1", 167.5, [P, 4, NB])
    NATO = place("pool_natural", 175.5, [P, 8, 2, NB])
    NR = place("rkv_natural", 143.5, [P, 6, 2, NB])
    NA = place("att_natural", 167.5, [P, 5, 2, NB])
    LORA = place("lora_natural", 187.5, [P, 2, 288])
    KIWI = place("index_key_natural", 189.75, [P, 2, 80])
    VA = place("att_values", 52, [P, 2, T])
    QTA = place("att_q_T", 32, [P, 8, T])
    QIT = place("index_q_T", 87.5, [P, 8, T])
    KTA = place("att_k_T", 40, [P, 2, T])
    KIT = place("index_k_T", 60, [P, T])
    SC = place("index_scores", 54, [P, 2, T])
    BIAS = place("att_bias", 42, [P, 2, T])
    RL = place("index_relu", 56, [P, 2, 2, T])
    SP = place("probs", 44, [P, 2, 2, T])
    PT = place("probs_T", 48, [P, 2, NB])
    ROPE = place("rope_angles", 203.5, [P, 8, 2, 16])
    ROT = place("rope_products", 204.5, [P, 4, 128])
    KI2 = place("index_key_twice", 206.5, [P, 2, P])
    RTT = place("r_T", 79.5, [P, 8, T])
    KTR = place("key_T", 87.5, [P, 8, T])
    VTR = place("value_T", 95.5, [P, 8, T])
    KK = place("unit_key_T", 103.5, [P, 8, T])
    WDU = place("decay_rate_up", 111.5, [P, 1024])
    TMPR = place("delta_tmp", 111.5, [P, 8, T])
    SIG = place("decay_T", 143.5, [P, 8, T])
    AT = place("rate_T", 151.5, [P, 8, T])
    GT = place("gate_T", 159.5, [P, 8, T])
    VN = place("value_nat", 175.5, [P, 2, 1024])
    LT = place("lora_T", 183.5, [P, 3, T])
    GU = place("gate_up", 191.5, [P, 2, 1024])
    NRM = place("norms_T", 191.5, [P, 8, T])
    LG = place("cum_decay_T", 199.5, [P, 8, T])
    GE = place("chunk_decay", 66.75, [P, 8, 8])
    BN = place("b_nat", 167.5, [P, 2, 1024])
    KN = place("key_nat", 183.5, [P, 2, 1024])
    AAB = place("a_ab", 191.5, [P, 32, C])
    AAK = place("a_ak", 111.5, [P, 32, C])
    ARB = place("a_rb", 115.5, [P, 32, C])
    ARK = place("a_rk", 143.5, [P, 32, C])
    TT = place("inverse_T", 147.5, [P, 32, C])
    AC = place("a_by_chunk", 195.5, [P, C, C])
    TC = place("inverse_by_chunk", 199.5, [P, C, C])
    TMPC = place("inverse_products", 203.5, [P, C * C])
    RS = place("chunk_rhs", 87.5, [P, 2, 1024])
    U = place("chunk_u", 151.5, [P, 2, 1024])
    ST = place("delta_state", 191.5, [P, 8, P])
    YT = place("delta_out_T", 167.5, [P, 8, T])
    SQ = place("delta_sq_T", 183.5, [P, 8, T])
    VAR = place("delta_var_T", 191.5, [P, 8, T])
    MEMN = place("memory_natural", 159.5, [P, 4, 2, NB])
    CQ = place("cross_q", 175.5, [P, 1, 2, NB])
    CKV = place("cross_kv", 179.5, [P, 2, 2, NB])
    CQT = place("cross_q_T", 187.5, [P, 4, T])
    CKT = place("cross_k_T", 191.5, [P, 4, T])
    CSP = place("cross_probs", 195.5, [P, 2, 2, T])
    CPT = place("cross_probs_T", 199.5, [P, 2, NB])
    UPN = place("hidden", 143.5, [P, 4, 2, NB])
    XTH2 = place("hidden_hi", 175.5, [P, KT, T], F32R)
    XTL2 = place("hidden_lo", 191.5, [P, KT, T], F32R)
    XTH3 = place("hidden_hi_odd", 111.5, [P, KT, T], F32R)
    XTL3 = place("hidden_lo_odd", 159.5, [P, KT, T], F32R)
    HIDDEN = ((XTH2, XTL2), (XTH3, XTL3))
    NFB = place("final_gain_bcast", 159.5, [P, 4, NB])

    BANKS = ctx.enter_context(nc.psum_tensor("banks", [P, 8, NB], F32))
    c_at = {}
    for f in (common_constants, gla_constants, pool_constants, second_constants):
        c_at.update(f()[0])

    def const(name, rows=P):
        o, n = c_at[name]
        return CONST[0:rows, o:o + n]

    def cols(name, f):
        return COLS[:, COL_AT[name] + f:COL_AT[name] + f + 1]

    ident = const("ident")

    def wv(w, r0, rows, c0, n):
        v = w[r0:r0 + rows, :].rearrange("(c k p) n -> c p k n", p=P, k=4)
        return lambda kc, blk: v[kc][:, :, bass.ds(c0 + blk * NB, n)]

    ada0, ada1 = a["w_ada"][0], a["w_ada"][1]
    ine = a["w_in_e"][0]
    stages = [
        Stage("ada0", wv(ada0, 0, D, 0, NB), 8, rows_only=True, dest=lambda b: ADAROW[0:4, bass.ds(b * NB, NB)]),
        Stage("ctx_kv", wv(ine, 0, D, 0, NB), 4, acts="ctx", dest=lambda b, h: NAT[:, bass.ds(b, 1), h, :]),
        Stage("ctx_r", wv(ine, 0, D, 2048, 32), 1, n=32, loop=False, dest="rank"),
        Stage("lat_kv", wv(ine, 0, D, 0, NB), 4, acts="lat", dest=lambda b, h: NAT[:, bass.ds(b, 1), h, :]),
        Stage("lat_r", wv(ine, 0, D, 2048, 32), 1, n=32, loop=False, dest="rank"),
        Stage("lat_rest", wv(ine, 0, D, 2080, NB), 12, dest=lambda b, h: NAT[:, bass.ds(b + 4, 1), h, :]),
        Stage("ada_plain", lambda kc, b: (wv(ada0, 0, D, 4096, NB)(kc, b) if b < 4 else wv(ada1, 0, D, 0, NB)(kc, b - 4)),
              16, loop=False, plain=True),
        Stage("gla_o", None, 2, loop=False),
        Stage("out_e", wv(a["w_out_e"][0], 0, D, 0, NB), 4, acts="y", dest=lambda b, h: Y[:, bass.ds(b, 1), h, :]),
        Stage("in_o", wv(a["w_in_o"][0], 0, D, 0, NB), 8, acts="x1T", dest=lambda b, h: NATO[:, bass.ds(b, 1), h, :]),
        Stage("pool", lambda kc, blk: a["w_pool"][0, blk].rearrange("(k p) n -> p k n", p=P), 4, kc=1, loop=False,
              acts="zT", kt0=lambda b: 4 * b, dest=lambda b, h: Y[:, b:b + 1, h, :]),
        Stage("out_o", wv(a["w_out_o"][0], 0, D, 0, NB), 4, acts="pT", dest=lambda b, h: Y[:, bass.ds(b, 1), h, :]),
        Stage("rkv", wv(a["w_in_2"][0], 0, D, 0, NB), 6, acts="x2T", scale=0, dest=lambda b, h: NR[:, bass.ds(b, 1), h, :]),
        Stage("lora", wv(a["w_in_2"][0], 0, D, 3072, 288), 1, n=288, loop=False, scale=0, dest=lambda b, h: LORA[:, h, :]),
        Stage("att4", wv(a["w_in_2"][0], 0, D, 3360, NB), 4, scale=0, dest=lambda b, h: NA[:, bass.ds(b, 1), h, :]),
        Stage("att1", wv(a["w_in_2"][0], 0, D, 5408, NB), 1, loop=False, scale=0, dest=lambda b, h: NA[:, 4, h, :]),
        Stage("kiwi", wv(a["w_in_2"][0], 0, D, 5920, 80), 1, n=80, loop=False, scale=0, dest=lambda b, h: KIWI[:, h, :]),
        Stage("delta_y", None, 2, loop=False),
        Stage("mix", wv(a["w_mix_out"][0], 0, D, 0, NB), 4, acts="mix", summed=True),
        Stage("cross_kv", wv(a["w_kv_cross"][0], 0, D, 0, NB), 2, acts="memT", scale=2, dest=lambda b, h: CKV[:, bass.ds(b, 1), h, :]),
        Stage("cross_q", wv(a["w_q_cross"][0], 0, D, 0, NB), 1, loop=False, acts="x3T", scale=4, dest=lambda b, h: CQ[:, 0, h, :]),
        Stage("cross_o", lambda kc, blk: a["w_o_cross"][0][:, blk * NB:(blk + 1) * NB].rearrange(
              "(k p) n -> p k n", p=P), 4, kc=1, loop=False, acts="cross_o", summed=True),
    ]

    def up(q):
        return Stage(f"up{q}", wv(a["w_up"][0], 0, D, q * D, NB), 4, func=ACT.Relu, acts="x4T", scale=6,
                     dest=lambda b, h: UPN[:, bass.ds(b, 1), h, :])

    def down(q):
        return Stage(f"down{q}", wv(a["w_down"][0], q * D, D, 0, NB), 4, x=HIDDEN[q % 2], acts=f"h{q}T", summed=True)

    FF = 4
    stages += [up(0), up(1), down(0), up(2), down(1), up(3), down(2), down(3)]
    if stop:
        stages = stages[:{"x1": 9, "x2": 12}[stop]]
    g = b = ring = 0
    st = {}
    for s in stages:
        s.g0, s.b0 = g, b
        s.ring0 = ring
        if s.view is not None:
            ring += s.nblk * s.kc
        if s.view is not None and not s.plain:
            g += s.nblk * s.kc
        s.follows_sum = b > 0 and summed
        summed = s.summed
        b += s.nblk + s.nblk % 2
        st[s.name] = s
        assert g % 4 == 0

    job_counts = [("mod0", 1), ("ctx_rT", 1), ("ctx_z", 8), ("ctx_D0", 4), ("ctx_S0", 4), ("ctx_D1", 4), ("ctx_S1", 4),
                  ("lat_rT", 1), ("lat_z", 8), ("G0", 4), ("G1", 4), ("qT", 4), ("kT", 4), ("diag", 2)]
    for d in range(2):
        for l in range(8):
            job_counts.append((f"level{d}_{l}", 2 if l < 7 else 1))
    job_counts += [("yT", 4), ("p1T", 4), ("p2T", 4), ("gt0", 4)]
    job_counts += [("mod1", 4), ("gt1", 4), ("x1T", 8), ("zT", 8), ("pT", 8)]
    job_counts += [("x2T", 8), ("aqT", 4), ("akT", 1), ("aiT", 4), ("aiiT", 1), ("idx", 16)]

    def attention_jobs(pre, units):
        out_ = []
        for u in range(units + 1):
            if u < units:
                out_.append((f"{pre}_s{u}", 1))
            if u >= 1:
                out_ += [(f"{pre}_p{u - 1}", 1), (f"{pre}_o{u - 1}", 1)]
        return out_

    job_counts += [("rT", 4), ("keyT", 4), ("valT", 4), ("loraT", 3), ("decay", 4), ("rate", 4), ("dgate", 4),
                   ("valN", 4), ("kknorm", 4), ("bonus", 4), ("bN", 4), ("keyN", 4), ("Aab", 8), ("Aak", 8),
                   ("Arb", 8), ("Ark", 8)]
    for c in range(8):
        job_counts += [(f"chunkR{c}", 2), (f"dsa_s{c}", 1), (f"chunkU{c}", 2)]
        if c > 0:
            job_counts.append((f"dsa_p{c - 1}", 1))
        if c < 7:
            job_counts.append((f"chunkS{c}", 2))
        if c > 0:
            job_counts.append((f"dsa_o{c - 1}", 1))
    job_counts += [("dsa_p7", 1), ("dsa_o7", 1)]
    job_counts += [("ymean", 4), ("yvar", 4), ("memT", 8), ("x3T", 8), ("ckT", 2), ("cqT", 2)]
    job_counts += attention_jobs("cross", 4)
    job_counts += [("x4T", 8), ("h0T", 8), ("h1T", 8), ("h2T", 8), ("h3T", 8)]
    J, n = {}, 0
    for name, k in job_counts:
        J[name] = n
        n += k
    NJ = dict(job_counts)

    def bank(j):
        return BANKS[:, 4 + j % 4, :]

    def bank_free(eng, j):
        if j >= 4:
            eng.wait_ge(S(f"side_free{j % 4}"), j // 4)

    def bank_full(eng, j):
        eng.wait_ge(S(f"side_full{j % 4}"), j // 4 + 1)

    def full(ins, j):
        ins.then_inc(S(f"side_full{j % 4}"), 1)

    def free(ins, j):
        ins.then_inc(S(f"side_free{j % 4}"), 1)

    job_order = [n for n in NJ if n in ("yT", "x1T", "zT", "pT", "x2T", "memT", "x3T", "x4T", "h0T", "h1T", "h2T", "h3T")]
    CUT = {n: sum(NJ[k] for k in job_order[:i]) for i, n in enumerate(job_order)}

    def index_head(j, e):
        return 4 * (j % 4) + 2 * e + j // 4 % 2

    def copied(eng, j):
        eng.wait_ge(S(f"side_free{j % 4}"), j // 4 + 1)

    def jobs_out(eng, name):
        last = J[name] + NJ[name]
        for q in range(4):
            k = (last - q + 3) // 4
            if k > 0:
                eng.wait_ge(S(f"side_free{q}"), k)

    class Chain:

        def __init__(self, eng, name):
            self.eng, self.sem, self.n = eng, S(name), 0

        def add(self, ins):
            ins.then_inc(self.sem, 1)
            self.n += 1

        def wait(self):
            if self.n:
                self.eng.wait_ge(self.sem, self.n)

        def link(self, ins):
            self.add(ins)
            self.wait()

        def done(self, name, k=1):
            self.wait()
            self.eng.sem_inc(S(name), k)

    landed = [S(f"chunk_landed{i}") for i in range(4)]
    hi_ready, lo_ready, chunk_used, block_out = S("hi_ready"), S("lo_ready"), S("chunk_used"), S("block_out")

    def acc(B, h):
        return BANKS[:, (B % 2) * 2 + h, :]

    ACTS = {"ctx": 0, "lat": 4, "mix": 8, "cross_o": 12}

    def mlp_streams(stream, tile_step, at, first=None):
        order = [("up", 0), ("up", 1)]
        for q in range(FF):
            order.append(("down", q))
            if q + 2 < FF:
                order.append(("up", q + 2))
        left = None
        for kind, q in order:
            after = {}
            if kind == "up":
                after = {4 * (b + 1) + at: tile_step(q, b) for b in range(3)}
            if left is not None:
                after[at] = tile_step(left, 3)
            if kind == "up" and q == 0 and first:
                after.update(first)
            left = q if kind == "up" else None
            stream(st[f"{kind}{q}"], after=after)

    block = ctx.enter_context(nc.Block())

    @block.sync
    def _(eng):
        def load(s, blk, kc, g):
            if not isinstance(g, int) or g >= 4:
                eng.wait_ge(lo_ready, g - 3)
            sl = kc if s.kc == 4 else g % 4
            eng.dma_start(RAW[:, sl, :, 0:s.n], s.view(kc, blk)).then_inc(landed[sl], 16)

        for s in stages:
            if s.view is None:
                continue
            if s.plain:
                for m in range(4 * s.nblk):
                    if m < 4:
                        eng.wait_ge(lo_ready, s.g0 - 3 + m)
                    else:
                        eng.wait_ge(S("plain_used"), m - 3)
                    eng.dma_start(RAW[:, m % 4], s.view(m % 4, m // 4)).then_inc(landed[m % 4], 16)
                eng.wait_ge(S("plain_used"), 4 * s.nblk)
            elif s.loop:
                first = 1 if s.g0 == 0 else 0
                for kc in range(4 * first):
                    load(s, 0, kc, kc)
                with eng.Fori(first, s.nblk) as i:
                    for kc in range(4):
                        load(s, i, kc, s.g0 + 4 * i + kc)
            else:
                for blk in range(s.nblk):
                    for kc in range(s.kc):
                        load(s, blk, kc, s.g0 + blk * s.kc + kc)

    def row_bcast(v):
        return v.rearrange("(a n) -> a n", a=1).to_broadcast([P, v.shape[0]])

    @block.gpsimd
    def _(eng):
        eng.dma_start(COLS[:, :], a["cols"]).then_inc(S("cols_in"), 16)
        eng.dma_start(CONST[:, 0:COMMON], a["common_consts"]).then_inc(S("consts_in"), 16)
        eng.dma_start(CONST[:, COMMON:COMMON + a["gla_consts"].shape[1]], a["gla_consts"]).then_inc(S("consts_in"), 16)
        eng.memset(RN2[:, :, :], 0.0).then_inc(S("rank_zeroed"), 1)
        eng.wait_ge(S("rank_zeroed"), 1)
        eng.memset(RN2[:, :, 16:17], 1.0).then_inc(S("rank_zeroed"), 1)
        eng.memset(RN2[:, :, 48:49], 1.0).then_inc(S("rank_zeroed"), 1)
        eng.dma_start(ADAROW[4:5, :], a["b_ada"][0:1, 0:4096]).then_inc(S("ada0_bias_in"), 16)
        eng.dma_start(XS[:, :, :], a["ctxT"]).then_inc(S("ctxT_in"), 16)
        eng.dma_start(XS2[:, :, :], a["xT"]).then_inc(S("xT_in"), 16)

        def gate_weights():
            eng.memset(WG[:, :], 0.0).then_inc(S("gate_w_zeroed"), 1)
            eng.wait_ge(S("gate_w_zeroed"), 1)
            eng.dma_start(WG[0:16, :], a["w_gate_f"][0]).then_inc(S("gate_w_in"), 16)
            eng.dma_start(WG[16:17, :], a["b_gate_f"]).then_inc(S("gate_w_in"), 16)
            eng.dma_start(WG[32:48, :], a["w_gate_b"][0]).then_inc(S("gate_w_in"), 16)
            eng.dma_start(WG[48:49, :], a["b_gate_b"]).then_inc(S("gate_w_in"), 16)

        jobs_out(eng, "mod0")
        gate_weights()
        jobs_out(eng, "kT")
        for b in range(16):
            bias = a["b_ada"][0:1, 4096 + b * NB:4096 + (b + 1) * NB] if b < 4 else \
                a["b_ada"][1:2, (b - 4) * NB:(b - 3) * NB]
            q = 32 * (b % 4) + 2
            eng.dma_start(ADAR[q:q + 1, b // 4, :], bias).then_inc(S("plain_bias_in"), 16)
        eng.wait_ge(S("gla_o_out"), 1)
        eng.dma_start(GNW[:, :], row_bcast(a["gla_norm_w"][0])).then_inc(S("gnw_in"), 16)
        eng.dma_start(LNG[:, :, :].rearrange("p a b -> p (a b)"), row_bcast(a["ln_g"][0])).then_inc(S("ln_in"), 16)
        eng.wait_ge(S("scores_read"), 1)
        eng.dma_start(LNB[:, :, :].rearrange("p a b -> p (a b)"), row_bcast(a["ln_b"][0])).then_inc(S("ln_in"), 16)
        jobs_out(eng, "p2T")
        for h in range(2):
            eng.dma_start(XN[:, :, h, :], a["x"][0, h * P:(h + 1) * P, :].rearrange("p (b n) -> p b n", n=NB))\
               .then_inc(S("x_in"), 16)
        def store():
            for h in range(2):
                eng.dma_start(out[0, h * P:(h + 1) * P, :].rearrange("p (b n) -> p b n", n=NB), XN[:, :, h, :])\
                   .then_inc(S("stored"), 16)
            eng.wait_ge(S("stored"), 32)

        def natural(dst, src, sem):
            for h in range(2):
                eng.dma_start(dst[:, :, h, :], src[h * P:(h + 1) * P, :].rearrange("p (b n) -> p b n", n=NB))\
                   .then_inc(S(sem), 16)

        def bcast(dst, v, sem):
            eng.dma_start(dst[:, :, :].rearrange("p a b -> p (a b)"), row_bcast(v)).then_inc(S(sem), 16)

        eng.dma_start(CONST[:, COMMON:COMMON + 1536], a["pool_consts"]).then_inc(S("pool_consts_in"), 16)
        if stop == "x1":
            eng.wait_ge(S("x1_done"), 1)
            store()
            return
        jobs_out(eng, "zT")
        eng.dma_start(CONST[:, COMMON:COMMON + a["second_consts"].shape[1]], a["second_consts"])\
           .then_inc(S("second_consts_in"), 16)
        bcast(LNG, a["ln_g"][1], "ln_in")
        eng.wait_ge(S("gated_z"), 4)
        bcast(LNB, a["ln_b"][1], "ln_in")
        if stop == "x2":
            eng.wait_ge(S("x2_done"), 1)
            store()
            return
        eng.wait_ge(S("x2_done"), 1)
        eng.dma_start(ROPE[:, 7, 0, 0:2].bitcast(I32), a["positions"]).then_inc(S("positions_in"), 16)
        eng.dma_start(WDU[0:64, :], a["w_decay_up_2"][0]).then_inc(S("ups_in"), 16)
        eng.dma_start(WDU[64:128, :], a["a_up_2"][0]).then_inc(S("ups_in"), 16)
        eng.dma_start(GU[:, 0, :], a["g_up_2"][0, 0:128, :]).then_inc(S("ups_in"), 16)
        eng.dma_start(GU[0:32, 1, :], a["g_up_2"][0, 128:160, :]).then_inc(S("ups_in"), 16)
        eng.wait_ge(S("a_ab_ready"), 1)
        sa = a["scratch_a"].rearrange("(u c) t s -> c t u s", c=4)
        for c in range(4):
            eng.dma_start(sa[c], AAB[C * c:C * (c + 1), :, :]).then_inc(S("a_ab_stored"), 16)
        eng.wait_ge(S("a_ab_stored"), 64)
        eng.dma_start(AC[:, :, :], a["scratch_a"]).then_inc(S("a_by_chunk_in"), 16)
        eng.wait_ge(S("inverse_ready"), 1)
        eng.dma_start(a["scratch_t"], TC[:, :, :]).then_inc(S("inverse_stored"), 16)
        eng.wait_ge(S("inverse_stored"), 16)
        sb = a["scratch_t"].rearrange("(u c) s t -> c s u t", c=4)
        for c in range(4):
            eng.dma_start(TT[C * c:C * (c + 1), :, :], sb[c]).then_inc(S("inverse_in"), 16)
        eng.wait_ge(S("y_delta"), 2)
        natural(MEMN, a["mem"][0], "mem_in")
        eng.wait_ge(S("h_summed"), 1)
        bcast(NFB, a["norm_final_2"], "final_gain_in")
        eng.wait_ge(S("out_ready"), 1)
        store()

    @block.scalar
    def _(eng):
        ch = Chain(eng, "act_steps")

        def hi(s, g0, i, c):
            sl = c % 4
            n = s.n
            eng.wait_ge(landed[sl], 16 * (s.ring0 // 4 + i + c // 4 + 1))
            eng.wait_ge(chunk_used, g0 + 4 * i + c + 1)
            eng.activation(WHI[:, c % 2, :, 0:n], RAW[:, sl, :, 0:n], ACT.Copy).then_inc(hi_ready, 1)

        def evac(s, i, par, last=False):
            if s.summed:
                return
            eng.wait_ge(chunk_used, s.g0 + s.kc * i + s.kc + 2)
            if s.rows_only:
                eng.activation(s.dest(i), BANKS[0:4, par * 2, :], ACT.Copy).then_inc(block_out, 2)
                return
            for h in range(2):
                src = BANKS[:, par * 2 + h, 0:s.n]
                if s.dest == "rank":
                    eng.activation(RN2[:, h, 0:16], src[:, 0:16], ACT.Copy).then_inc(S("rank_out"), 1)
                    eng.activation(RN2[:, h, 32:48], src[:, 16:32], ACT.Copy).then_inc(block_out, 1 if h == 0 else 3)
                else:
                    scale = 1.0 if s.scale is None else RSTD[:, s.scale + h:s.scale + h + 1]
                    eng.activation(s.dest(i, h), src, s.func or ACT.Copy, scale=scale)\
                       .then_inc(block_out, 3 if h == 1 and s.nblk % 2 else 1)

        held = []

        def stream(s, each=None, after=None, hold=False):
            after = after or {}
            if held:
                copy, then_ = held.pop(), after.get(1)
                after = after | {1: lambda: (copy(), then_ and then_())}
            if s.follows_sum and not s.summed:
                then = after.get(3)
                after = after | {3: lambda: (eng.wait_ge(block_out, 4 + 2 * s.b0), then and then())}
            if s.loop and each is None and not any(c > 3 for c in after):
                for c in range(4):
                    hi(s, s.g0, 0, c)
                    if c in after:
                        after[c]()
                if s.nblk > 2:
                    with eng.Fori(0, s.nblk // 2 - 1) as j:
                        for c in range(4, 12):
                            hi(s, s.g0, 2 * j, c)
                            if c == 5:
                                evac(s, 2 * j, 0)
                            if c == 9:
                                evac(s, 2 * j + 1, 1)
                e = s.nblk - 2
                for c in range(4, 8):
                    hi(s, s.g0, e, c)
                    if c == 5:
                        evac(s, e, 0)
            else:
                back = min(s.kc, 2)
                for c in range(s.nblk * s.kc):
                    hi(s, s.g0, 0, c)
                    b = c // s.kc - 1
                    if b >= 0 and c % s.kc == back - 1:
                        evac(s, b, b % 2)
                        if each:
                            each(b)
                    if c in after:
                        after[c]()

            def last():
                evac(s, s.nblk - 1, (s.nblk - 1) % 2)
                if each:
                    each(s.nblk - 1)

            if hold:
                held.append(last)
            else:
                last()

        def acts_out(name, scale=None, bias=None, func=None, xh=XTH, f0=0, jobs=None):
            for j in jobs or range(NJ[name]):
                jj = J[name] + j
                bank_full(eng, jj)
                if scale is None:
                    eng.activation(xh[:, f0 + 2 * j:f0 + 2 * j + 2, :].rearrange("p a b -> p (a b)"), bank(jj),
                                   func or ACT.Copy).then_inc(S("tile_hi"), 1)
                    continue
                for e in range(2):
                    f = 2 * j + e
                    ins = eng.activation(xh[:, f0 + f, :], bank(jj)[:, e * T:(e + 1) * T], func or ACT.Identity,
                                         scale=scale(f), bias=bias(f) if bias else 0.0)
                ins.then_inc(S("tile_hi"), 1)

        def silu_c():
            eng.wait_ge(S("cols_in"), 16)
            ch.link(eng.activation(STAT[:, 0:32], COLS[:, 0:32], ACT.Silu))
            src = STAT[:, 0:32].rearrange("p (v k) -> p v k", v=2)
            eng.wait_ge(S("cond_zeroed"), 1)
            ch.add(eng.activation(CM[:, 0:64].rearrange("p (k v e) -> p e v k", v=2, e=2)[:, 0], src, ACT.Copy))
            ch.add(eng.activation(CF[:, :, :].rearrange("p k v -> p v k"), src, ACT.Copy))
            ch.done("cond_hi")

        def split_hi(src, q):
            ch.add(eng.activation(XTH[:, 4 * q:4 * q + 4, :], src[:, 4 * q:4 * q + 4, :], ACT.Copy))
            ch.done("acts_hi")

        def modulate(X, col, q):
            for k in range(4 * q, 4 * q + 4):
                ch.add(eng.activation(X[:, k, :], X[:, k, :], ACT.Identity, scale=MODT[:, 16 + k, col:col + 1],
                                      bias=MODT[:, k, col:col + 1]))
            ch.wait()

        roots = [0]

        def root(v):
            roots[0] += 1
            eng.wait_ge(S("square_in"), roots[0])
            ch.add(eng.activation(v, v, ACT.Sqrt))
            ch.done("root_out")

        def gate_logs(pre, LA, TMP):
            bank_full(eng, J[pre + "_rT"])
            free(eng.activation(RT[:, :], bank(J[pre + "_rT"])[0:64, 0:T], ACT.Copy), J[pre + "_rT"])
            for j in range(8):
                d, h, cb = j // 4, j // 2 % 2, j % 2
                jj = J[pre + "_z"] + j
                bank_full(eng, jj)
                free(eng.activation(LA[:, d, cb, h, :], bank(jj), ACT.Copy), jj)
            for d in range(2):
                eng.wait_ge(S("neg_abs"), (1 if pre == "ctx" else 3) + d)
                ch.link(eng.activation(TMP[:, :, :, :], TMP[:, :, :, :], ACT.Exp))
                ch.add(eng.activation(TMP[:, :, :, :], TMP[:, :, :, :], ACT.Ln, bias=1.0))
                ch.done("log1p")

        silu_c()
        stream(st["ada0"])
        eng.wait_ge(S("ctxT_in"), 16)
        eng.wait_ge(S("mod0_ready"), 1)
        for q in range(4):
            modulate(XS, 1, q)
            split_hi(XS, q)
        eng.wait_ge(S("xT_in"), 16)
        stream(st["ctx_kv"], after={q: lambda q=q: modulate(XS2, 0, q) for q in range(4)}, hold=True)
        stream(st["ctx_r"])
        gate_logs("ctx", LA_C, TMP_C)
        for d in range(2):
            for j in range(4):
                jj = J[f"ctx_D{d}"] + j
                if j == 0:
                    if d == 0:
                        eng.wait_ge(S("ctx_la"), 1)
                    else:
                        eng.wait_ge(S("side_full%d" % ((J["ctx_S0"] + 3) % 4)), (J["ctx_S0"] + 3) // 4 + 1)
                bank_full(eng, jj)
                free(eng.activation(TMP_C[:, j % 2, j // 2, :], bank(jj), ACT.Exp), jj)
            for j in range(4):
                jj = J[f"ctx_S{d}"] + j
                bank_full(eng, jj)
                free(eng.activation(S0[:, d, j, :, :].rearrange("p a b -> p (a b)"), bank(jj), ACT.Copy), jj)
        eng.wait_ge(chunk_used, st["ctx_r"].g0 + 4 + 2)
        for q in range(4):
            split_hi(XS2, q)
        stream(st["lat_kv"], hold=True)
        stream(st["lat_r"], hold=True)

        def silu_gate(b):
            if b in (2, 3, 10, 11):
                eng.wait_ge(block_out, 4 + 2 * (st["lat_rest"].b0 + b + 1))
                ch.add(eng.activation(NAT[:, b + 4, :, :], NAT[:, b + 4, :, :], ACT.Silu))

        stream(st["lat_rest"], silu_gate)
        ch.done("silu_gates")
        gate_logs("lat", LA_L, TMP_L)
        for j in range(4):
            jj = J["G0"] + j
            bank_full(eng, jj)
            free(eng.activation(GF_[:, 2 * j:2 * j + 2, :].rearrange("p a b -> p (a b)"), bank(jj), ACT.Copy), jj)
        for j in range(4):
            jj = J["G1"] + j
            bank_full(eng, jj)
            free(eng.activation(GB_[:, 2 * j:2 * j + 2, :].rearrange("p a b -> p (a b)"), bank(jj), ACT.Copy), jj)
        eng.wait_ge(S("mixed_products"), 1)
        for j in range(4):
            jj = J["qT"] + j
            bank_full(eng, jj)
            free(eng.activation(QT[:, 2 * j:2 * j + 2, :].rearrange("p a b -> p (a b)"), bank(jj), ACT.Copy,
                                scale=DK ** -0.5), jj)
        for j in range(4):
            jj = J["kT"] + j
            bank_full(eng, jj)
            free(eng.activation(KTT[:, 2 * j:2 * j + 2, :].rearrange("p a b -> p (a b)"), bank(jj), ACT.Copy), jj)
        def plain_out(b):
            s = st["ada_plain"]
            eng.wait_ge(S("plain_used"), 4 * (b + 1))
            q = 32 * (b % 4)
            eng.activation(ADAR[q:q + 2, b // 4, :], BANKS[q:q + 2, ((s.b0 + b) % 2) * 2, :], ACT.Copy)\
               .then_inc(block_out, 2)

        for n in range(18):
            if 1 <= n < 17:
                plain_out(n - 1)
            Wn = (W0, W1)[n % 2]
            if n < 16:
                eng.wait_ge(S("decay_args"), n + 1)
                ch.add(eng.activation(Wn[:, :, :], Wn[:, :, :], ACT.Exp))
            else:
                if n == 16:
                    jobs_out(eng, "level1_6")
                else:
                    jobs_out(eng, "level1_7")
                ch.add(eng.activation(Wn[:, :, :], (GF_, GB_)[n - 16][:, :, :], ACT.Exp))
            ch.done("decay_exp")
        s = st["gla_o"]
        for B in range(2):
            eng.wait_ge(S("gla_o_full"), B + 1)
            for h in range(2):
                eng.activation(O[:, B, 2 * h:2 * h + 2, :].rearrange("p a b -> p (a b)"), acc(B, h), ACT.Copy)\
                   .then_inc(block_out, 1)
        eng.wait_ge(block_out, 4 + 2 * (s.b0 + 2))
        eng.sem_inc(S("gla_o_out"), 1)
        for h in range(2):
            for k in range(HEADS):
                ch.add(eng.activation(MTMP[:, 0:2, :].rearrange("p a b -> p (a b)"), O[:, h, k, :], ACT.Square,
                                      accum_out=STAT[:, h * 4 + k:h * 4 + k + 1]))
                ch.wait()
        ch.done("o_squares")
        root(STAT[:, 0:8])
        for name, dst in (("yT", None), ("p1T", P1T), ("p2T", P2T)):
            if dst is None:
                acts_out("yT")
                continue
            for j in range(4):
                jj = J[name] + j
                bank_full(eng, jj)
                free(eng.activation(dst[:, 2 * j:2 * j + 2, :].rearrange("p a b -> p (a b)"), bank(jj), ACT.Copy), jj)
        for q in range(2):
            eng.wait_ge(S("conv_done"), q + 1)
            ch.add(eng.activation(XTH[:, 8 + 4 * q:12 + 4 * q, :], XS[:, 8 + 4 * q:12 + 4 * q, :], ACT.Copy))
            ch.done("conv_hi")
        for j in range(4):
            jj = J["gt0"] + j
            bank_full(eng, jj)
            free(eng.activation(GTB[:, j, :], bank(jj), ACT.Copy), jj)
        stream(st["out_e"])
        root(STAT[:, 66:71:4])
        if stop == "x1":
            return

        def tiles_out(name, dst, n=T, scale=None, bias=None, func=None, f0=0):
            for j in range(NJ[name]):
                jj = J[name] + j
                bank_full(eng, jj)
                if scale is None:
                    free(eng.activation(dst[:, f0 + 2 * j:f0 + 2 * j + 2, :].rearrange("p a b -> p (a b)"), bank(jj),
                                        func or ACT.Copy), jj)
                    continue
                for e in range(2):
                    f = 2 * j + e
                    ins = eng.activation(dst[:, f0 + f, :], bank(jj)[:, e * T:(e + 1) * T], func or ACT.Identity,
                                         scale=scale(f), bias=bias(f) if bias else 0.0)
                free(ins, jj)

        def wait_jobs(*names):
            for n in names:
                jobs_out(eng, n)

        for j in range(4):
            jj = J["gt1"] + j
            bank_full(eng, jj)
            free(eng.activation(GTB1[:, j, :], bank(jj), ACT.Copy), jj)
        eng.wait_ge(S("norm_cols"), 1)
        norm_cols = dict(scale=lambda f: NORMC[:, 0, f:f + 1], bias=lambda f: NORMC[:, 1, f:f + 1])
        acts_out("x1T", **norm_cols)
        stream(st["in_o"])
        acts_out("zT")
        eng.wait_ge(block_out, 4 + 2 * st["pool"].b0)
        for q in range(4):
            ch.add(eng.activation(NATO[:, 4 + q:5 + q, :, :], NATO[:, 4 + q:5 + q, :, :], ACT.Silu))
            ch.done("silu_pool")
        stream(st["pool"])
        acts_out("pT", scale=lambda f: cols("pool_scale", f))
        stream(st["out_o"])
        root(STAT[:, 66:71:4])
        if stop == "x2":
            return

        NORMED = place("squares_scratch", 191.5, [P, 4, 2, NB])

        def rms_squares(src, c, scratch):
            for h in range(2):
                ch.link(eng.activation(scratch[:, :, h, :], src[:, :, h, :], ACT.Square,
                                       accum_out=STAT[:, 88 + h:89 + h]))
            ch.done("rms_squares")
            roots[0] += 1
            eng.wait_ge(S("square_in"), roots[0])
            ch.add(eng.activation(RSTD[:, c:c + 2], RSTD[:, c:c + 2], ACT.Sqrt))
            ch.done("root_out")
            rms_squares.n += 1
            eng.wait_ge(S("rstd_ready"), rms_squares.n)

        rms_squares.n = 0

        def attention_steps(pre, SPb, PTb, dst, f0):
            def probs_copy(u):
                jj = J[f"{pre}_p{u}"]
                if u >= 2:
                    bank_full(eng, J[f"{pre}_o{u - 2}"])
                bank_full(eng, jj)
                free(eng.activation(PTb[:, u % 2, :], bank(jj), ACT.Copy), jj)

            def out_copy(u):
                pair, half = u // 2, u % 2
                jj = J[f"{pre}_o{u}"]
                bank_full(eng, jj)
                free(eng.activation(dst[:, f0 + 2 * pair:f0 + 2 * pair + 2, half * P:(half + 1) * P],
                                    bank(jj)[:, 0:T].rearrange("p (a b) -> p a b", a=2), ACT.Copy), jj)

            def exps(u):
                eng.wait_ge(S(pre + "_shifted"), u + 1)
                for e in range(2):
                    ch.add(eng.activation(SPb[:, u % 2, e, :], SPb[:, u % 2, e, :], ACT.Exp,
                                          bias=STAT[:, 64 + 4 * (u % 2) + e:65 + 4 * (u % 2) + e],
                                          accum_out=STAT[:, 66 + 4 * (u % 2) + e:67 + 4 * (u % 2) + e]))
                ch.done(pre + "_exp")

            return exps, probs_copy, out_copy

        def softmax_rows(pre, units, SPb, PTb, dst, f0):
            exps, probs_copy, out_copy = attention_steps(pre, SPb, PTb, dst, f0)
            for u in range(units):
                exps(u)
                if u >= 1:
                    probs_copy(u - 1)
                    out_copy(u - 1)
            probs_copy(units - 1)
            out_copy(units - 1)

        eng.wait_ge(S("norm_cols"), 2)
        acts_out("x2T", **norm_cols)
        stream(st["rkv"], after={3: lambda: (eng.wait_ge(S("x2_done"), 1), rms_squares(XN, 0, Y))}, hold=True)
        def sines():
            eng.wait_ge(S("angles"), 1)
            ch.add(eng.activation(ROPE[:, 0:2, :, :], ROPE[:, 2:4, :, :], ACT.Sin))
            ch.done("sines")

        stream(st["lora"], hold=True)
        stream(st["att4"], after={3: sines}, hold=True)
        stream(st["att1"], hold=True)
        stream(st["kiwi"])
        ch.add(eng.activation(VA[:, :, :], NA[:, 2, :, 256:512], ACT.Copy))
        ch.done("att_values_kept")
        tiles_out("aqT", QTA)
        jj = J["akT"]
        bank_full(eng, jj)
        free(eng.activation(KTA[:, :, :].rearrange("p a b -> p (a b)"), bank(jj), ACT.Copy), jj)
        tiles_out("aiT", QIT)
        jj = J["aiiT"]
        bank_full(eng, jj)
        free(eng.activation(KIT[:, :], bank(jj)[:, 0:T], ACT.Copy), jj)
        for j in range(16):
            jj = J["idx"] + j
            if j >= 2:
                eng.wait_ge(S("index_added"), j - 1)
            bank_full(eng, jj)
            free(eng.activation(RL[:, j % 2, :, :].rearrange("p a b -> p (a b)"), bank(jj), ACT.Relu), jj)
        tiles_out("rT", RTT)
        tiles_out("keyT", KTR)
        tiles_out("valT", VTR)
        for j, w in enumerate((P, P, 32)):
            jj = J["loraT"] + j
            bank_full(eng, jj)
            free(eng.activation(LT[0:w, j, :], bank(jj)[0:w, 0:T], ACT.Copy), jj)
        eng.wait_ge(S("lora_mixed"), 1)
        ch.add(eng.activation(LT[0:64, 0, :], LT[0:64, 0, :], ACT.Tanh))
        ch.add(eng.activation(LT[:, 1, :], LT[:, 1, :], ACT.Sigmoid))
        ch.add(eng.activation(LT[0:32, 2, :], LT[0:32, 2, :], ACT.Sigmoid))
        ch.done("lora_acts")
        tiles_out("decay", SIG, scale=lambda f: 1.0, bias=lambda f: cols("w_decay0_2", f), func=ACT.Sigmoid)
        tiles_out("rate", AT, scale=lambda f: 1.0, bias=lambda f: cols("a0_2", f), func=ACT.Sigmoid)
        tiles_out("dgate", GT)

        def natural_out(name, dst):
            for j in range(4):
                jj = J[name] + j
                bank_full(eng, jj)
                free(eng.activation(dst[:, j // 2, (j % 2) * NB:(j % 2 + 1) * NB], bank(jj), ACT.Copy), jj)

        natural_out("valN", VN)
        tiles_out("kknorm", NRM, func=ACT.Sqrt)
        DEC = float(np.exp(-0.5))
        eng.wait_ge(S("cum_ready"), 1)
        ch.add(eng.activation(NRM[:, :, :], LG[:, :, :], ACT.Exp, scale=DEC))
        ch.add(eng.activation(SIG[:, :, :], SIG[:, :, :], ACT.Exp, scale=-DEC))
        ch.done("inv_decay")
        eng.wait_ge(S("cum_read"), 1)
        ch.wait()
        ch.add(eng.activation(LG[:, :, :], LG[:, :, :], ACT.Exp, scale=-DEC))
        ch.done("decays")
        natural_out("bN", BN)
        natural_out("keyN", KN)
        exps, probs_copy, out_copy = attention_steps("dsa", SP, PT, XS, 8)
        for c in range(8):
            half, r = c // 4, slice(C * (c % 4), C * (c % 4) + C)
            for name, dst in ((f"chunkR{c}", RS), (f"chunkU{c}", U)):
                jj = J[name]
                bank_full(eng, jj)
                free(eng.activation(dst[r, half, 0:NB], bank(jj)[r, :], ACT.Copy), jj)
            if c > 0:
                probs_copy(c - 1)
            exps(c)
            if c > 0:
                out_copy(c - 1)
        probs_copy(7)
        out_copy(7)
        wait_jobs("dsa_o7")
        s = st["delta_y"]
        eng.wait_ge(S("delta_y_full"), 1)
        for q in range(4):
            eng.activation(YT[:, 2 * q:2 * q + 2, :].rearrange("p a b -> p (a b)"), BANKS[:, q, :], ACT.Copy)\
               .then_inc(block_out, 1)
        eng.wait_ge(S("y_centred"), 1)
        ch.add(eng.activation(SQ[:, :, :], YT[:, :, :], ACT.Square))
        ch.done("y_squares")
        eng.wait_ge(S("y_var"), 1)
        ch.add(eng.activation(VAR[:, :, :], VAR[:, :, :], ACT.Sqrt))
        ch.done("y_std")
        for q in range(4):
            if q < 2:
                eng.wait_ge(S("y_delta"), q + 1)
            split_hi(XS, q)
        stream(st["mix"])
        acts_out("memT", scale=lambda f: cols("norm_mem_2", f))
        stream(st["cross_kv"], after={3: lambda: rms_squares(MEMN, 2, NORMED)})
        acts_out("x3T", scale=lambda f: cols("norm_cross_2", f))
        stream(st["cross_q"], after={3: lambda: rms_squares(XN, 4, Y)})
        tiles_out("ckT", CKT)
        tiles_out("cqT", CQT)
        softmax_rows("cross", 4, CSP, CPT, XS, 0)
        wait_jobs("cross_o3")
        split_hi(XS, 0)
        stream(st["cross_o"])
        acts_out("x4T", scale=lambda f: cols("norm_mlp_2", f))

        def hidden_out(q, b):
            return lambda: acts_out(f"h{q}T", xh=HIDDEN[q % 2][0], jobs=(2 * b, 2 * b + 1))

        mlp_streams(lambda s, after: stream(s, None, after, not s.summed), hidden_out, 3, first={3: lambda: rms_squares(XN, 6, Y)})
        eng.wait_ge(S("h_summed"), 1)
        rms_squares(XN, 6, UPN)

    @block.vector
    def _(eng):
        ch = Chain(eng, "dve_steps")

        def lo(s, g0, i, c):
            n = s.n
            eng.wait_ge(hi_ready, g0 + 4 * i + c + 1)
            eng.tensor_tensor(WLO[:, c % 2, :, 0:n], RAW[:, c % 4, :, 0:n], WHI[:, c % 2, :, 0:n].bitcast(F32),
                              ALU.subtract).then_inc(lo_ready, 1)

        held = []

        def stream(s, each=None, after=None, hold=False):
            after = after or {}
            if held:
                step, then_ = held.pop(), after.get(2)
                after = after | {2: lambda: (step(), then_ and then_())}

            def take(b):
                if s.summed:
                    eng.wait_ge(block_out, 4 + 2 * (s.b0 + b))
                    eng.wait_ge(chunk_used, s.g0 + s.kc * (b + 1) + 2)
                else:
                    eng.wait_ge(block_out, 4 + 2 * (s.b0 + b + 1))
                each(b)

            if s.loop and each is None:
                first = 1 if after else 0
                for c in range(4 * first):
                    lo(s, s.g0, 0, c)
                    if c in after:
                        after[c]()
                with eng.Fori(first, s.nblk) as i:
                    for c in range(4):
                        lo(s, s.g0, i, c)
            else:
                for c in range(s.nblk * s.kc):
                    lo(s, s.g0, 0, c)
                    b = c // s.kc - 1
                    if each and b >= 0 and c % s.kc == min(s.kc, 3) - 1:
                        take(b)
                    if c in after:
                        after[c]()
                if each and hold:
                    held.append(lambda: take(s.nblk - 1))
                elif each:
                    take(s.nblk - 1)

        def acts_in(name, scale=None, bias=None, xh=XTH, xl=XTL, f0=0, jobs=None):
            for j in jobs or range(NJ[name]):
                jj = J[name] + j
                eng.wait_ge(S("tile_hi"), CUT[name] + j + 1)
                bank_full(eng, jj)
                if scale is None:
                    both = [t[:, f0 + 2 * j:f0 + 2 * j + 2, :].rearrange("p a b -> p (a b)") for t in (xl, xh)]
                    free(eng.tensor_tensor(both[0], bank(jj), both[1].bitcast(F32), ALU.subtract), jj)
                    continue
                for e in range(2):
                    f = 2 * j + e
                    src = bank(jj)[:, e * T:(e + 1) * T]
                    if bias is None:
                        ins = eng.scalar_tensor_tensor(out=xl[:, f, :], in0=src, scalar=scale(f),
                                                       in1=xh[:, f, :].bitcast(F32), op0=ALU.mult, op1=ALU.subtract)
                    else:
                        ch.link(eng.tensor_scalar(TILE[:, e, :], src, scale(f), bias(f), ALU.mult, ALU.add))
                        ins = eng.tensor_tensor(xl[:, f, :], TILE[:, e, :], xh[:, f, :].bitcast(F32), ALU.subtract)
                free(ins, jj)

        def split_lo(src, name, groups=4):
            for q in range(groups):
                r = slice(4 * q, 4 * q + 4)
                eng.wait_ge(S("acts_hi"), ACTS[name] + q + 1)
                eng.tensor_tensor(XTL[:, r, :], src[:, r, :], XTH[:, r, :].bitcast(F32), ALU.subtract)\
                   .then_inc(S("acts_lo"), 1)

        roots = [0]

        def rsqrt(v):
            roots[0] += 1
            ch.done("square_in")
            eng.wait_ge(S("root_out"), roots[0])
            ch.link(eng.reciprocal(v, v))

        def gate_logs(pre, LA, TMP):
            jobs_out(eng, pre + "_z")
            for d in range(2):
                z = LA[:, d, :, :, :].rearrange("p a b c -> p (a b c)")
                t = TMP[:, :, :, :].rearrange("p a b c -> p (a b c)")
                ch.add(eng.scalar_tensor_tensor(out=t, in0=z, scalar=-1.0, in1=z, op0=ALU.mult, op1=ALU.min))
                ch.done("neg_abs")
                eng.wait_ge(S("log1p"), (1 if pre == "ctx" else 3) + d)
                ch.link(eng.scalar_tensor_tensor(out=z, in0=z, scalar=0.0, in1=t, op0=ALU.min, op1=ALU.subtract))
            ch.done(pre + "_la")

        eng.memset(CM[:, :].bitcast(F32), 0.0).then_inc(S("cond_zeroed"), 1)
        eng.sem_inc(block_out, 4)
        eng.wait_ge(S("cond_hi"), 1)
        e2 = CM[:, 0:64].rearrange("p (k v e) -> p e v k", v=2, e=2)
        ch.add(eng.tensor_tensor(e2[:, 1], STAT[:, 0:32].rearrange("p (v k) -> p v k", v=2), e2[:, 0].bitcast(F32),
                                 ALU.subtract))
        ch.done("cond_lo")
        stream(st["ada0"])
        jm = J["mod0"]
        bank_full(eng, jm)
        ch.add(eng.tensor_copy(MODT[:, 0:16, :].rearrange("p a b -> p (a b)"), bank(jm)[:, 0:32]))
        free(eng.tensor_scalar(MODT[:, 16:32, :].rearrange("p a b -> p (a b)"), bank(jm)[:, 32:64], 1.0, None,
                               ALU.add), jm)
        jobs_out(eng, "mod0")
        ch.done("mod0_ready")
        split_lo(XS, "ctx")
        stream(st["ctx_kv"])
        stream(st["ctx_r"])
        gate_logs("ctx", LA_C, TMP_C)
        for d in range(2):
            jobs_out(eng, f"ctx_D{d}")
            ch.add(eng.tensor_tensor(TMP_C[:, :, :, :].rearrange("p a b c -> p (a b c)"),
                                     TMP_C[:, :, :, :].rearrange("p a b c -> p (a b c)"),
                                     NAT[:, 0:2, :, :].rearrange("p a b c -> p (a b c)"), ALU.mult))
            ch.done("ctx_kd")
        split_lo(XS2, "lat")
        stream(st["lat_kv"])
        stream(st["lat_r"])

        def product(x, y):
            ch.add(eng.tensor_tensor(NAT[:, x:x + 2, :, :].rearrange("p a b c -> p (a b c)"),
                                     NAT[:, x:x + 2, :, :].rearrange("p a b c -> p (a b c)"),
                                     NAT[:, y:y + 2, :, :].rearrange("p a b c -> p (a b c)"), ALU.mult))

        stream(st["lat_rest"], lambda b: product(10, 12) if b == 9 else None)
        gate_logs("lat", LA_L, TMP_L)
        eng.wait_ge(S("silu_gates"), 1)
        product(8, 14)
        ch.done("mixed_products")
        jobs_out(eng, "kT")
        steps = [(d, l) for d in range(2) for l in range(8)]

        def pairs(t, b):
            return t[:, :, :].rearrange("p f t -> p (f t)").rearrange("p (m two b) -> p two m b", two=2, b=b)

        def args(n):
            d, l = steps[n]
            b = 1 << l
            Wv, Gv = pairs((W0, W1)[n % 2], b), pairs((GF_, GB_)[d], b)
            m = 8 * T // (2 * b)
            if n >= 2:
                dd, ll = steps[n - 2]
                jobs_out(eng, f"level{dd}_{ll}")
            if d == 0:
                ref = Gv[:, 0, :, b - 1:b].to_broadcast([P, m, b])
                ch.add(eng.tensor_tensor(Wv[:, 0], ref, Gv[:, 0], ALU.subtract))
                ch.add(eng.tensor_tensor(Wv[:, 1], Gv[:, 1], ref, ALU.subtract))
            else:
                ref = Gv[:, 1, :, 0:1].to_broadcast([P, m, b])
                ch.add(eng.tensor_tensor(Wv[:, 0], Gv[:, 0], ref, ALU.subtract))
                ch.add(eng.tensor_tensor(Wv[:, 1], ref, Gv[:, 1], ALU.subtract))
            ch.done("decay_args")

        def factors(n):
            d, l = steps[n]
            b = 1 << l
            Wv = pairs((W0, W1)[n % 2], b)
            first, second = ((KTT, QT), (QT, KTT))[d]
            eng.wait_ge(S("decay_exp"), n + 1)
            ch.add(eng.tensor_tensor(Wv[:, 0], Wv[:, 0], pairs(first, b)[:, 0], ALU.mult))
            ch.add(eng.tensor_tensor(Wv[:, 1], Wv[:, 1], pairs(second, b)[:, 1], ALU.mult))
            ch.done("factors")

        def collect(n):
            d, l = steps[n]
            name = f"level{d}_{l}"
            if l == 7:
                jj = J[name]
                bank_full(eng, jj)
                free(eng.tensor_copy(ACCX[:, :, d, :], bank(jj).rearrange("p (a b) -> p a b", a=4)), jj)
                return
            for j in range(2):
                jj = J[name] + j
                bank_full(eng, jj)
                mask = const(f"mask{d}_{l}").rearrange("p (a b) -> p a b", a=1).to_broadcast([P, 4, P])
                ch.wait()
                free(eng.tensor_tensor(MTMP[:, :, :], bank(jj).rearrange("p (a b) -> p a b", a=4), mask, ALU.mult), jj)
                eng.wait_ge(S(f"side_free{jj % 4}"), jj // 4 + 1)
                dst = ACCD[:, 2 * j:2 * j + 2, :, :].rearrange("p a b c -> p (a b c)")
                ch.link(eng.tensor_tensor(dst, dst, MTMP[:, :, :].rearrange("p a b -> p (a b)"), ALU.add))

        for j in range(2):
            jj = J["diag"] + j
            bank_full(eng, jj)
            free(eng.scalar_tensor_tensor(out=ACCD[:, 2 * j:2 * j + 2, :, :].rearrange("p a b c -> p (a b) c"),
                                          in0=bank(jj).rearrange("p (a b) -> p a b", a=4), scalar=2.0,
                                          in1=ident.rearrange("p (a b) -> p a b", a=1).to_broadcast([P, 4, P]),
                                          op0=ALU.mult, op1=ALU.mult), jj)
        jobs_out(eng, "diag")
        args(0)
        for n in range(16):
            factors(n)
            if n >= 1:
                collect(n - 1)
            if n + 1 < 16:
                args(n + 1)
        collect(15)
        for n in (16, 17):
            eng.wait_ge(S("decay_exp"), n + 1)
            Wn = (W0, W1)[n % 2]
            ch.add(eng.tensor_tensor(Wn[:, :, :], Wn[:, :, :], QT[:, :, :], ALU.mult))
            ch.wait()
        jobs_out(eng, "level1_7")
        ch.done("state_factors")
        eng.wait_ge(S("o_squares"), 1)
        ch.link(eng.tensor_scalar(STAT[:, 0:8], STAT[:, 0:8], 1.0 / DK, EPS, ALU.mult, ALU.add))
        rsqrt(STAT[:, 0:8])
        eng.wait_ge(S("gnw_in"), 16)
        for h in range(2):
            for k in range(HEADS):
                ch.link(eng.scalar_tensor_tensor(out=O[:, h, k, :], in0=O[:, h, k, :],
                                                 scalar=STAT[:, h * 4 + k:h * 4 + k + 1], in1=GNW[:, :],
                                                 op0=ALU.mult, op1=ALU.mult))
        for h in range(2):
            ch.add(eng.tensor_tensor(O[:, h, :, :].rearrange("p (c k) v -> p c (k v)", c=2),
                                     O[:, h, :, :].rearrange("p (c k) v -> p c (k v)", c=2),
                                     NAT[:, 6:8, h, :], ALU.mult))
        ch.done("y_b")
        eng.sem_inc(S("scores_read"), 1)
        acts_in("yT")
        jobs_out(eng, "p2T")
        for f in range(8):
            x4 = P1T[:, f, :].rearrange("p (r c) -> p r c", c=ROW)
            o4 = CV[:, f, :].rearrange("p (r c) -> p r c", c=ROW)
            ch.link(eng.tensor_scalar(CV[:, f, :], P1T[:, f, :], cols("conv_w1", f), None, ALU.mult))
            ch.link(eng.scalar_tensor_tensor(out=o4[:, :, 1:ROW], in0=x4[:, :, 0:ROW - 1], scalar=cols("conv_w0", f),
                                             in1=o4[:, :, 1:ROW], op0=ALU.mult, op1=ALU.add))
            ch.link(eng.scalar_tensor_tensor(out=o4[:, :, 0:ROW - 1], in0=x4[:, :, 1:ROW], scalar=cols("conv_w2", f),
                                             in1=o4[:, :, 0:ROW - 1], op0=ALU.mult, op1=ALU.add))
            ch.link(eng.tensor_tensor(XS[:, 8 + f, :], CV[:, f, :], P2T[:, f, :], ALU.mult))
            if f % 4 == 3:
                eng.sem_inc(S("conv_done"), 1)
        for q in range(2):
            eng.wait_ge(S("conv_hi"), q + 1)
            r = slice(8 + 4 * q, 12 + 4 * q)
            ch.add(eng.tensor_tensor(XTL[:, r, :], XS[:, r, :], XTH[:, r, :].bitcast(F32), ALU.subtract))
            ch.done("conv_lo")

        def residual_norm(name, s, G, natural_gain):
            jobs_out(eng, name)

            def each(b):
                for h in range(2):
                    ch.add(eng.tensor_tensor(Y[:, b, h, :], Y[:, b, h, :], G[:, b, :], ALU.mult))
                ch.wait()
                ch.link(eng.scalar_tensor_tensor(out=XN[:, b, :, :].rearrange("p b c -> p (b c)"),
                                                 in0=XN[:, b, :, :].rearrange("p b c -> p (b c)"), scalar=ALPHA,
                                                 in1=Y[:, b, :, :].rearrange("p b c -> p (b c)"),
                                                 op0=ALU.mult, op1=ALU.add))
                for h in range(2):
                    ch.add(eng.bn_stats(STAT[:, h * 32 + 6 * b:h * 32 + 6 * b + 6], XN[:, b, h, :]))

            stream(s, each)
            ch.wait()
            for h in range(2):
                ch.add(eng.bn_aggr(STAT[:, 64 + 4 * h:66 + 4 * h], STAT[:, h * 32:h * 32 + 24]))
            ch.wait()
            for h in range(2):
                ch.add(eng.tensor_scalar(STAT[:, 66 + 4 * h:67 + 4 * h], STAT[:, 65 + 4 * h:66 + 4 * h], EPS, None,
                                         ALU.add))
            rsqrt(STAT[:, 66:71:4])
            for b in range(4):
                for h in range(2):
                    ch.add(eng.tensor_scalar(XN[:, b, h, :], XN[:, b, h, :], STAT[:, 64 + 4 * h:65 + 4 * h],
                                             STAT[:, 66 + 4 * h:67 + 4 * h], ALU.subtract, ALU.mult))
                ch.done("block_normed")

        def gain_bias(sem_value):
            eng.wait_ge(S("ln_in"), sem_value)
            for h in range(2):
                ch.add(eng.tensor_tensor(XN[:, :, h, :], XN[:, :, h, :], LNG[:, :, :], ALU.mult))
            ch.wait()
            for h in range(2):
                ch.add(eng.tensor_tensor(XN[:, :, h, :], XN[:, :, h, :], LNB[:, :, :], ALU.add))

        norm_cols = dict(scale=lambda f: NORMC[:, 0, f:f + 1], bias=lambda f: NORMC[:, 1, f:f + 1])
        eng.wait_ge(S("x_in"), 32)
        residual_norm("gt0", st["out_e"], GTB, None)
        g0, b0 = COL_AT["ln_g0"], COL_AT["ln_b0"]
        for j in range(4):
            jm = J["mod1"] + j
            bank_full(eng, jm)
            sh, sc = slice(4 * j, 4 * j + 4), slice(KT + 4 * j, KT + 4 * j + 4)
            ch.add(eng.tensor_copy(MODT[:, sh, 0:1].rearrange("p a b -> p (a b)"), bank(jm)[:, sh]))
            free(eng.tensor_scalar(MODT[:, sc, 0:1].rearrange("p a b -> p (a b)"), bank(jm)[:, sc], 1.0, None,
                                   ALU.add), jm)
        jobs_out(eng, "mod1")
        ch.wait()
        sc1 = MODT[:, 16:32, 0:1].rearrange("p a b -> p (a b)")
        ch.add(eng.tensor_tensor(NORMC[:, 0, :], COLS[:, g0:g0 + KT], sc1, ALU.mult))
        ch.link(eng.tensor_tensor(NORMC[:, 1, :], COLS[:, b0:b0 + KT], sc1, ALU.mult))
        ch.add(eng.tensor_tensor(NORMC[:, 1, :], NORMC[:, 1, :], MODT[:, 0:16, 0:1].rearrange("p a b -> p (a b)"),
                                 ALU.add))
        ch.done("norm_cols")
        if stop == "x1":
            gain_bias(32)
            ch.done("x1_done")
            return

        def flat(t):
            return t.rearrange("p a b c -> p (a b c)")

        acts_in("x1T", **norm_cols)
        stream(st["in_o"], after={1: lambda: gain_bias(32)})
        acts_in("zT")

        def gate_z(b):
            eng.wait_ge(S("silu_pool"), b + 1)
            ch.add(eng.tensor_tensor(Y[:, b, :, :], Y[:, b, :, :], NATO[:, 4 + b, :, :], ALU.mult))
            ch.done("gated_z")

        stream(st["pool"], gate_z)
        acts_in("pT", scale=lambda f: cols("pool_scale", f))
        g0, b0, m0 = COL_AT["ln_g1"], COL_AT["ln_b1"], COL_AT["norm_mix_2"]
        jobs_out(eng, "x1T")
        ch.add(eng.tensor_tensor(NORMC[:, 0, :], COLS[:, g0:g0 + KT], COLS[:, m0:m0 + KT], ALU.mult))
        ch.add(eng.tensor_tensor(NORMC[:, 1, :], COLS[:, b0:b0 + KT], COLS[:, m0:m0 + KT], ALU.mult))
        ch.done("norm_cols")
        residual_norm("gt1", st["out_o"], GTB1, None)
        if stop == "x2":
            gain_bias(64)
            ch.done("x2_done")
            return
        acts_in("x2T", **norm_cols)

        def inverse_rms(c):
            inverse_rms.n += 1
            eng.wait_ge(S("rms_squares"), inverse_rms.n)
            ch.link(eng.tensor_scalar(RSTD[:, c:c + 2], STAT[:, 88:90], 1.0 / D, EPS, ALU.mult, ALU.add))
            rsqrt(RSTD[:, c:c + 2])
            eng.sem_inc(S("rstd_ready"), 1)

        inverse_rms.n = 0

        def attention_steps(pre, SPb, scale, bias):
            def shift(u):
                half = u % 2
                m = 64 + 4 * (u % 2)
                if u >= 2:
                    bank_full(eng, J[f"{pre}_p{u - 2}"])
                jj = J[f"{pre}_s{u}"]
                bank_full(eng, jj)
                sc = bank(jj).rearrange("p (a b) -> p a b", a=2)
                if bias is None:
                    free(eng.tensor_scalar(SPb[:, u % 2], sc, scale, None, ALU.mult), jj)
                else:
                    b = bias[:, half, :].rearrange("p (a b) -> p a b", a=1).to_broadcast([P, 2, T])
                    free(eng.scalar_tensor_tensor(out=SPb[:, u % 2], in0=sc, scalar=scale, in1=b, op0=ALU.mult,
                                                  op1=ALU.add), jj)
                copied(eng, jj)
                ch.link(eng.tensor_reduce(STAT[:, m:m + 2], SPb[:, u % 2], AX.X, ALU.max))
                ch.add(eng.tensor_scalar(STAT[:, m:m + 2], STAT[:, m:m + 2], -1.0, None, ALU.mult))
                ch.done(pre + "_shifted")

            def divide(u):
                z = 66 + 4 * (u % 2)
                eng.wait_ge(S(pre + "_exp"), u + 1)
                ch.link(eng.reciprocal(STAT[:, z:z + 2], STAT[:, z:z + 2]))
                for e in range(2):
                    ch.add(eng.tensor_scalar(SPb[:, u % 2, e, :], SPb[:, u % 2, e, :], STAT[:, z + e:z + e + 1], None,
                                             ALU.mult))
                ch.done(pre + "_probs")

            return shift, divide

        def softmax_rows(pre, units, SPb, scale, bias):
            shift, divide = attention_steps(pre, SPb, scale, bias)
            for u in range(units):
                shift(u)
                divide(u)

        stream(st["rkv"], after={1: lambda: (gain_bias(64), ch.done("x2_done")), 3: lambda: inverse_rms(0)})
        stream(st["lora"])

        def angles():
            eng.wait_ge(S("positions_in"), 16)
            eng.wait_ge(S("second_consts_in"), 16)
            ch.link(eng.tensor_copy(ROPE[:, 6, 0, 0:2], ROPE[:, 7, 0, 0:2].bitcast(I32)))
            for h in range(2):
                ch.add(eng.tensor_scalar(ROPE[:, 2, h, :], const("inv_freq"), ROPE[:, 6, 0, h:h + 1], None, ALU.mult))
            ch.wait()
            magic = 1.5 * 2.0 ** 23
            ch.link(eng.tensor_scalar(ROPE[:, 4], ROPE[:, 2], float(1 / (2 * np.pi)), magic, ALU.mult, ALU.add))
            ch.link(eng.tensor_scalar(ROPE[:, 4], ROPE[:, 4], magic, None, ALU.subtract))
            for part in (-6.28125, -0.0019350051879882812, -3.019916050e-07):
                ch.link(eng.scalar_tensor_tensor(out=ROPE[:, 2], in0=ROPE[:, 4], scalar=part, in1=ROPE[:, 2],
                                                 op0=ALU.mult, op1=ALU.add))
            ch.link(eng.tensor_scalar(ROPE[:, 3], ROPE[:, 2], float(np.pi / 2), None, ALU.add))
            ch.link(eng.tensor_scalar(ROPE[:, 4], ROPE[:, 3], float(np.pi), -float(2 * np.pi), ALU.is_gt, ALU.mult))
            ch.link(eng.tensor_tensor(ROPE[:, 3], ROPE[:, 3], ROPE[:, 4], ALU.add))
            ch.add(eng.tensor_scalar(ROPE[:, 2:4], ROPE[:, 2:4], 3.1415925, -3.1415925, ALU.min, ALU.max))
            ch.done("angles")

        def rope(x, heads, width, half, step):
            sin = ROPE[:, 0, rope.h, 0:16:step].rearrange("p (a b) -> p a b", a=1).to_broadcast([P, heads, half])
            cos = ROPE[:, 1, rope.h, 0:16:step].rearrange("p (a b) -> p a b", a=1).to_broadcast([P, heads, half])
            x1, x2 = x[:, :, 0:half], x[:, :, half:2 * half]
            t = [ROT[:, k, 0:heads * half].rearrange("p (a b) -> p a b", a=heads) for k in range(4)]
            ch.add(eng.tensor_tensor(t[0], x1, cos, ALU.mult))
            ch.add(eng.tensor_tensor(t[1], x2, sin, ALU.mult))
            ch.add(eng.tensor_tensor(t[2], x2, cos, ALU.mult))
            ch.link(eng.tensor_tensor(t[3], x1, sin, ALU.mult))
            ch.add(eng.tensor_tensor(x1, t[0], t[1], ALU.subtract))
            ch.link(eng.tensor_tensor(x2, t[2], t[3], ALU.add))

        def rope_block(b):
            eng.wait_ge(S("sines"), 1)
            for h in range(2):
                rope.h = h
                if b < 2:
                    rope(NA[:, b, h, :].rearrange("p (c d) -> p c d", d=128), 4, 128, 16, 1)
                elif b == 2:
                    rope(NA[:, 2, h, 0:256].rearrange("p (c d) -> p c d", d=128), 2, 128, 16, 1)
                else:
                    rope(NA[:, b, h, :].rearrange("p (c d) -> p c d", d=64), 8, 64, 8, 2)

        stream(st["att4"], rope_block, after={3: angles}, hold=True)
        stream(st["att1"], lambda b: rope_block(4), hold=True)
        stream(st["kiwi"])
        eng.wait_ge(block_out, 4 + 2 * st["delta_y"].b0)
        for h in range(2):
            rope.h = h
            rope(KIWI[:, h, 0:64].rearrange("p (c d) -> p c d", d=64), 1, 64, 8, 2)
            for e in range(2):
                ch.add(eng.tensor_copy(KI2[:, h, e * 64:(e + 1) * 64], KIWI[:, h, 0:64]))
            ch.add(eng.tensor_scalar(KIWI[:, h, 64:80], KIWI[:, h, 64:80], 1.0 / 32.0, None, ALU.mult))
        ch.done("roped")
        ch.link(eng.memset(SC[:, :, :], 0.0))
        for j in range(16):
            half = j // 8
            jj = J["idx"] + j
            copied(eng, jj)
            for e in range(2):
                hd = index_head(j, e)
                ch.link(eng.scalar_tensor_tensor(out=SC[:, half, :], in0=RL[:, j % 2, e, :],
                                                 scalar=KIWI[:, half, 64 + hd:65 + hd], in1=SC[:, half, :],
                                                 op0=ALU.mult, op1=ALU.add))
            eng.sem_inc(S("index_added"), 1)
        for h in range(2):
            ch.link(eng.tensor_tensor(SC[:, h, :], SC[:, h, :], const(f"causal_{h}"), ALU.add))
        for r in range(8):
            for h in range(2):
                ch.add(eng.max(STAT[:, 72 + 8 * h:80 + 8 * h], SC[:, h, :]))
            ch.wait()
            for h in range(2):
                ch.add(eng.match_replace(SC[:, h, :], STAT[:, 72 + 8 * h:80 + 8 * h], SC[:, h, :], -3e38))
            ch.wait()
        ch.link(eng.tensor_scalar(BIAS[:, :, :], SC[:, :, :], -2e38, -1e30, ALU.is_ge, ALU.mult))
        for h in range(2):
            ch.add(eng.tensor_tensor(BIAS[:, h, :], BIAS[:, h, :], const(f"causal_{h}"), ALU.min))
        ch.wait()

        def mix(t, name, tile0, ntiles, rows=P, mu=None):
            d = TMPX[0:rows, 0:ntiles, :]
            x = t[0:rows, tile0:tile0 + ntiles, :]
            ch.add(eng.tensor_tensor(d[:, :, 1:T], x[:, :, 0:T - 1], x[:, :, 1:T], ALU.subtract))
            ch.link(eng.tensor_scalar(d[:, :, 0:1], x[:, :, 0:1], -1.0, None, ALU.mult))
            for f in range(ntiles):
                ch.add(eng.scalar_tensor_tensor(out=x[:, f, :], in0=d[:, f, :], scalar=mu(f)[0:rows, :],
                                                in1=x[:, f, :], op0=ALU.mult, op1=ALU.add))
            ch.wait()

        TMPX = KK
        jobs_out(eng, "loraT")
        mix(LT, "lora", 0, 2, mu=lambda f: cols("mu_lora", f))
        mix(LT, "lora", 2, 1, 32, mu=lambda f: cols("mu_lora", 2))
        ch.done("lora_mixed")
        for t, name in ((VTR, "mu_v"), (KTR, "mu_k"), (RTT, "mu_r")):
            mix(t, name, 0, 8, mu=lambda f: cols(name, f))
            ch.done("mixed")

        def tt(o, x, y, op):
            ch.link(eng.tensor_tensor(o[:, :, :], x[:, :, :], y[:, :, :], op))

        for f in range(8):
            ch.add(eng.tensor_scalar(KK[:, f, :], KTR[:, f, :], cols("k_k_2", f), None, ALU.mult))
        ch.wait()
        jobs_out(eng, "rate")
        tt(TMPR, KK, KK, ALU.mult)
        ch.done("kk_squares")
        jobs_out(eng, "kknorm")
        ch.link(eng.tensor_scalar(NRM[:, :, :], NRM[:, :, :], 1e-12, None, ALU.max))
        ch.link(eng.reciprocal(NRM[:, :, :], NRM[:, :, :]))
        tt(KK, KK, NRM, ALU.mult)
        for f in range(8):
            ch.add(eng.tensor_scalar(TMPR[:, f, :], AT[:, f, :], -1.0, cols("k_a_2", f), ALU.add, ALU.mult))
        ch.wait()
        ch.link(eng.scalar_tensor_tensor(out=KTR[:, :, :], in0=TMPR[:, :, :], scalar=1.0, in1=KTR[:, :, :],
                                         op0=ALU.add, op1=ALU.mult))
        for f in range(8):
            ch.add(eng.scalar_tensor_tensor(out=TMPR[:, f, :], in0=RTT[:, f, :], scalar=cols("r_k_2", f),
                                            in1=KTR[:, f, :], op0=ALU.mult, op1=ALU.mult))
        ch.done("bonus_in")
        tt(AT, KK, AT, ALU.mult)
        for f in range(8):
            ch.add(eng.tensor_tensor_scan(LG[:, f, :], const("restart"), SIG[:, f, :], 0.0, ALU.mult, ALU.add))
        ch.wait()
        tt(SIG, LG, SIG, ALU.subtract)
        ch.done("cum_ready")
        eng.wait_ge(S("inv_decay"), 1)
        tt(KTR, KTR, NRM, ALU.mult)
        tt(AT, AT, NRM, ALU.mult)
        ch.link(eng.scalar_tensor_tensor(out=KK[:, :, :], in0=KK[:, :, :], scalar=-1.0, in1=SIG[:, :, :],
                                         op0=ALU.mult, op1=ALU.mult))
        ch.done("cum_read")
        eng.wait_ge(S("decays"), 1)
        tt(RTT, RTT, LG, ALU.mult)
        ch.link(eng.tensor_copy(GE[:, :, :], LG[:, :, C - 1:T:C]))
        ch.done("scaled")
        for j in range(4):
            jj = J["bonus"] + j
            bank_full(eng, jj)
            v = VTR[:, 2 * j:2 * j + 2, :].rearrange("p a b -> p (a b)")
            free(eng.tensor_tensor(v, v, bank(jj), ALU.mult), jj)

        def collect(name, dst, mask):
            for j in range(8):
                jj = J[name] + j
                bank_full(eng, jj)
                for c in range(4):
                    r = slice(C * c, C * (c + 1))
                    ins = eng.tensor_tensor(dst[r, 4 * j:4 * j + 4, :],
                                            bank(jj)[r, :].rearrange("p (u q) -> p u q", u=4)[:, :, C * c:C * (c + 1)],
                                            const(mask)[r, :].rearrange("p (a b) -> p a b", a=1)
                                            .to_broadcast([C, 4, C]), ALU.mult)
                free(ins, jj)

        jobs_out(eng, "keyN")
        collect("Aab", AAB, "below")
        jobs_out(eng, "Aab")
        eng.sem_inc(S("a_ab_ready"), 1)
        collect("Aak", AAK, "above")
        collect("Arb", ARB, "above_eq")
        collect("Ark", ARK, "above_eq")
        eng.wait_ge(S("a_by_chunk_in"), 16)
        jobs_out(eng, "Ark")
        ch.link(eng.tensor_copy(TC[:, :, :].rearrange("p a b -> p (a b)"), const("eye32")))
        for t in range(1, C):
            prod = TMPC[:, 0:t * t].rearrange("p (s r) -> p s r", s=t)
            ch.link(eng.tensor_tensor(prod, TC[:, 0:t, 0:t], AC[:, t:t + 1, 0:t].to_broadcast([P, t, t]), ALU.mult))
            ch.link(eng.tensor_reduce(TC[:, 0:t, t:t + 1], prod, AX.X, ALU.add))
        ch.done("inverse_ready")
        eng.wait_ge(S("a_by_chunk_in"), 16)
        ch.link(eng.memset(ST[:, :, :], 0.0))
        ch.done("state_ready")
        shift, divide = attention_steps("dsa", SP, 128.0 ** -0.5, BIAS)
        for c in range(8):
            half, r = c // 4, slice(C * (c % 4), C * (c % 4) + C)
            for name, dst in ((f"chunkR{c}", RS), (f"chunkU{c}", U)):
                jj = J[name] + 1
                bank_full(eng, jj)
                free(eng.tensor_copy(dst[r, half, NB:2 * NB], bank(jj)[r, :]), jj)
            shift(c)
            if c == 7:
                divide(c)
                break
            for b in range(2):
                jj = J[f"chunkS{c}"] + b
                bank_full(eng, jj)
                for p in range(2):
                    q = slice(RN * p, RN * (p + 1))
                    dst = ST[q, 4 * b:4 * b + 4, RN * p:RN * (p + 1)]
                    src = bank(jj)[q, :].rearrange("p (f v) -> p f v", f=4)[:, :, RN * p:RN * (p + 1)]
                    ins = eng.tensor_tensor(dst, dst, src, ALU.add)
                free(ins, jj)
            jobs_out(eng, f"chunkS{c}")
            for p in range(2):
                q = slice(RN * p, RN * (p + 1))
                dst = ST[q, :, RN * p:RN * (p + 1)]
                ch.add(eng.tensor_tensor(dst, dst, GE[q, :, c:c + 1].to_broadcast([RN, 8, RN]), ALU.mult))
            ch.done("state_ready")
            divide(c)
        eng.wait_ge(block_out, 4 + 2 * (st["delta_y"].b0 + 2))
        for j in range(4):
            jj = J["ymean"] + j
            bank_full(eng, jj)
            y = YT[:, 2 * j:2 * j + 2, :].rearrange("p a b -> p (a b)")
            free(eng.tensor_tensor(y, y, bank(jj), ALU.subtract), jj)
        jobs_out(eng, "ymean")
        eng.sem_inc(S("y_centred"), 1)
        for j in range(4):
            jj = J["yvar"] + j
            bank_full(eng, jj)
            free(eng.tensor_scalar(VAR[:, 2 * j:2 * j + 2, :].rearrange("p a b -> p (a b)"), bank(jj), 64e-5, None,
                                   ALU.add), jj)
        jobs_out(eng, "yvar")
        eng.sem_inc(S("y_var"), 1)
        eng.wait_ge(S("y_std"), 1)
        for q in range(2):
            r = slice(4 * q, 4 * q + 4)
            ch.link(eng.reciprocal(VAR[:, r, :], VAR[:, r, :]))
            tt(YT[:, r], YT[:, r], VAR[:, r], ALU.mult)
            for f in range(4 * q, 4 * q + 4):
                ch.add(eng.tensor_scalar(YT[:, f, :], YT[:, f, :], cols("lnx_w_2", f), cols("lnx_b_2", f), ALU.mult,
                                         ALU.add))
            ch.wait()
            tt(YT[:, r], YT[:, r], VTR[:, r], ALU.add)
            tt(XS[:, r], YT[:, r], GT[:, r], ALU.mult)
            ch.done("y_delta")
        split_lo(XS, "mix")

        def sum_block(s, sem=None):
            def each(b):
                for h in range(2):
                    eng.tensor_tensor(XN[:, b, h, :], XN[:, b, h, :], BANKS[:, (b % 2) * 2 + h, :], ALU.add)\
                       .then_inc(block_out, 1)
                if sem:
                    eng.wait_ge(block_out, 4 + 2 * (s.b0 + b + 1))
                    eng.sem_inc(S(sem), 1)
            return each

        stream(st["mix"], sum_block(st["mix"], "h_block"), hold=True)
        acts_in("memT", scale=lambda f: cols("norm_mem_2", f))
        stream(st["cross_kv"], after={3: lambda: inverse_rms(2)})
        acts_in("x3T", scale=lambda f: cols("norm_cross_2", f))
        stream(st["cross_q"], after={3: lambda: inverse_rms(4)})
        softmax_rows("cross", 4, CSP, 128.0 ** -0.5, None)
        split_lo(XS, "cross_o", 1)
        stream(st["cross_o"], sum_block(st["cross_o"], "h_block"))
        acts_in("x4T", scale=lambda f: cols("norm_mlp_2", f))

        def square(b):
            ch.add(eng.tensor_tensor(UPN[:, b, :, :], UPN[:, b, :, :], UPN[:, b, :, :], ALU.mult))
            ch.done("hidden_squared")

        def hidden_in(q, b):
            return lambda: acts_in(f"h{q}T", xh=HIDDEN[q % 2][0], xl=HIDDEN[q % 2][1], jobs=(2 * b, 2 * b + 1))

        mlp_streams(lambda s, after: stream(s, sum_block(s) if s.summed else square, after, s.name != "down3"),
                    hidden_in, 3,
                    first={3: lambda: inverse_rms(6)})
        eng.wait_ge(block_out, 4 + 2 * (st["down3"].b0 + 4))
        ch.done("h_summed")
        inverse_rms(6)
        eng.wait_ge(S("final_gain_in"), 16)
        for h in range(2):
            ch.add(eng.scalar_tensor_tensor(out=XN[:, :, h, :], in0=XN[:, :, h, :], scalar=RSTD[:, 6 + h:7 + h],
                                            in1=NFB[:, :, :], op0=ALU.mult, op1=ALU.mult))
        ch.done("out_ready")

    @block.tensor
    def _(eng):
        def chunk(s, B, par, kc, c, g, kt, nk):
            eng.wait_ge(lo_ready, g + 1)
            for k in range(4):
                t = kt + k
                if s.rows_only:
                    for m, w in enumerate((WHI, WLO)):
                        ins = eng.matmul(BANKS[:, par * 2, 0:s.n], CM[:, 4 * t:4 * t + P], w[:, c % 2, k, 0:s.n],
                                         start=(kc == 0 and k == 0 and m == 0),
                                         stop=(kc == nk - 1 and k == 3 and m == 1))
                    continue
                for h in range(2):
                    xh, xl = s.x or (XTH, XTL)
                    for m, (x, w) in enumerate(((xh, WHI), (xh, WLO), (xl, WHI))):
                        ins = eng.matmul(BANKS[:, par * 2 + h, 0:s.n], x[:, t, h * P:(h + 1) * P],
                                         w[:, c % 2, k, 0:s.n], start=(kc == 0 and k == 0 and m == 0),
                                         stop=(kc == nk - 1 and k == 3 and m == 2))
            ins.then_inc(chunk_used, 1)

        def acts_ready(s, kt):
            if s.acts == "y":
                if kt < 8:
                    copied(eng, J["yT"] + kt // 2)
                    copied(eng, J["yT"] + kt // 2 + 1)
                else:
                    eng.wait_ge(S("conv_lo"), kt // 4 - 1)
            elif s.acts in ACTS:
                eng.wait_ge(S("acts_lo"), ACTS[s.acts] + kt // 4 + 1)
            elif s.acts:
                copied(eng, J[s.acts] + kt // 2)
                copied(eng, J[s.acts] + kt // 2 + 1)

        def stream(s, after=None):
            after = after or {}
            peeled = s.nblk if not s.loop else 2 * (max(after) // 8 + 1) if after else 0
            for b in range(peeled):
                eng.wait_ge(block_out, 2 * (s.b0 + b) + 2)
                for kc in range(s.kc):
                    g = s.g0 + b * s.kc + kc
                    acts_ready(s, s.kt0(b) + 4 * kc)
                    chunk(s, None, b % 2, kc, g, g, s.kt0(b) + 4 * kc, s.kc)
                    if b * s.kc + kc in after:
                        after[b * s.kc + kc]()
            if peeled < s.nblk:
                with eng.Fori(peeled // 2, s.nblk // 2) as i:
                    for b in range(2):
                        eng.wait_ge(block_out, 2 * s.b0 + 4 * i + 2 * b + 2)
                        for kc in range(4):
                            if b == 0 and not peeled:
                                acts_ready(s, 4 * kc)
                            chunk(s, None, b, kc, kc, s.g0 + 8 * i + 4 * b + kc, 4 * kc, 4)

        def gate_logs(pre):
            eng.wait_ge(block_out, 4 + 2 * (st[pre + "_r"].b0 + 2))
            jj = J[pre + "_rT"]
            bank_free(eng, jj)
            for h in range(2):
                ins = eng.transpose(bank(jj)[0:64, h * P:(h + 1) * P], RN2[:, h, :], ident)
            full(ins, jj)
            jobs_out(eng, pre + "_rT")
            eng.wait_ge(S("gate_w_in"), 64)
            for j in range(8):
                d, h, cb = j // 4, j // 2 % 2, j % 2
                jj = J[pre + "_z"] + j
                bank_free(eng, jj)
                full(eng.matmul(bank(jj), RT[32 * d:32 * d + 17, h * P:(h + 1) * P],
                                WG[32 * d:32 * d + 17, cb * NB:(cb + 1) * NB], start=True, stop=True), jj)

        def transposes(name, src, ready=None, jobs=None):
            for j in jobs or range(NJ[name]):
                if ready and j % 2 == 0:
                    eng.wait_ge(S(ready[0]), ready[1] + j // 2 + 1)
                jj = J[name] + j
                bank_free(eng, jj)
                for f in (2 * j, 2 * j + 1):
                    for h in range(2):
                        ins = eng.transpose(bank(jj)[:, (f % 2) * T + h * P:(f % 2) * T + (h + 1) * P], src(f, h), ident)
                full(ins, jj)

        eng.sem_inc(chunk_used, 2)
        eng.wait_ge(S("cond_lo"), 1)
        stream(st["ada0"])
        eng.wait_ge(block_out, 4 + 16)
        eng.wait_ge(S("ada0_bias_in"), 16)
        eng.wait_ge(S("consts_in"), 32)
        jj = J["mod0"]
        for f in range(32):
            ins = eng.matmul(bank(jj)[:, 2 * f:2 * f + 2], ADAROW[:, f * P:(f + 1) * P], const("comb", 5),
                             start=True, stop=True)
        full(ins, jj)
        stream(st["ctx_kv"])
        stream(st["ctx_r"])
        eng.wait_ge(S("rank_zeroed"), 3)
        gate_logs("ctx")
        eng.wait_ge(S("ctx_la"), 1)
        for d in range(2):
            for j in range(4):
                th, cb = j // 2, j % 2
                jj = J[f"ctx_D{d}"] + j
                terms = [(th, "gt" if d == 0 else "lt")]
                if th == d:
                    terms.append((1 - d, "ones16"))
                bank_free(eng, jj)
                for n, (sh, m) in enumerate(terms):
                    ins = eng.matmul(bank(jj), const(m), LA_C[:, d, cb, sh, :], start=(n == 0),
                                     stop=(n == len(terms) - 1))
                full(ins, jj)
            eng.wait_ge(S("ctx_kd"), d + 1)
            for j in range(4):
                jj = J[f"ctx_S{d}"] + j
                bank_free(eng, jj)
                for k2 in range(2):
                    for h in range(2):
                        c0 = j * DK + k2 * P
                        v0 = j * DK
                        ins = eng.matmul(bank(jj)[:, k2 * DK:(k2 + 1) * DK],
                                         TMP_C[:, c0 // NB, h, c0 % NB:c0 % NB + P],
                                         NAT[:, 2 + v0 // NB, h, v0 % NB:v0 % NB + DK], start=(h == 0), stop=(h == 1))
                full(ins, jj)
        stream(st["lat_kv"])
        stream(st["lat_r"])
        stream(st["lat_rest"])
        gate_logs("lat")
        eng.wait_ge(S("lat_la"), 1)
        for d in range(2):
            for j in range(4):
                jj = J[f"G{d}"] + j
                bank_free(eng, jj)
                for f in (2 * j, 2 * j + 1):
                    o0 = (f % 2) * T
                    la = [LA_L[:, d, f // 4, h, (f % 4) * P:(f % 4 + 1) * P] for h in range(2)]
                    o, _ = c_at["le" if d == 0 else "ones16"]
                    eng.matmul(bank(jj)[:, o0:o0 + T], la[d], CONST[:, o:o + T], start=True, stop=False,
                               skip_group_check=True)
                    ins = eng.matmul(bank(jj)[:, o0 + (1 - d) * P:o0 + (2 - d) * P], la[1 - d],
                                     const("le" if d == 0 else "ge"), start=False, stop=True, skip_group_check=True)
                full(ins, jj)
        transposes("qT", lambda f, h: NAT[:, 4 + f // 4, h, (f % 4) * P:(f % 4 + 1) * P])
        transposes("kT", lambda f, h: NAT[:, 0 + f // 4, h, (f % 4) * P:(f % 4 + 1) * P])
        jobs_out(eng, "kT")

        def scores(name, A, B):
            for j in range(2):
                jj = J[name] + j
                bank_free(eng, jj)
                for hd in (2 * j, 2 * j + 1):
                    for h in range(2):
                        for k2 in range(2):
                            o0 = (hd % 2) * T + h * P
                            ins = eng.matmul(bank(jj)[:, o0:o0 + P], A[:, 2 * hd + k2, h * P:(h + 1) * P],
                                             B[:, 2 * hd + k2, h * P:(h + 1) * P], start=(k2 == 0), stop=(k2 == 1))
                full(ins, jj)

        def plain_block(b):
            s = st["ada_plain"]
            q = 32 * (b % 4)
            eng.wait_ge(block_out, 2 * (s.b0 + b) + 2)
            for kc in range(4):
                eng.wait_ge(landed[kc], 16 * (s.ring0 // 4 + b + 1))
                for k in range(4):
                    ins = eng.matmul(BANKS[q:q + 2, ((s.b0 + b) % 2) * 2, :], CF[:, 4 * kc + k, :], RAW[:, kc, k, :],
                                     start=(kc == 0 and k == 0), stop=(kc == 3 and k == 3))
                ins.then_inc(S("plain_used"), 1)

        scores("diag", KTT, QT)
        n = 0
        for d in range(2):
            for l in range(8):
                Wn = (W0, W1)[n % 2]
                n += 1
                eng.wait_ge(S("factors"), n)
                if l < 7:
                    scores(f"level{d}_{l}", Wn, Wn)
                    plain_block(n - 1)
                    continue
                jj = J[f"level{d}_7"]
                bank_free(eng, jj)
                for hd in range(HEADS):
                    for k2 in range(2):
                        ins = eng.matmul(bank(jj)[:, hd * P:(hd + 1) * P], Wn[:, 2 * hd + k2, d * P:(d + 1) * P],
                                         Wn[:, 2 * hd + k2, (1 - d) * P:(2 - d) * P], start=(k2 == 0), stop=(k2 == 1))
                full(ins, jj)
                plain_block(n - 1)
        eng.wait_ge(S("state_factors"), 1)
        s = st["gla_o"]
        for B in range(2):
            eng.wait_ge(block_out, 2 * (s.b0 + B) + 2)
            for hd in range(HEADS):
                dst = acc(B, hd // 2)[:, (hd % 2) * DK:(hd % 2 + 1) * DK]
                terms = [(ACCD[:, hd, B, :], B), (ACCX[:, hd, 1 - B, :], 1 - B)]
                v0 = hd * DK
                for n, (sc, jh) in enumerate(terms):
                    eng.matmul(dst, sc, NAT[:, 2 + v0 // NB, jh, v0 % NB:v0 % NB + DK], start=(n == 0), stop=False)
                for d in range(2):
                    for k2 in range(2):
                        ins = eng.matmul(dst, (W0, W1)[d][:, 2 * hd + k2, B * P:(B + 1) * P], S0[:, d, hd, k2, :],
                                         start=False, stop=(d == 1 and k2 == 1))
            ins.then_inc(S("gla_o_full"), 1)
        eng.wait_ge(S("y_b"), 1)
        transposes("yT", lambda f, h: O[:, h, f // 2, (f % 2) * P:(f % 2 + 1) * P])
        transposes("p1T", lambda f, h: NAT[:, 10 + f // 4, h, (f % 4) * P:(f % 4 + 1) * P])
        transposes("p2T", lambda f, h: NAT[:, 8 + f // 4, h, (f % 4) * P:(f % 4 + 1) * P])
        def gate_bcast(name, b0):
            for j in range(4):
                b = b0 + j
                q = 32 * (b % 4)
                jj = J[name] + j
                bank_free(eng, jj)
                full(eng.matmul(bank(jj), const("comb_wide3")[q:q + 3, :], ADAR[q:q + 3, b // 4, :], start=True,
                                stop=True), jj)

        eng.wait_ge(S("plain_bias_in"), 256)
        gate_bcast("gt0", 0)
        stream(st["out_e"])
        for j in range(4):
            jj = J["mod1"] + j
            bank_free(eng, jj)
            q = 32 * j
            for f in [4 * j + k for k in range(4)] + [KT + 4 * j + k for k in range(4)]:
                ins = eng.matmul(bank(jj)[:, f:f + 1], ADAR[q:q + 3, 1 + f // KT, (f % 4) * P:(f % 4 + 1) * P],
                                 const("comb3")[q:q + 3, 0:1], start=True, stop=True)
            full(ins, jj)
        if stop == "x1":
            return

        gate_bcast("gt1", 12)

        def natural(buf):
            return lambda f, h: buf[:, f // 4, h, (f % 4) * P:(f % 4 + 1) * P]

        transposes("x1T", natural(XN), ("block_normed", 0))
        stream(st["in_o"])
        eng.wait_ge(block_out, 4 + 2 * (st["in_o"].b0 + 4))
        eng.wait_ge(S("pool_consts_in"), 16)
        for j in range(8):
            jj = J["zT"] + j
            bank_free(eng, jj)
            for f in (2 * j, 2 * j + 1):
                w = (2, 4, 8, 8)[f // 4]
                for h in range(2):
                    ins = eng.matmul(bank(jj)[:, (f % 2) * T:(f % 2 + 1) * T],
                                     NATO[:, f // 4, h, (f % 4) * P:(f % 4 + 1) * P], const(f"pool{w}_{h}"),
                                     start=(h == 0), stop=(h == 1))
            full(ins, jj)
        stream(st["pool"])
        transposes("pT", natural(Y), ("gated_z", 0))
        stream(st["out_o"])
        if stop == "x2":
            return

        def attention_steps(pre, q_T, k_T, kv, V, SPb, PTb):
            def scores(u):
                pair, half = u // 2, u % 2
                jj = J[f"{pre}_s{u}"]
                bank_free(eng, jj)
                for e in range(2):
                    ins = eng.matmul(bank(jj)[:, e * T:(e + 1) * T], q_T[:, 2 * pair + e, half * P:(half + 1) * P],
                                     k_T[:, kv(2 * pair + e), :], start=True, stop=True)
                full(ins, jj)

            def probs(u):
                eng.wait_ge(S(pre + "_probs"), u + 1)
                jj = J[f"{pre}_p{u}"]
                bank_free(eng, jj)
                for e in range(2):
                    for sh in range(2):
                        ins = eng.transpose(bank(jj)[:, (2 * e + sh) * P:(2 * e + sh + 1) * P],
                                            SPb[:, u % 2, e, sh * P:(sh + 1) * P], ident)
                full(ins, jj)

            def outputs(u):
                pair = u // 2
                copied(eng, J[f"{pre}_p{u}"])
                jj = J[f"{pre}_o{u}"]
                bank_free(eng, jj)
                for e in range(2):
                    for sh in range(2):
                        ins = eng.matmul(bank(jj)[:, e * P:(e + 1) * P], V(kv(2 * pair + e), sh),
                                         PTb[:, u % 2, (2 * e + sh) * P:(2 * e + sh + 1) * P], start=(sh == 0),
                                         stop=(sh == 1))
                full(ins, jj)

            return scores, probs, outputs

        def attention(pre, units, *where):
            scores_, probs, outputs = attention_steps(pre, *where)
            for u in range(units):
                scores_(u)
                if u >= 1:
                    probs(u - 1)
                    outputs(u - 1)
            probs(units - 1)
            outputs(units - 1)

        transposes("x2T", natural(XN), ("block_normed", 4))
        for n in ("rkv", "lora", "att4", "att1", "kiwi"):
            stream(st[n])
        eng.wait_ge(S("roped"), 1)
        transposes("aqT", natural(NA))
        transposes("akT", lambda f, h: NA[:, 2, h, f * P:(f + 1) * P])
        transposes("aiT", lambda f, h: NA[:, 3 + f // 4, h, (f % 4) * P:(f % 4 + 1) * P])
        jj = J["aiiT"]
        bank_free(eng, jj)
        for h in range(2):
            ins = eng.transpose(bank(jj)[:, h * P:(h + 1) * P], KI2[:, h, :], ident)
        full(ins, jj)
        jobs_out(eng, "aiiT")
        for j in range(16):
            half = j // 8
            jj = J["idx"] + j
            bank_free(eng, jj)
            for e in range(2):
                hd = index_head(j, e)
                r = slice(64 * (hd % 2), 64 * (hd % 2) + 64)
                ins = eng.matmul(bank(jj)[:, e * T:(e + 1) * T], QIT[r, hd // 2, half * P:(half + 1) * P], KIT[r, :],
                                 start=True, stop=True)
            full(ins, jj)
        transposes("rT", lambda f, h: NR[:, f // 4, h, (f % 4) * P:(f % 4 + 1) * P])
        transposes("keyT", lambda f, h: NR[:, 2 + f // 4, h, (f % 4) * P:(f % 4 + 1) * P])
        transposes("valT", lambda f, h: NR[:, 4 + f // 4, h, (f % 4) * P:(f % 4 + 1) * P])
        for j, (c0, w) in enumerate(((0, P), (P, P), (2 * P, 32))):
            jj = J["loraT"] + j
            bank_free(eng, jj)
            for h in range(2):
                ins = eng.transpose(bank(jj)[0:w, h * P:(h + 1) * P], LORA[:, h, c0:c0 + w], ident)
            full(ins, jj)
        eng.wait_ge(S("lora_acts"), 1)
        eng.wait_ge(S("ups_in"), 64)

        def feature_jobs(name, terms):
            for j in range(4):
                jj = J[name] + j
                bank_free(eng, jj)
                for f in (2 * j, 2 * j + 1):
                    for n, (lhs, rhs) in enumerate(terms):
                        ins = eng.matmul(bank(jj)[:, (f % 2) * T:(f % 2 + 1) * T], lhs(f), rhs(f), start=(n == 0),
                                         stop=(n == len(terms) - 1))
                full(ins, jj)

        feature_jobs("decay", [(lambda f: WDU[0:64, f * P:(f + 1) * P], lambda f: LT[0:64, 0, :])])
        feature_jobs("rate", [(lambda f: WDU[64:128, f * P:(f + 1) * P], lambda f: LT[64:128, 0, :])])
        feature_jobs("dgate", [(lambda f: GU[:, 0, f * P:(f + 1) * P], lambda f: LT[:, 1, :]),
                               (lambda f: GU[0:32, 1, f * P:(f + 1) * P], lambda f: LT[0:32, 2, :])])

        def token_jobs(name, src):
            for j in range(4):
                jj = J[name] + j
                bank_free(eng, jj)
                h = j // 2
                for q in range(4):
                    ins = eng.transpose(bank(jj)[:, q * P:(q + 1) * P], src[:, (j % 2) * 4 + q, h * P:(h + 1) * P],
                                        ident)
                full(ins, jj)

        eng.wait_ge(S("mixed"), 1)
        token_jobs("valN", VTR)
        eng.wait_ge(S("kk_squares"), 1)
        feature_jobs("kknorm", [(lambda f: const("head_ones"), lambda f: TMPR[:, f, :])])
        eng.wait_ge(S("bonus_in"), 1)
        feature_jobs("bonus", [(lambda f: const("head_ones"), lambda f: TMPR[:, f, :])])
        eng.wait_ge(S("scaled"), 1)
        token_jobs("bN", AT)
        token_jobs("keyN", KTR)

        def unit(half, hd):
            return half * 16 + (hd % 2) * 8 + hd // 2

        def chunk_matrices(name, A, B):
            for j in range(8):
                jj = J[name] + j
                bank_free(eng, jj)
                half, par = j // 4, j // 2 % 2
                for q in range(4):
                    f = (j % 2) * 4 + q
                    r = slice(RN * par, RN * (par + 1))
                    ins = eng.matmul(bank(jj)[:, q * P:(q + 1) * P], A[r, f, half * P:(half + 1) * P],
                                     B[r, f, half * P:(half + 1) * P], start=True, stop=True)
                full(ins, jj)

        chunk_matrices("Aab", KK, AT)
        chunk_matrices("Aak", KTR, KK)
        chunk_matrices("Arb", AT, RTT)
        chunk_matrices("Ark", KTR, RTT)
        jobs_out(eng, "Ark")
        s = st["delta_y"]
        eng.wait_ge(block_out, 2 * (s.b0 + 1) + 2)
        eng.wait_ge(S("att_values_kept"), 1)
        att_scores, att_probs, att_outputs = attention_steps(
            "dsa", QTA, KTA, lambda hd: hd // 4, lambda g, sh: VA[:, sh, g * P:(g + 1) * P], SP, PT)
        for c in range(8):
            half, r = c // 4, slice(C * (c % 4), C * (c % 4) + C)
            tok = slice(C * c, C * (c + 1))
            eng.wait_ge(S("state_ready"), c + 1)
            for b in range(2):
                jj = J[f"chunkR{c}"] + b
                bank_free(eng, jj)
                for q in range(4):
                    f = 4 * b + q
                    eng.matmul(bank(jj)[r, q * P:(q + 1) * P], KK[:, f, tok], ST[:, f, :], start=True, stop=True,
                               skip_group_check=True)
                    for p in range(2):
                        hd = 2 * f + p
                        ins = eng.matmul(bank(jj)[r, q * P + RN * p:q * P + RN * (p + 1)], AAK[r, unit(half, hd), :],
                                         VN[r, half, hd * RN:(hd + 1) * RN], start=False, stop=True,
                                         skip_group_check=True)
                full(ins, jj)
            att_scores(c)
            if c == 0:
                eng.wait_ge(S("inverse_in"), 64)
            for b in range(2):
                copied(eng, J[f"chunkR{c}"] + b)
            for b in range(2):
                jj = J[f"chunkU{c}"] + b
                bank_free(eng, jj)
                for q in range(8):
                    hd = 8 * b + q
                    ins = eng.matmul(bank(jj)[r, q * RN:(q + 1) * RN], TT[r, unit(half, hd), :],
                                     RS[r, half, hd * RN:(hd + 1) * RN], start=True, stop=True)
                full(ins, jj)
            for f in range(8):
                eng.matmul(BANKS[:, f // 2, (f % 2) * T + C * c:(f % 2) * T + C * (c + 1)], ST[:, f, :],
                           RTT[:, f, tok], start=(c == 0 and f % 2 == 0), stop=False, skip_group_check=True)
            if c > 0:
                att_probs(c - 1)
            for b in range(2):
                copied(eng, J[f"chunkU{c}"] + b)
            if c < 7:
                for b in range(2):
                    jj = J[f"chunkS{c}"] + b
                    bank_free(eng, jj)
                    for q in range(4):
                        for p in range(2):
                            hd = 2 * (4 * b + q) + p
                            dst = bank(jj)[RN * p:RN * (p + 1), q * P + RN * p:q * P + RN * (p + 1)]
                            v = slice(hd * RN, (hd + 1) * RN)
                            eng.matmul(dst, BN[r, half, v], U[r, half, v], start=True, stop=False)
                            ins = eng.matmul(dst, KN[r, half, v], VN[r, half, v], start=False, stop=True)
                    full(ins, jj)
            for hd in range(RH):
                f, p = hd // 2, hd % 2
                dst = BANKS[RN * p:RN * (p + 1), f // 2, (f % 2) * T + C * c:(f % 2) * T + C * (c + 1)]
                v = slice(hd * RN, (hd + 1) * RN)
                eng.matmul(dst, U[r, half, v], ARB[r, unit(half, hd), :], start=False, stop=False,
                           skip_group_check=True)
                ins = eng.matmul(dst, VN[r, half, v], ARK[r, unit(half, hd), :], start=False, stop=(c == 7),
                                 skip_group_check=True)
            if c == 7:
                ins.then_inc(S("delta_y_full"), 1)
            if c > 0:
                att_outputs(c - 1)
        att_probs(7)
        att_outputs(7)
        eng.wait_ge(block_out, 4 + 2 * (s.b0 + 2))
        feature_jobs("ymean", [(lambda f: const("head_mean"), lambda f: YT[:, f, :])])
        eng.wait_ge(S("y_squares"), 1)
        feature_jobs("yvar", [(lambda f: const("head_mean"), lambda f: SQ[:, f, :])])
        stream(st["mix"])
        eng.wait_ge(S("mem_in"), 32)
        transposes("memT", natural(MEMN))
        stream(st["cross_kv"])
        transposes("x3T", natural(XN), ("h_block", 0))
        stream(st["cross_q"])
        eng.wait_ge(block_out, 4 + 2 * st["cross_o"].b0)
        transposes("ckT", natural(CKV))
        transposes("cqT", natural(CQ))
        jobs_out(eng, "cqT")
        attention("cross", 4, CQT, CKT, lambda hd: hd, lambda g, sh: CKV[:, 1, sh, g * P:(g + 1) * P], CSP, CPT)
        stream(st["cross_o"])
        transposes("x4T", natural(XN), ("h_block", 4))

        def hidden_step(q, b):
            return lambda: transposes(f"h{q}T", natural(UPN), ("hidden_squared", 4 * q), (2 * b, 2 * b + 1))

        mlp_streams(stream, hidden_step, 2)

    ctx.close()


def columns(v):
    return np.ascontiguousarray(v.reshape(-1, P).T)


def transposed(x):
    return np.ascontiguousarray(x.T.reshape(-1, P, x.shape[0]).transpose(1, 0, 2))


def kernel(**inputs):
    import concourse.bacc as bacc
    from concourse.bass_utils import run_bass_kernel_spmd as run

    v = {k: np.ascontiguousarray(x) for k, x in inputs.items()}
    mu = v["rwkv_mu_2"][0]
    col = {
        "c": v["c"][0], "c_ctx": v["c_ctx"], "conv_w0": v["conv_w"][0, 0], "conv_w1": v["conv_w"][0, 1],
        "conv_w2": v["conv_w"][0, 2], "pool_scale": v["pool_scale"][0], "norm_mix_2": v["norm_mix_2"][0],
        "norm_cross_2": v["norm_cross_2"][0], "norm_mem_2": v["norm_mem_2"][0], "norm_mlp_2": v["norm_mlp_2"][0],
        "ln_g0": v["ln_g"][0], "ln_b0": v["ln_b"][0], "ln_g1": v["ln_g"][1], "ln_b1": v["ln_b"][1],
        "mu_lora": np.concatenate([mu[3072:3360], np.zeros(96, np.float32)]),
        "mu_r": mu[0:1024], "mu_k": mu[1024:2048], "mu_v": mu[2048:3072],
    }
    for n in ("w_decay0_2", "a0_2", "k_k_2", "k_a_2", "r_k_2", "lnx_w_2", "lnx_b_2"):
        col[n] = v[n][0].reshape(-1)
    arrays = {"cols": np.concatenate([columns(col[n]) for n in COL_NAMES], 1),
              "common_consts": common_constants()[1], "gla_consts": gla_constants()[1],
              "pool_consts": pool_constants()[1], "second_consts": second_constants()[1],
              "mem": v["mem_2"], "positions": np.ascontiguousarray(v["positions_2"].reshape(2, P).T),
              "ctxT": transposed(v["ctx"][0]), "xT": transposed(v["x"][0])}
    for n in ("x", "w_ada", "b_ada", "ln_g", "ln_b", "w_in_e", "w_gate_f", "b_gate_f", "w_gate_b", "b_gate_b",
              "gla_norm_w", "w_out_e", "w_in_o", "w_pool", "w_out_o", "norm_final_2"):
        arrays[n] = v[n]
    for n in ("w_in", "w_mix_out", "w_q_cross", "w_kv_cross", "w_o_cross", "w_up", "w_down"):
        arrays[n if n != "w_in" else "w_in_2"] = v[n + "_2"]
    for n in ("w_decay_up_2", "a_up_2", "g_up_2"):
        arrays[n] = v[n]
    nc = bacc.Bacc("TRN2", target_bir_lowering=False, num_devices=1)
    args = {n: nc.dram_tensor("in_" + n, x.shape, mybir.dt.from_np(x.dtype), kind="ExternalInput").ap()
            for n, x in arrays.items()}
    for n in ("scratch_a", "scratch_t"):
        args[n] = nc.dram_tensor(n, (P, C, C), F32, kind="Internal").ap()
    out = nc.dram_tensor("out", (1, T, D), F32, kind="ExternalOutput").ap()
    build(nc, args, out, STOP)
    r = run(nc, [{"in_" + n: x for n, x in arrays.items()}], core_ids=[0])
    return r.results[0]["out"]
```
